# Optimizing a Trainium2 kernel written in Bass

```python
import math
import jax, jax.numpy as jnp
from jax import lax
import numpy as np

D_MODEL = 2048
BATCH = 1
SEQ = 256
DEPTH = 2

N_MIXERS = 2
PLE_DIM = 256
D_FF = ((8 * D_MODEL // 3 + 255) // 256) * 256
EPS = 1e-6

GM_WIDTH = D_MODEL
GM_CHUNK = 128
GM_HEAD_DIM = 128
GM_HEADS = GM_WIDTH // GM_HEAD_DIM

S5_WIDTH = D_MODEL
S5_GROUP = 16
S5_GROUPS = S5_WIDTH // S5_GROUP
S5_STATE = 64
DT_MIN = 1e-3
DT_MAX = 1e-1

N_A = (DEPTH + 1) // 2
N_B = DEPTH // 2

kernel_name = "hybrid_gmlp_s5_interleaved_trunk"

def _rms_norm(x, g):
    xf = x.astype(jnp.float32)
    y = xf * lax.rsqrt(jnp.mean(xf * xf, axis=-1, keepdims=True) + EPS)
    return (y * g.astype(jnp.float32)).astype(x.dtype)

def _layer_norm(x, g, b):
    xf = x.astype(jnp.float32)
    mu = jnp.mean(xf, axis=-1, keepdims=True)
    xc = xf - mu
    y = xc * lax.rsqrt(jnp.mean(xc * xc, axis=-1, keepdims=True) + EPS)
    return (y * g.astype(jnp.float32) + b.astype(jnp.float32)).astype(x.dtype)

def _gmlp_mixer(h, w_in, ln_g, ln_b, w_s, b_s, w_out):
    bsz, seq, _ = h.shape
    z = jax.nn.gelu(h @ w_in)
    u, v = jnp.split(z, 2, axis=-1)
    v = _layer_norm(v, ln_g, ln_b)
    vc = v.reshape(bsz, seq // GM_CHUNK, GM_CHUNK, GM_HEADS, GM_HEAD_DIM)
    causal = jnp.tril(jnp.ones((GM_CHUNK, GM_CHUNK), dtype=bool))
    w_causal = jnp.where(causal, w_s, jnp.zeros_like(w_s)).astype(v.dtype)
    sv = jnp.einsum('hts,bnshd->bnthd', w_causal, vc) + b_s.T[:, :, None].astype(v.dtype)
    return (u * sv.reshape(bsz, seq, GM_WIDTH)) @ w_out

def _lin_combine(left, right):
    a_l, b_l = left
    a_r, b_r = right
    return a_r * a_l, a_r * b_l + b_r

def _s5_mixer(h, w_in, a_re, a_im, log_dt, b_re, b_im, c_re, c_im, d, w_out):
    f32 = jnp.float32
    bsz, seq, _ = h.shape
    u = (h @ w_in).astype(f32)
    lam = lax.complex(a_re.astype(f32), a_im.astype(f32))
    dt = jnp.exp(log_dt.astype(f32))[:, None]
    lam_bar = jnp.exp(lam * dt)
    b_bar = ((lam_bar - 1.0) / lam)[..., None] * lax.complex(b_re.astype(f32), b_im.astype(f32))
    ug = u.reshape(bsz, seq, S5_GROUPS, S5_GROUP)
    bu = lax.complex(jnp.einsum('blgc,gpc->blgp', ug, jnp.real(b_bar)),
                     jnp.einsum('blgc,gpc->blgp', ug, jnp.imag(b_bar)))
    a = jnp.broadcast_to(lam_bar, (1, seq) + lam_bar.shape)
    _, s = lax.associative_scan(_lin_combine, (a, bu), axis=1)
    y = (jnp.einsum('blgp,gcp->blgc', jnp.real(s), c_re.astype(f32))
         - jnp.einsum('blgp,gcp->blgc', jnp.imag(s), c_im.astype(f32)))
    y = y.reshape(bsz, seq, S5_WIDTH) + d.astype(f32) * u
    g = jax.nn.gelu(y).astype(h.dtype)
    val, gate = jnp.split(g @ w_out, 2, axis=-1)
    return val * jax.nn.sigmoid(gate)

def _swiglu(h, w1, w3, w2):
    return (jax.nn.silu(h @ w1) * (h @ w3)) @ w2

def _normal(k, shape, scale):
    return jax.random.normal(k, shape, jnp.float32) * scale

def setup_inputs(seed: int = 0) -> dict:
    key = jax.random.key(seed)
    ks = jax.random.split(key, 32)
    D = D_MODEL
    x = _normal(ks[0], (BATCH, SEQ, D), 1.0)
    p = _normal(ks[1], (DEPTH, BATCH, SEQ, PLE_DIM), 1.0)
    norm_mix = 1.0 + _normal(ks[2], (DEPTH, D), 0.02)
    norm_ffn = 1.0 + _normal(ks[3], (DEPTH, D), 0.02)
    norm_ple = 1.0 + _normal(ks[4], (DEPTH, D), 0.02)
    norm_final = 1.0 + _normal(ks[5], (D,), 0.02)
    gm_w_in = _normal(ks[6], (N_A, D, 2 * GM_WIDTH), D ** -0.5)
    gm_ln_g = 1.0 + _normal(ks[7], (N_A, GM_WIDTH), 0.02)
    gm_ln_b = _normal(ks[8], (N_A, GM_WIDTH), 0.02)
    gm_w_s = _normal(ks[9], (N_A, GM_HEADS, GM_CHUNK, GM_CHUNK), GM_CHUNK ** -0.5)
    gm_b_s = 1.0 + _normal(ks[10], (N_A, GM_HEADS, GM_CHUNK), 0.02)
    gm_w_out = _normal(ks[11], (N_A, GM_WIDTH, D), GM_WIDTH ** -0.5)
    s5_w_in = _normal(ks[12], (N_B, D, S5_WIDTH), D ** -0.5)
    s5_a_re = -0.5 + _normal(ks[13], (N_B, S5_GROUPS, S5_STATE), 0.01)
    n_idx = jnp.arange(S5_STATE, dtype=jnp.float32)
    s5_a_im = math.pi * n_idx + _normal(ks[14], (N_B, S5_GROUPS, S5_STATE), 0.01)
    s5_log_dt = jax.random.uniform(ks[15], (N_B, S5_GROUPS), jnp.float32,
                                   math.log(DT_MIN), math.log(DT_MAX))
    b_scale = (S5_GROUP ** -0.5) / math.sqrt(2.0)
    s5_b_re = _normal(ks[16], (N_B, S5_GROUPS, S5_STATE, S5_GROUP), b_scale)
    s5_b_im = _normal(ks[17], (N_B, S5_GROUPS, S5_STATE, S5_GROUP), b_scale)
    c_scale = (S5_STATE ** -0.5) / math.sqrt(2.0)
    s5_c_re = _normal(ks[18], (N_B, S5_GROUPS, S5_GROUP, S5_STATE), c_scale)
    s5_c_im = _normal(ks[19], (N_B, S5_GROUPS, S5_GROUP, S5_STATE), c_scale)
    s5_d = _normal(ks[20], (N_B, S5_WIDTH), 1.0)
    s5_w_out = _normal(ks[21], (N_B, S5_WIDTH, 2 * D), S5_WIDTH ** -0.5)
    ffn_w1 = _normal(ks[22], (DEPTH, D, D_FF), D ** -0.5)
    ffn_w3 = _normal(ks[23], (DEPTH, D, D_FF), D ** -0.5)
    ffn_w2 = _normal(ks[24], (DEPTH, D_FF, D), D_FF ** -0.5)
    ple_w_gate = _normal(ks[25], (DEPTH, D, D), D ** -0.5)
    ple_w_proj = _normal(ks[26], (DEPTH, PLE_DIM, D), PLE_DIM ** -0.5)
    return {
        "x": x, "p": p,
        "norm_mix": norm_mix, "norm_ffn": norm_ffn, "norm_ple": norm_ple, "norm_final": norm_final,
        "gm_w_in": gm_w_in, "gm_ln_g": gm_ln_g, "gm_ln_b": gm_ln_b,
        "gm_w_s": gm_w_s, "gm_b_s": gm_b_s, "gm_w_out": gm_w_out,
        "s5_w_in": s5_w_in, "s5_a_re": s5_a_re, "s5_a_im": s5_a_im, "s5_log_dt": s5_log_dt,
        "s5_b_re": s5_b_re, "s5_b_im": s5_b_im, "s5_c_re": s5_c_re, "s5_c_im": s5_c_im,
        "s5_d": s5_d, "s5_w_out": s5_w_out,
        "ffn_w1": ffn_w1, "ffn_w3": ffn_w3, "ffn_w2": ffn_w2,
        "ple_w_gate": ple_w_gate, "ple_w_proj": ple_w_proj,
    }

def reference(x, p, norm_mix, norm_ffn, norm_ple, norm_final,
              gm_w_in, gm_ln_g, gm_ln_b, gm_w_s, gm_b_s, gm_w_out,
              s5_w_in, s5_a_re, s5_a_im, s5_log_dt, s5_b_re, s5_b_im, s5_c_re, s5_c_im,
              s5_d, s5_w_out,
              ffn_w1, ffn_w3, ffn_w2, ple_w_gate, ple_w_proj):
    for i in range(DEPTH):
        j = i // N_MIXERS
        h = _rms_norm(x, norm_mix[i])
        if i % N_MIXERS == 0:
            x = x + _gmlp_mixer(h, gm_w_in[j], gm_ln_g[j], gm_ln_b[j], gm_w_s[j], gm_b_s[j], gm_w_out[j])
        else:
            x = x + _s5_mixer(h, s5_w_in[j], s5_a_re[j], s5_a_im[j], s5_log_dt[j],
                              s5_b_re[j], s5_b_im[j], s5_c_re[j], s5_c_im[j], s5_d[j], s5_w_out[j])
        x = x + _swiglu(_rms_norm(x, norm_ffn[i]), ffn_w1[i], ffn_w3[i], ffn_w2[i])
        gate = jax.nn.sigmoid(_rms_norm(x, norm_ple[i]) @ ple_w_gate[i])
        x = x + gate * (p[i] @ ple_w_proj[i])
    return _rms_norm(x, norm_final)


_drawn_inputs = setup_inputs


def setup_inputs(seed=0):
    import zlib

    import numpy as np

    out = dict(_drawn_inputs(seed))
    spreads = {}
    factors = {'norm_mix': 3.339,
     'norm_ffn': 10.795,
     'norm_ple': 200.0,
     'norm_final': 20.744,
     'gm_ln_g': 26.571,
     'gm_ln_b': 26.836,
     'gm_b_s': 16.971,
     's5_a_re': 64.0,
     's5_a_im': 33.944,
     's5_log_dt': 36.312,
     's5_b_re': 47.936,
     's5_b_im': 47.072,
     's5_c_re': 47.592,
     's5_c_im': 47.248,
     'p': 5.743,
     's5_w_in': 3.991,
     's5_d': 3.992,
     's5_w_out': 3.512,
     'ple_w_gate': 8.0,
     'ple_w_proj': 5.743}
    for name, (base, spread) in spreads.items():
        noise = np.random.default_rng([zlib.crc32(name.encode()), seed]).standard_normal(out[name].shape)
        drawn = base * np.exp(spread * noise) if base else spread * noise
        out[name] = __import__('jax').numpy.asarray(drawn.astype(out[name].dtype))
    for name, factor in factors.items():
        out[name] = (out[name] * factor).astype(out[name].dtype)
    return out
```

```python
import math
from contextlib import ExitStack

import concourse.bass as bass
from concourse import mybir

F32 = mybir.dt.float32
F32R = mybir.dt.float32r
I32 = mybir.dt.int32
ACT = mybir.ActivationFunctionType
ALU = mybir.AluOpType
AX = mybir.AxisListType
RADD = bass.bass_isa.ReduceOp.add

P = 128
TOK = 256
D = 2048
KB = D // P
DFF = 5632
FB = DFF // P
NW = 512
QB = NW // P
NT = D // NW
TK = 2
KT = KB // TK
FT = FB // TK
NU = DFF // NW
RING = 4
PLE = 256
EPS = 1e-6
HEADS = 16

GROUPS = 128
CH = 16
ST = 64
T = 4
NC = TOK // T
PAIRS = GROUPS // 2
QP = 4
DUOS = KB // 2

STAGES = [
    ("pro", 1, dict(u=8, o=8, q=8, r=4)),
    ("build", KB, dict(u=2, o=2)),
    ("v", NT, dict(t=KT, u=1)),
    ("us", NT, dict(t=KT, u=2, o=1, cross=1, z=1, nl=1, q=2)),
    ("out0", NT, dict(t=KT, u=1, q=2, r=1)),
    ("up0", NU, dict(t=2 * KT, u=2, cross=2, z=2, nl=1, q=2)),
    ("down0", NT, dict(t=FT, u=1, q=2, r=1)),
    ("proj0", NT, dict(t=1, u=1, cross=1)),
    ("gate0", NT, dict(t=KT, u=1, cross=1, z=1, nl=1, g=1, q=2, r=1)),
    ("win", NT, dict(t=KT, u=1, cross=1)),
    ("core", DUOS, dict(u=2, o=2, nl=1, q=1)),
    ("out1", NT, dict(t=2 * KT, u=2, cross=2, nl=1, g=1, q=2, r=1)),
    ("up1", NU, dict(t=2 * KT, u=2, cross=2, z=2, nl=1, q=2)),
    ("down1", NT, dict(t=FT, u=1, q=2, r=1)),
    ("proj1", NT, dict(t=1, u=1, cross=1)),
    ("gate1", NT, dict(t=KT, u=1, cross=1, z=1, nl=1, g=1, r=1)),
    ("fin", 1, dict(u=5, o=5)),
]


def plan():
    at, now = {}, dict(t=0, u=0, o=0, cross=0, z=0, nl=0, g=0, q=0, r=0)
    for name, times, per in STAGES:
        at[name] = dict(now)
        assert now["t"] % RING == 0 and now["u"] % 2 == 0
        for k, v in per.items():
            now[k] += v * times
    return at


AT = plan()


class Chain:

    def __init__(self, eng, sem):
        self.eng, self.sem, self.n, self.base, self.i, self.per = eng, sem, 0, 0, 0, 0

    def __call__(self, ins):
        ins.then_inc(self.sem, 1)
        self.n += 1
        self.eng.wait_ge(self.sem, self.base + self.i * self.per + self.n)

    def enter(self, i, per):
        self.base, self.i, self.per, self.n = self.base + self.n, i, per, 0

    def leave(self, times):
        assert self.n == self.per, (self.n, self.per)
        self.base, self.i, self.n = self.base + self.per * times, 0, 0


def trunk(nc, x, p, norm_mix, norm_ffn, norm_ple, norm_final, gm_w_in, gm_ln_g, gm_ln_b, gm_w_s, gm_b_s,
          gm_w_out, s5_w_in, s5_a_re, s5_a_im, s5_log_dt, s5_b_re, s5_b_im, s5_c_re, s5_c_im, s5_d,
          s5_w_out, ffn_w1, ffn_w3, ffn_w2, ple_w_gate, ple_w_proj, out):
    ctx = ExitStack()
    with ctx:
        def sem(name):
            return ctx.enter_context(nc.semaphore(name))

        KBYTE = 1024
        base = (nc.sbuf_base + 63) // 64 * 64
        arena = ctx.enter_context(nc.sbuf_tensor("arena", [P, (206 * KBYTE + 512) // 4], F32))
        top = [base]

        def place(name, shape, dt=F32, at=None):
            size = 4
            for s in shape[1:]:
                size *= s
            if at is None:
                at = top[0]
                top[0] += (size + 31) // 32 * 32
                assert top[0] <= base + 206 * KBYTE + 256, name
            return nc.alloc_sbuf_tensor_at(name, shape, dt, offset=at)

        X = place("X", [P, D // P * TOK])
        h_at = top[0]
        H = place("H", [P, KB, 2 * TOK], F32R)
        m_at = top[0]
        M = place("M", [P, FB, 2 * TOK], F32R)
        RAW = place("RAW", [P, RING, TK * NW])
        WHI = place("WHI", [P, RING, TK * NW], F32R)
        WLO = place("WLO", [P, RING, TK * NW], F32R)
        T1 = place("T1", [P, QB * TOK])
        Z = place("Z", [P, QB * TOK])
        PT = place("PT", [P, 2 * (PLE // P), 2 * TOK], F32R)
        IDENT = place("IDENT", [P, P])
        VEC = place("VEC", [P, 8, KB])
        SS = place("SS", [P, TOK])
        SUM = place("SUM", [P, TOK])
        RSTD = place("RSTD", [P, TOK])
        RCOL = place("RCOL", [P, 2])
        ONE = place("ONE", [1, P])
        RHO = place("RHO", [P, PAIRS])
        PAR = place("PAR", [P, 2])
        STAT = place("STAT", [P, 2, 4 * 6])
        MV = place("MV", [P, 2, 2])
        LNR = place("LNR", [P, 2, 1])
        EPSB = place("EPSB", [P, 1])
        BAND = place("BAND", [P, QP])

        def h_view(name, shape, off, dt=F32):
            return place(name, shape, dt, at=h_at + off * KBYTE)

        def m_view(name, shape, off, dt=F32):
            return place(name, shape, dt, at=m_at + off * KBYTE)

        XN = m_view("XN", [P, 2, D], 32)
        WN = m_view("WN", [P, HEADS, P], 48)
        NAT = m_view("NAT", [P, P], 56)
        AN = m_view("AN", [PAIRS, 3, P], 57)
        LDN = m_view("LDN", [PAIRS, 2], 59)
        PN = m_view("PN", [P, 2, 2, PLE], 60)
        V = h_view("V", [P, 2, D], 0)
        WT = h_view("WT", [P, HEADS, P], 16)
        LG = m_view("LG", [P, 2, D], 64)
        BS = m_view("BS", [1, HEADS, P], 80)
        ROT = m_view("ROT", [P, 2, PAIRS, NC], 32)
        SA = h_view("SA", [P, 3, PAIRS], 0)
        LAM = h_view("LAM", [P, 2, T + 1, PAIRS], 1)
        FAC = h_view("FAC", [P, 2, PAIRS], 4)
        ROTP = h_view("ROTP", [P, 2, 7, PAIRS], 5)
        PW = h_view("PW", [P, 16, PAIRS], 9)
        PI = h_view("PI", [P, PAIRS], 13, I32)
        CN = h_view("CN", [P, 2, ST], 24)
        CM = h_view("CM", [P, 2, 2, ST], 25)
        BD = h_view("BD", [P, 2, QP, 2, CH], 26)
        KS = h_view("KS", [P, T, P], 29)
        QT = m_view("QT", [P, T, 2, P], 64)
        DT = m_view("DT", [P, T + 1, 2, P], 68)
        QS = m_view("QS", [P, T, 2, P], 73)
        TA = m_view("TA", [P, 4, P], 77)
        TB = m_view("TB", [P, 4, P], 79)
        TC = m_view("TC", [P, 4, P], 81)
        TDD = m_view("TDD", [P, 4, P], 83)
        RA = m_view("RA", [P, 2, PAIRS // 2, NC // 2], 64)
        RB = m_view("RB", [P, 2, PAIRS // 2, NC // 2], 72)
        TQ = [h_view("TQ0", [P, 2, T, 2, P], 0), m_view("TQ1", [P, 2, T, 2, P], 64)]
        TD = [h_view("TD0", [P, 2, T, 2, P], 8), m_view("TD1", [P, 2, T, 2, P], 72)]
        TKK = [h_view("TK0", [P, 2, T, P], 16), m_view("TK1", [P, 2, T, P], 80)]
        TE = [h_view("TE0", [P, 2, 2, QP, NC], 20), m_view("TE1", [P, 2, 2, QP, NC], 84)]
        UD = m_view("UD", [P, 2, 2, T, NC], 0)
        SD = m_view("SD", [P, 2, 2, 2, QP, NC], 4)
        CA = m_view("CA", [P, QP, 2, NC], 12)
        CB = m_view("CB", [P, QP, 2, NC], 14)
        CV = m_view("CV", [P, 2, QP, NC], 16)
        CW = m_view("CW", [P, 2, QP, NC], 18)
        RT = m_view("RT", [P, QP, NC], 20)
        KEEP = m_view("KEEP", [P, QP, NC], 21)
        UF = m_view("UF", [P, KB, 2, TOK], 32)
        VAL = m_view("VAL", [P, QB * TOK], 64)
        GATED = m_view("GATED", [P, FB, 2, TOK], 0)
        PROJ = m_view("PROJ", [P, D // P * TOK], 32)
        ON = m_view("ON", [P, 2, D], 64)
        XF = m_view("XF", [P, 2, QB, TOK], 80)

        PS = ctx.enter_context(nc.psum_tensor("PS", [P, 8, NW], F32))

        tabq = nc.dram_tensor("tabq", (KB, P, T * 2 * P), F32).ap()
        tabd = nc.dram_tensor("tabd", (KB, P, T * 2 * P), F32).ap()
        tabk = nc.dram_tensor("tabk", (KB, P, T * P), F32).ap()
        tabe = nc.dram_tensor("tabe", (KB, 2, P, QP * NC), F32).ap()

        raw_in = [sem(f"raw_in{s}") for s in range(RING)]
        hi_ready = sem("hi_ready")
        lo_ready = sem("lo_ready")
        split_used = sem("split_used")
        acc_done = sem("acc_done")
        acc_free = sem("acc_free")
        cross_copied = sem("cross_copied")
        z_ready = sem("z_ready")
        nl_ready = sem("nl_ready")
        gated_ready = sem("gated_ready")
        operand_hi = sem("operand_hi")
        operand_ready = sem("operand_ready")
        squares_ready = sem("squares_ready")
        squares_summed = sem("squares_summed")
        square_total = sem("square_total")
        root_ready = sem("root_ready")
        rstd_ready = sem("rstd_ready")
        dve_chain = sem("dve_chain")
        pool_chain = sem("pool_chain")
        x_in = sem("x_in")
        small_in = sem("small_in")
        ws_in = sem("ws_in")
        ws_masked = sem("ws_masked")
        ident_ready = sem("ident_ready")
        masks_ready = sem("masks_ready")
        ldt_spread = sem("ldt_spread")
        p_hi = sem("p_hi")
        p_ready = sem("p_ready")
        ln_in = sem("ln_in")
        v_ready = sem("v_ready")
        ln_var = sem("ln_var")
        ln_root = sem("ln_root")
        angle_ready = sem("angle_ready")
        sine_ready = sem("sine_ready")
        rot_ready = sem("rot_ready")
        rot_out = sem("rot_out")
        bc_in = sem("bc_in")
        bc_used = sem("bc_used")
        cm_ready = sem("cm_ready")
        qt_ready = sem("qt_ready")
        dt_ready = sem("dt_ready")
        tab_out = sem("tab_out")
        tab_in = [sem("tab_in0"), sem("tab_in1")]
        core_ready = sem("core_ready")
        u_ready = sem("u_ready")
        ud_ready = sem("ud_ready")
        sd_ready = sem("sd_ready")
        rt_ready = sem("rt_ready")
        rt_used = sem("rt_used")
        xf_ready = sem("xf_ready")
        out_ready = sem("out_ready")
        out_done = sem("out_done")

        block = ctx.enter_context(nc.Block())

        def tile_src(w, k0, col):
            return w.rearrange("(k p) n -> p k n", p=P)[:, k0:k0 + TK, bass.ds(col, NW)]

        def quad(s, lo):
            return PS[:, QB * s:QB * s + QB, lo:lo + TOK]

        def flat3(t):
            return t[:, :].rearrange("p (m t) -> p m t", t=TOK)

        @block.sync
        def _(sp):
            def load(src, t, slot, first=False):
                if not first:
                    sp.wait_ge(lo_ready, t - (RING - 1))
                sp.dma_start(RAW[:, slot, :].rearrange("p (k n) -> p k n", k=TK), src).then_inc(raw_in[slot], 16)

            def column(w, t0, col, depth, j0=0, first=False, done=0):
                for j in range(done, depth):
                    load(tile_src(w, TK * j, col), t0 + j, (j0 + j) % RING, first)

            sp.dma_start(XN[:, :, :], x[0].rearrange("(h p) d -> p h d", p=P)).then_inc(x_in, 16)
            t = AT["v"]["t"]
            column(gm_w_in[0], t, D, RING, first=True)

            u0 = AT["build"]["u"]
            with nc.sync.Fori(0, KB) as b:
                sp.wait_ge(bc_used, b + 1)
                for ri, (bw, cw) in enumerate([(s5_b_re, s5_c_re), (s5_b_im, s5_c_im)]):
                    sp.dma_start(CN[:, ri, :],
                                   cw[0].rearrange("g c s -> (g c) s")[bass.ds(b * P, P), :]).then_inc(bc_in, 16)
                    for g in range(2):
                        src = bw[0].rearrange("(q g) s c -> g s q c", g=2)[g, :, bass.ds(b * QP, QP), :]
                        sp.dma_start(BD[ST * g:ST * g + ST, ri, :, g, :], src).then_inc(bc_in, 16)
                sp.wait_ge(dt_ready, b + 1)
                sp.dma_start(tabd[bass.ds(b, 1)].rearrange("b p n -> p (b n)"),
                               DT[:, 1:T + 1, :, :].rearrange("p j r n -> p (j r n)")).then_inc(tab_out, 16)
                sp.wait_ge(acc_free, b * 2 + (u0 + 2))
                sp.dma_start(tabq[bass.ds(b, 1)].rearrange("b p n -> p (b n)"),
                               QS[:, :, :, :].rearrange("p j r n -> p (j r n)")).then_inc(tab_out, 16)
                sp.dma_start(tabk[bass.ds(b, 1)].rearrange("b p n -> p (b n)"),
                               KS[:, :, :].rearrange("p j n -> p (j n)")).then_inc(tab_out, 16)
            sp.wait_ge(rot_ready, 1)
            for b in range(KB):
                for ri in range(2):
                    sp.dma_start(tabe[b, ri],
                                   ROT[:, ri, QP * b:QP * b + QP, :].rearrange("p q k -> p (q k)")).then_inc(rot_out, 16)

            for n in range(NT):
                done = RING if n == 0 else 0
                column(gm_w_in[0], t + KT * n, D + NW * n, KT, done=done)
            with nc.sync.Fori(0, NT) as n:
                column(gm_w_in[0], AT["us"]["t"] + n * KT, n * NW, KT)
            with nc.sync.Fori(0, NT) as n:
                column(gm_w_out[0], AT["out0"]["t"] + n * KT, n * NW, KT)

            def ffn_and_gate(i):
                with nc.sync.Fori(0, NU) as n:
                    t0 = AT[f"up{i}"]["t"] + n * (2 * KT)
                    column(ffn_w1[i], t0, n * NW, KT)
                    column(ffn_w3[i], t0 + KT, n * NW, KT)
                with nc.sync.Fori(0, NT // 2) as n:
                    t0 = AT[f"down{i}"]["t"] + n * (2 * FT)
                    column(ffn_w2[i], t0, n * (2 * NW), FT)
                    column(ffn_w2[i], t0 + FT, n * (2 * NW) + NW, FT, j0=FT)
                for n in range(NT):
                    column(ple_w_proj[i], AT[f"proj{i}"]["t"] + n, NW * n, 1, j0=n)
                with nc.sync.Fori(0, NT) as n:
                    column(ple_w_gate[i], AT[f"gate{i}"]["t"] + n * KT, n * NW, KT)

            ffn_and_gate(0)
            with nc.sync.Fori(0, NT) as n:
                column(s5_w_in[0], AT["win"]["t"] + n * KT, n * NW, KT)
            t = AT["out1"]["t"]
            column(s5_w_out[0], t, 0, RING)
            def tables(d, par):
                for bl in range(2):
                    b = d * 2 + bl
                    sp.dma_start(TQ[par][:, bl].rearrange("p j r n -> p (j r n)"),
                                   tabq[bass.ds(b, 1)].rearrange("b p n -> p (b n)")).then_inc(tab_in[par], 16)
                    sp.dma_start(TD[par][:, bl].rearrange("p j r n -> p (j r n)"),
                                   tabd[bass.ds(b, 1)].rearrange("b p n -> p (b n)")).then_inc(tab_in[par], 16)
                    sp.dma_start(TKK[par][:, bl].rearrange("p j n -> p (j n)"),
                                   tabk[bass.ds(b, 1)].rearrange("b p n -> p (b n)")).then_inc(tab_in[par], 16)
                    sp.dma_start(TE[par][:, bl].rearrange("p r q k -> p r (q k)"),
                                   tabe[bass.ds(b, 1)].rearrange("b r p n -> p (b r) n")).then_inc(tab_in[par], 16)

            sp.wait_ge(rot_out, 16 * 2 * KB)
            sp.wait_ge(tab_out, 16 + 48 * KB)
            sp.wait_ge(split_used, AT["core"]["t"])
            tables(0, 0)
            tables(1, 1)
            o0 = AT["core"]["o"]
            with nc.sync.Fori(0, DUOS // 2 - 1) as e:
                for par in range(2):
                    sp.wait_ge(acc_done, e * 4 + (2 * par + o0 + 3))
                    tables(e * 2 + (par + 2), par)
            column(s5_w_out[0], t, 0, KT, done=RING)
            column(s5_w_out[0], t + KT, D, KT)
            with nc.sync.Fori(1, NT) as n:
                t0 = t + n * (2 * KT)
                column(s5_w_out[0], t0, n * NW, KT)
                column(s5_w_out[0], t0 + KT, n * NW + D, KT)
            ffn_and_gate(1)
            for n in range(NT):
                sp.wait_ge(out_ready, n + 1)
                sp.dma_start(out[0, :, NW * n:NW * n + NW].rearrange("(h p) d -> p h d", p=P),
                             ON[:, :, NW * n:NW * n + NW]).then_inc(out_done, 16)
            sp.wait_ge(out_done, 16 * NT)

        @block.gpsimd
        def _(pool):
            step = Chain(pool, pool_chain)
            vectors = [norm_mix[0], norm_mix[1], norm_ffn[0], norm_ffn[1], norm_ple[0], norm_ple[1], norm_final, s5_d[0]]
            for i, v in enumerate(vectors):
                pool.dma_start(NAT[KB * i:KB * i + KB, :], v.rearrange("(k p) -> k p", p=P)).then_inc(small_in, 16)
            pool.dma_start(AN[:, 0, :], s5_a_re[0].rearrange("(q g) s -> q (g s)", g=2)).then_inc(small_in, 16)
            pool.dma_start(AN[:, 1, :], s5_a_im[0].rearrange("(q g) s -> q (g s)", g=2)).then_inc(small_in, 16)
            pool.dma_start(LDN[:, :], s5_log_dt[0].rearrange("(q g) -> q g", g=2)).then_inc(small_in, 16)
            for l in range(2):
                pool.dma_start(PN[:, l, :, :], p[l, 0].rearrange("(h p) d -> p h d", p=P)).then_inc(small_in, 16)
            pool.dma_start(WN[:, :, :], gm_w_s[0].rearrange("h t s -> t h s")).then_inc(ws_in, 16)
            step(nc.gpsimd.memset(IDENT[:, :], 0.0))
            nc.gpsimd.affine_select(out=IDENT[:, :], in_=IDENT[:, :], compare_op=ALU.not_equal, fill=1.0, base=0,
                                    pattern=[[-1, P]], channel_multiplier=1).then_inc(ident_ready, 1)
            nc.gpsimd.memset(ONE[0:1, :], 1.0)
            nc.gpsimd.memset(EPSB[:, :], EPS)
            step(nc.gpsimd.memset(BAND[:, :], 1.0))
            step(nc.gpsimd.affine_select(out=BAND[:, :], in_=BAND[:, :], compare_op=ALU.is_ge, fill=0.0,
                                         base=0, pattern=[[-2 * CH, QP]], channel_multiplier=1))
            step(nc.gpsimd.affine_select(out=BAND[:, :], in_=BAND[:, :], compare_op=ALU.is_ge, fill=0.0,
                                         base=CH - 1, pattern=[[2 * CH, QP]], channel_multiplier=-1))
            step(nc.gpsimd.tensor_tensor(BAND[:, 0:2], BAND[:, 0:2], BAND[:, 2:4], ALU.add))
            step(nc.gpsimd.tensor_tensor(PAR[:, 0:1], BAND[:, 0:1], BAND[:, 1:2], ALU.add))
            nc.gpsimd.tensor_scalar(PAR[:, 1:2], PAR[:, 0:1], -1.0, 1.0, ALU.mult, ALU.add).then_inc(masks_ready, 1)
            nc.gpsimd.memset(BD[:, :, :, :, :], 0.0).then_inc(bc_used, 1)
            nc.gpsimd.memset(KS[:, :, :], 0.0).then_inc(tab_out, 16)
            pool.wait_ge(ws_in, 16)
            nc.gpsimd.affine_select(out=WN[:, :, :], in_=WN[:, :, :], compare_op=ALU.is_ge, fill=0.0, base=0,
                                    pattern=[[0, HEADS], [-1, P]], channel_multiplier=1).then_inc(ws_masked, 1)

            def all_reduce(k):
                pool.wait_ge(squares_summed, AT[k]["r"])
                nc.gpsimd.partition_all_reduce(SUM[:, :], SS[:, :], P, RADD).then_inc(square_total, 1)

            all_reduce("build")

            pool.wait_ge(tab_out, 16 + 48 * KB)
            pool.dma_start(LG[:, 0, :], gm_ln_g[0].unsqueeze(0).to_broadcast([P, D])).then_inc(ln_in, 16)
            pool.dma_start(LG[:, 1, :], gm_ln_b[0].unsqueeze(0).to_broadcast([P, D])).then_inc(ln_in, 16)
            pool.dma_start(BS[0:1, :, :], gm_b_s[0:1, :, :]).then_inc(ln_in, 16)

            all_reduce("up0")
            all_reduce("proj0")
            all_reduce("win")

            def decay(d, bl):
                nc.gpsimd.tensor_tensor(RT[:, :, :], KEEP[:, :, :],
                                        RHO[:, bass.ds((d * 2 + bl) * QP, QP)].unsqueeze(2).to_broadcast([P, QP, NC]),
                                        ALU.mult).then_inc(rt_ready, 1)

            pool.wait_ge(split_used, AT["core"]["t"])
            step(nc.gpsimd.memset(KEEP[:, :, :], 1.0))
            step(nc.gpsimd.memset(KEEP[:, :, 0:1], 0.0))
            nc.gpsimd.memset(SD[:, :, :, :, :, 0:1], 0.0).then_inc(core_ready, 1)
            decay(0, 0)
            pool.wait_ge(rt_used, 1)
            decay(0, 1)
            with nc.gpsimd.Fori(1, DUOS) as d:
                for bl in range(2):
                    pool.wait_ge(rt_used, d * 2 + bl)
                    decay(d, bl)

            all_reduce("up1")
            all_reduce("proj1")
            all_reduce("fin")

        @block.scalar
        def _(act):
            def split(t, rnd, slot, first=False):
                act.wait_ge(raw_in[slot], rnd * 16 + 16)
                if not first:
                    act.wait_ge(split_used, t - (RING - 1))
                nc.scalar.activation(WHI[:, slot, :], RAW[:, slot, :], ACT.Copy).then_inc(hi_ready, 1)

            def splits(stage, i, per, j0, count):
                for j in range(j0, j0 + count):
                    split(AT[stage]["t"] + RING + i * per + j, AT[stage]["t"] // RING + 1 + i * (per // RING) + j // RING,
                          j % RING)

            def column_end(stage, c, per=KT):
                return AT[stage]["t"] + per + c * per

            def cross(u, s, r, t_end):
                act.wait_ge(split_used, t_end)
                act.wait_ge(acc_free, u)
                act.wait_ge(squares_summed, r)
                nc.scalar.activation(flat3(T1), quad(s, TOK), ACT.Copy).then_inc(cross_copied, 1)

            def high_parts(n, vec, dst, signal, value):
                act.wait_ge(signal, value)
                for m in range(QB):
                    k = n * QB + m
                    last = nc.scalar.activation(dst[:, bass.ds(k, 1), 0:TOK].rearrange("p k t -> p (k t)"),
                                                X[:, bass.ds(k * TOK, TOK)], ACT.Identity,
                                                scale=VEC[:, vec, bass.ds(k, 1)])
                last.then_inc(operand_hi, 2)

            def squares(n, r, signal, value):
                act.wait_ge(signal, value)
                if not (isinstance(r, int) and r == 0):
                    act.wait_ge(squares_summed, r)
                nc.scalar.activation(T1[:, :], X[:, bass.ds(n * (QB * TOK), QB * TOK)], ACT.Square).then_inc(squares_ready, 1)

            def root(k):
                act.wait_ge(square_total, k)
                nc.scalar.activation(SUM[:, :], SUM[:, :], ACT.Sqrt, scale=1.0 / D, bias=EPSB[:, 0:1]).then_inc(root_ready, 1)

            act.wait_ge(masks_ready, 1)
            act.wait_ge(acc_done, 1)
            nc.scalar.activation(VEC[:, :, :].rearrange("p v k -> p (v k)"), PS[:, 0, 0:P], ACT.Copy)
            nc.scalar.activation(SA[:, :, :], PS[:, 1:4, 0:PAIRS], ACT.Copy).then_inc(acc_free, 1)
            act.wait_ge(acc_free, 1)
            for n in range(NT):
                high_parts(n, 0, M, acc_free, n + 2)
                squares(n, n, acc_free, n + 2)
            act.wait_ge(acc_done, 6)
            nc.scalar.activation(WT[:, :, :].rearrange("p h t -> p (h t)"),
                                 PS[:, 4:8, :].rearrange("p b n -> p (b n)"), ACT.Copy).then_inc(acc_free, 1)
            root(1)
            act.wait_ge(acc_done, 7)
            nc.scalar.activation(RCOL[:, :], PS[:, 0, 0:2], ACT.Copy).then_inc(acc_free, 1)
            act.wait_ge(acc_done, 8)
            act.wait_ge(acc_free, 7)
            for h in range(2):
                last = nc.scalar.activation(PT[:, 2 * h:2 * h + 2, 0:TOK], PS[:, 4 + h, :].rearrange("p (k t) -> p k t", t=TOK),
                                            ACT.Copy)
            last.then_inc(p_hi, 1)
            act.wait_ge(angle_ready, 1)
            nc.scalar.activation(PW[:, 8:10, :], PW[:, 8:10, :], ACT.Sin).then_inc(sine_ready, 1)
            u0 = AT["build"]["u"]
            with nc.scalar.Fori(0, KB) as b:
                act.wait_ge(acc_done, b * 2 + (u0 + 1))
                act.wait_ge(tab_out, b * 48 + 16)
                nc.scalar.activation(DT[:, 0, 0, :], PS[:, 0, 0:P], ACT.Copy)
                nc.scalar.activation(DT[:, 0, 1, :], PS[:, 0, P:2 * P], ACT.Copy, scale=-1.0).then_inc(acc_free, 1)
                act.wait_ge(acc_done, b * 2 + (u0 + 2))
                nc.scalar.activation(QS[:, :, :, :].rearrange("p j r n -> p (j r n)"),
                                     PS[:, 4:6, :].rearrange("p b n -> p (b n)"), ACT.Copy)
                for q in range(QP):
                    r = slice(32 * q, 32 * q + 32)
                    last = nc.scalar.activation(KS[r, :, r], PS[r, 6, 0:P].rearrange("p (j c) -> p j c", j=T), ACT.Copy)
                last.then_inc(acc_free, 1)

            for j in range(RING):
                split(j, 0, j, first=True)

            u0 = AT["v"]["u"]
            with nc.scalar.Fori(0, NT // 2) as e:
                for s in range(2):
                    splits("v", e, 2 * KT, KT * s, KT)
                    act.wait_ge(split_used, column_end("v", e * 2 + s))
                    act.wait_ge(acc_free, e * 2 + (u0 + s))
                    for th in range(2):
                        last = nc.scalar.activation(V[:, th, bass.ds(e * (2 * NW) + s * NW, NW)], PS[:, QB * s + th, :],
                                                    ACT.Gelu_apprx_tanh, scale=RCOL[:, th:th + 1])
                    last.then_inc(acc_free, 1)

            def us(n):
                a = AT["us"]
                u = n * 2 + a["u"]
                cross(u, 0, a["r"], column_end("us", n))
                act.wait_ge(z_ready, n + (a["z"] + 1))
                nc.scalar.activation(T1[:, :], Z[:, :], ACT.Gelu_apprx_tanh).then_inc(nl_ready, 1)
                act.wait_ge(acc_free, u + 2)
                nc.scalar.activation(M[:, bass.ds(n * QB + KB, QB), 0:TOK], flat3(Z), ACT.Copy).then_inc(operand_hi, 2)

            splits("us", 0, KT, 0, 4)
            act.wait_ge(ln_var, 1)
            nc.scalar.activation(LNR[:, :, :], MV[:, :, 1:2], ACT.Sqrt, bias=EPSB[:, 0:1]).then_inc(ln_root, 1)
            splits("us", 0, KT, 4, 4)
            us(0)
            with nc.scalar.Fori(1, NT) as n:
                splits("us", n, KT, 0, KT)
                us(n)

            def residual_stage(stage, depth, vec):
                a = AT[stage]
                with nc.scalar.Fori(0, NT // 2) as e:
                    for s in range(2):
                        splits(stage, e, 2 * depth, depth * s, depth)
                        n = e * 2 + s
                        high_parts(n, vec, H, acc_free, n + (a["u"] + 1))
                        squares(n, n + a["r"], acc_free, n + (a["u"] + 1))

            def gated_quad(stage, n, vec, dst, signal, value):
                a = AT[stage]
                act.wait_ge(signal, value)
                nc.scalar.activation(T1[:, :], Z[:, :], ACT.Sigmoid).then_inc(nl_ready, 1)
                if dst is not None:
                    high_parts(n, vec, dst, gated_ready, n + (a["g"] + 1))
                squares(n, n + a["r"], gated_ready, n + (a["g"] + 1))

            def ffn_and_gate(i, k):
                a = AT[f"up{i}"]
                with nc.scalar.Fori(0, NU) as n:
                    splits(f"up{i}", n, 2 * KT, 0, KT)
                    cross(n * 2 + a["u"], 0, a["r"], column_end(f"up{i}", n * 2))
                    act.wait_ge(z_ready, n * 2 + (a["z"] + 1))
                    nc.scalar.activation(GATED[:, bass.ds(n * QB, QB), 1, :], flat3(Z), ACT.Silu).then_inc(nl_ready, 1)
                    splits(f"up{i}", n, 2 * KT, KT, KT)
                    cross(n * 2 + (a["u"] + 1), 1, a["r"], column_end(f"up{i}", n * 2 + 1))
                    act.wait_ge(z_ready, n * 2 + (a["z"] + 2))
                    nc.scalar.activation(M[:, bass.ds(n * QB, QB), 0:TOK], flat3(Z), ACT.Copy).then_inc(operand_hi, 2)
                residual_stage(f"down{i}", FT, 4 + i)
                a = AT[f"proj{i}"]
                for n in range(NT):
                    splits(f"proj{i}", 0, NT, n, 1)
                    cross(a["u"] + n, n % 2, a["r"], column_end(f"proj{i}", n, 1))
                root(k)
                a = AT[f"gate{i}"]
                if i == 0:
                    with nc.scalar.Fori(0, NT // 2) as e:
                        for s in range(2):
                            n = e * 2 + s
                            splits("gate0", e, 2 * KT, KT * s, KT)
                            cross(n + a["u"], s, n + a["r"], column_end("gate0", n))
                            gated_quad("gate0", n, 1, M, z_ready, n + (a["z"] + 1))
                else:
                    for n in range(NT):
                        splits("gate1", 0, KT, KT * n, KT if n < NT - 1 else KT - RING)
                        cross(n + a["u"], n % 2, n + a["r"], column_end("gate1", n))
                        gated_quad("gate1", n, None, None, z_ready, n + (a["z"] + 1))

            residual_stage("out0", KT, 2)
            root(2)
            ffn_and_gate(0, 3)
            root(4)
            a = AT["win"]
            with nc.scalar.Fori(0, NT // 2) as e:
                for s in range(2):
                    splits("win", e, 2 * KT, KT * s, KT)
                    cross(e * 2 + (a["u"] + s), s, a["r"], column_end("win", e * 2 + s))

            a = AT["core"]

            def chunked(d, par):
                for bl in range(2):
                    last = nc.scalar.activation(UD[:, par, bl, :, :],
                                                UF[:, bass.ds(d * 2 + bl, 1), 1, :].rearrange("p b (k j) -> p (b j) k", j=T),
                                                ACT.Copy)
                last.then_inc(ud_ready, 1)

            def s5_gelu(d):
                act.wait_ge(acc_free, d * 2 + (a["u"] + 3) if not (isinstance(d, int) and d == DUOS - 1) else a["u"] + 2 * DUOS)
                act.wait_ge(operand_ready, d + a["q"])
                nc.scalar.activation(T1[:, 0:2 * TOK], Z[:, 0:2 * TOK], ACT.Gelu_apprx_tanh).then_inc(nl_ready, 1)
                act.wait_ge(nl_ready, d + (a["nl"] + 1))
                nc.scalar.activation(M[:, bass.ds(d * 2 + KB, 2), 0:TOK],
                                     T1[:, 0:2 * TOK].rearrange("p (b t) -> p b t", t=TOK), ACT.Copy).then_inc(operand_hi, 1)

            act.wait_ge(u_ready, NT)
            act.wait_ge(core_ready, 1)
            chunked(0, 0)
            chunked(1, 1)
            with nc.scalar.Fori(0, DUOS // 2 - 1) as e:
                for par in range(2):
                    d = e * 2 + par
                    act.wait_ge(acc_done, d * 2 + (a["o"] + 3))
                    chunked(d + 2, par)
                    s5_gelu(d)
            s5_gelu(DUOS - 2)
            s5_gelu(DUOS - 1)

            a = AT["out1"]
            with nc.scalar.Fori(0, NT) as n:
                u = n * 2 + a["u"]
                splits("out1", n, 2 * KT, 0, KT)
                cross(u, 0, n + a["r"], column_end("out1", n * 2))
                splits("out1", n, 2 * KT, KT, KT)
                cross(u + 1, 1, n + a["r"], column_end("out1", n * 2 + 1))
                gated_quad("out1", n, 3, H, acc_free, u + 2)
            root(5)
            ffn_and_gate(1, 6)
            root(7)
            u0, o0 = AT["fin"]["u"], AT["fin"]["o"]
            act.wait_ge(acc_done, o0 + 1)
            nc.scalar.activation(RCOL[:, :], PS[:, 0, 0:2], ACT.Copy).then_inc(acc_free, 1)
            act.wait_ge(acc_free, u0 + 1)
            for n in range(NT):
                act.wait_ge(acc_done, o0 + n + 2)
                for th in range(2):
                    last = nc.scalar.activation(ON[:, th, NW * n:NW * n + NW], PS[:, QB * ((n + 1) % 2) + th, :],
                                                ACT.Identity, scale=RCOL[:, th:th + 1])
                last.then_inc(out_ready, 1)

        @block.vector
        def _(dve):
            step = Chain(dve, dve_chain)
            V_ = nc.vector

            def split(t, slot):
                dve.wait_ge(hi_ready, t + 1)
                V_.tensor_tensor(WLO[:, slot, :], RAW[:, slot, :], WHI[:, slot, :].bitcast(F32), ALU.subtract).then_inc(lo_ready, 1)

            def splits(stage, i, per, j0, count):
                for j in range(j0, j0 + count):
                    split(AT[stage]["t"] + RING + i * per + j, j % RING)

            def total(u, s, c, dst):
                dve.wait_ge(cross_copied, c + 1)
                V_.tensor_tensor(dst, quad(s, 0), flat3(T1), ALU.add).then_inc(acc_free, 1)
                dve.wait_ge(acc_free, u + 1)

            def scaled(dst, signal):
                V_.tensor_tensor(dst, flat3(Z), RSTD[:, :].unsqueeze(1).to_broadcast([P, QB, TOK]), ALU.mult).then_inc(signal, 1)

            def low_parts(n, vec, dst, q):
                dve.wait_ge(operand_hi, q + 2)
                for m in range(QB):
                    k = n * QB + m
                    last = V_.scalar_tensor_tensor(dst[:, bass.ds(k, 1), TOK:2 * TOK].rearrange("p k t -> p (k t)"),
                                                   X[:, bass.ds(k * TOK, TOK)], VEC[:, vec, bass.ds(k, 1)],
                                                   dst[:, bass.ds(k, 1), 0:TOK].rearrange("p k t -> p (k t)").bitcast(F32),
                                                   ALU.mult, ALU.subtract)
                last.then_inc(operand_ready, 2)

            def sum_squares(r):
                dve.wait_ge(squares_ready, r + 1)
                step(V_.tensor_reduce(Z[:, 0:TOK], T1[:, :].rearrange("p (m t) -> p t m", t=TOK), AX.X, ALU.add))
                if not (isinstance(r, int) and r == 0):
                    dve.wait_ge(squares_summed, r)
                V_.tensor_tensor(SS[:, :], SS[:, :], Z[:, 0:TOK], ALU.add).then_inc(squares_summed, 1)

            def rstd(k):
                dve.wait_ge(root_ready, k)
                V_.reciprocal(RSTD[:, :], SUM[:, :]).then_inc(rstd_ready, 1)
                dve.wait_ge(rstd_ready, k)
                step(V_.memset(SS[:, :], 0.0))

            dve.wait_ge(small_in, 16 * 13)
            V_.tensor_copy(AN[:, 2, :].rearrange("q (g s) -> q g s", g=2),
                           LDN[:, :].unsqueeze(2).to_broadcast([PAIRS, 2, ST])).then_inc(ldt_spread, 1)
            step(V_.memset(SS[:, :], 0.0))
            dve.wait_ge(acc_free, 1)
            for n in range(NT):
                dve.wait_ge(acc_done, n + 2)
                V_.tensor_copy(X[:, QB * TOK * n:QB * TOK * (n + 1)].rearrange("p (m t) -> p m t", t=TOK),
                               quad((n + 1) % 2, 0)).then_inc(acc_free, 1)
                dve.wait_ge(acc_free, n + 2)
                low_parts(n, 0, M, 2 * n)
                sum_squares(n)
            rstd(1)
            dve.wait_ge(p_hi, 1)
            for h in range(2):
                last = V_.tensor_tensor(PT[:, 2 * h:2 * h + 2, TOK:2 * TOK], PS[:, 4 + h, :].rearrange("p (k t) -> p k t", t=TOK),
                                        PT[:, 2 * h:2 * h + 2, 0:TOK].bitcast(F32), ALU.subtract)
            last.then_inc(acc_free, 1)

            W = lambda i: PW[:, i, :]
            LOG2E, MAGIC = 1.4426950408889634, 12582912.0

            def tt(o, a, b, op):
                step(V_.tensor_tensor(o, a, b, op))

            def ts(o, a, s1, s2, op0, op1):
                step(V_.tensor_scalar(o, a, s1, s2, op0, op1))

            def stt(o, a, s, b, op0, op1):
                step(V_.scalar_tensor_tensor(o, a, s, b, op0, op1))

            def exponential(dst, src, minus_one):
                c, k, r, q = W(10), W(11), W(12), W(13)
                ts(c, src, -88.5, 89.0, ALU.max, ALU.min)
                ts(k, c, LOG2E, MAGIC, ALU.mult, ALU.add)
                ts(k, k, MAGIC, -127.0, ALU.subtract, ALU.max)
                stt(r, k, -0.693359375, c, ALU.mult, ALU.add)
                stt(r, k, 2.12194440e-4, r, ALU.mult, ALU.add)
                ts(q, r, 1.0 / math.factorial(8), 0.0, ALU.mult, ALU.add)
                for n in range(7, 0, -1):
                    stt(q, q, 1.0 / math.factorial(n), r, ALU.add, ALU.mult)
                ts(PI[:, :], k, 127.0, 8388608.0, ALU.add, ALU.mult)
                two_k = PI[:, :].bitcast(F32)
                tt(q, q, two_k, ALU.mult)
                if minus_one:
                    ts(c, two_k, -1.0, 0.0, ALU.add, ALU.add)
                    tt(dst, q, c, ALU.add)
                else:
                    tt(dst, q, two_k, ALU.add)

            a_re, a_im, dt = SA[:, 0, :], SA[:, 1, :], SA[:, 2, :]
            exponential(dt, dt, False)
            tt(W(0), a_re, dt, ALU.mult)
            exponential(W(1), W(0), True)
            tt(W(2), a_im, dt, ALU.mult)
            ts(W(3), W(2), 0.5 / math.pi, MAGIC, ALU.mult, ALU.add)
            ts(W(3), W(3), MAGIC, 0.0, ALU.subtract, ALU.add)
            stt(W(2), W(3), -6.28125, W(2), ALU.mult, ALU.add)
            stt(W(2), W(3), -0.00193500518798828125, W(2), ALU.mult, ALU.add)
            stt(W(2), W(3), -3.0199159819567521e-7, W(2), ALU.mult, ALU.add)
            ts(W(8), W(2), 0.5, 0.0, ALU.mult, ALU.add)
            stt(W(9), W(8), -1.0, W(8), ALU.mult, ALU.max)
            V_.tensor_scalar(W(9), W(9), -1.0, math.pi / 2, ALU.mult, ALU.add).then_inc(angle_ready, 1)
            dve.wait_ge(sine_ready, 1)
            sn, cm1, im, re, r1 = W(2), W(3), W(4), W(5), W(6)
            tt(sn, W(8), W(9), ALU.mult)
            ts(sn, sn, 2.0, 0.0, ALU.mult, ALU.add)
            tt(cm1, W(8), W(8), ALU.mult)
            ts(cm1, cm1, -2.0, 0.0, ALU.mult, ALU.add)
            ts(r1, W(1), 1.0, 0.0, ALU.add, ALU.add)
            tt(im, r1, sn, ALU.mult)
            ts(re, cm1, 1.0, 0.0, ALU.add, ALU.add)
            ts(ROTP[:, 0, 6, :], re, 1.0, 0.0, ALU.mult, ALU.add)
            ts(ROTP[:, 1, 6, :], sn, 1.0, 0.0, ALU.mult, ALU.add)
            tt(re, re, W(1), ALU.mult)
            tt(re, re, cm1, ALU.add)
            ts(LAM[:, 0, 1, :], re, 1.0, 0.0, ALU.add, ALU.add)
            ts(LAM[:, 1, 1, :], im, 1.0, 0.0, ALU.mult, ALU.add)
            tt(W(7), a_re, a_re, ALU.mult)
            tt(W(8), a_im, a_im, ALU.mult)
            tt(W(7), W(7), W(8), ALU.add)
            step(V_.reciprocal(W(7), W(7)))
            tt(W(8), re, a_re, ALU.mult)
            tt(W(9), im, a_im, ALU.mult)
            tt(W(8), W(8), W(9), ALU.add)
            tt(FAC[:, 0, :], W(8), W(7), ALU.mult)
            tt(W(8), im, a_re, ALU.mult)
            tt(W(9), re, a_im, ALU.mult)
            tt(W(8), W(8), W(9), ALU.subtract)
            tt(FAC[:, 1, :], W(8), W(7), ALU.mult)
            tt(W(7), r1, r1, ALU.mult)
            tt(RHO[:, :], W(7), W(7), ALU.mult)

            def product(out_re, out_im, x_re, x_im, y_re, y_im, sc):
                V_.tensor_tensor(sc[0], x_re, y_re, ALU.mult)
                V_.tensor_tensor(sc[1], x_im, y_im, ALU.mult)
                V_.tensor_tensor(sc[2], x_re, y_im, ALU.mult)
                tt(sc[3], x_im, y_re, ALU.mult)
                V_.tensor_tensor(out_re, sc[0], sc[1], ALU.subtract)
                tt(out_im, sc[2], sc[3], ALU.add)

            sc = [W(10), W(11), W(12), W(13)]
            for j in range(2, T + 1):
                product(LAM[:, 0, j, :], LAM[:, 1, j, :], LAM[:, 0, j - 1, :], LAM[:, 1, j - 1, :],
                        LAM[:, 0, 1, :], LAM[:, 1, 1, :], sc)
            for m in (-2, -1, 0, 1, 2, 3, 4):
                a, b = (6 if m < 0 else m), (6 if m == -2 else m + 1)
                product(ROTP[:, 0, b, :], ROTP[:, 1, b, :], ROTP[:, 0, a, :], ROTP[:, 1, a, :],
                        ROTP[:, 0, a, :], ROTP[:, 1, a, :], sc)

            V_.memset(ROT[:, 0, :, 0:1], 1.0)
            step(V_.memset(ROT[:, 1, :, 0:1], 0.0))
            HP = PAIRS // 2
            for m in range(int(math.log2(NC))):
                n = 1 << m
                for h in range(2):
                    pairs = slice(HP * h, HP * h + HP)
                    old = ROT[:, :, pairs, 0:n]
                    turn = lambda ri: ROTP[:, ri, m, pairs].unsqueeze(1).unsqueeze(3).to_broadcast([P, 2, HP, n])
                    V_.tensor_tensor(RA[:, :, :, 0:n], old, turn(0), ALU.mult)
                    tt(RB[:, :, :, 0:n], old, turn(1), ALU.mult)
                    V_.tensor_tensor(ROT[:, 0, pairs, n:2 * n], RA[:, 0, :, 0:n], RB[:, 1, :, 0:n], ALU.subtract)
                    last = V_.tensor_tensor(ROT[:, 1, pairs, n:2 * n], RA[:, 1, :, 0:n], RB[:, 0, :, 0:n], ALU.add)
                    if m == int(math.log2(NC)) - 1 and h == 1:
                        last.then_inc(rot_ready, 1)
                    else:
                        step(last)

            dve.wait_ge(masks_ready, 1)
            dve.wait_ge(rot_ready, 1)
            u0 = AT["build"]["u"]
            with nc.vector.Fori(0, KB) as b:
                step.enter(b, 3)
                pairs = bass.ds(b * QP, QP)
                dve.wait_ge(bc_in, b * 96 + 96)
                for g in range(2):
                    last = V_.tensor_scalar(CM[:, :, g, :], CN[:, :, :], PAR[:, g:g + 1], None, ALU.mult)
                last.then_inc(cm_ready, 1)
                bb = lambda ri: BD[:, ri, :, :, :].rearrange("p q g c -> p q (g c)")
                fac = lambda ri: FAC[:, ri, pairs].unsqueeze(2).to_broadcast([P, QP, 32])
                s4 = [x_[:, 0, :].rearrange("p (q c) -> p q c", q=QP) for x_ in (TA, TB, TC, TDD)]
                o3 = lambda ri: QT[:, 0, ri, :].rearrange("p (q c) -> p q c", q=QP)
                V_.tensor_tensor(s4[0], bb(0), fac(0), ALU.mult)
                V_.tensor_tensor(s4[1], bb(1), fac(1), ALU.mult)
                V_.tensor_tensor(s4[2], bb(0), fac(1), ALU.mult)
                V_.tensor_tensor(s4[3], bb(1), fac(0), ALU.mult).then_inc(bc_used, 1)
                dve.wait_ge(bc_used, b + 2)
                V_.tensor_tensor(o3(0), s4[0], s4[1], ALU.subtract)
                tt(o3(1), s4[2], s4[3], ALU.add)
                lam = lambda ri, j0, j1: LAM[:, ri, j0:j1, pairs].unsqueeze(3).to_broadcast([P, j1 - j0, QP, 32])
                rep = lambda x_, n_: x_.rearrange("p (q c) -> p q c", q=QP).unsqueeze(1).to_broadcast([P, n_, QP, 32])
                cut = lambda x_, n_: x_[:, 0:n_, :].rearrange("p j (q c) -> p j q c", q=QP)
                J = T - 1
                V_.tensor_tensor(cut(TA, J), rep(QT[:, 0, 0, :], J), lam(0, 1, T), ALU.mult)
                V_.tensor_tensor(cut(TB, J), rep(QT[:, 0, 1, :], J), lam(1, 1, T), ALU.mult)
                V_.tensor_tensor(cut(TC, J), rep(QT[:, 0, 0, :], J), lam(1, 1, T), ALU.mult)
                tt(cut(TDD, J), rep(QT[:, 0, 1, :], J), lam(0, 1, T), ALU.mult)
                V_.tensor_tensor(QT[:, 1:T, 0, :], TA[:, 0:J, :], TB[:, 0:J, :], ALU.subtract)
                V_.tensor_tensor(QT[:, 1:T, 1, :], TC[:, 0:J, :], TDD[:, 0:J, :], ALU.add).then_inc(qt_ready, 1)
                dve.wait_ge(acc_free, b * 2 + (u0 + 1))
                dve.wait_ge(qt_ready, b + 1)
                V_.tensor_tensor(cut(TA, T), rep(DT[:, 0, 0, :], T), lam(0, 1, T + 1), ALU.mult)
                V_.tensor_tensor(cut(TB, T), rep(DT[:, 0, 1, :], T), lam(1, 1, T + 1), ALU.mult)
                V_.tensor_tensor(cut(TC, T), rep(DT[:, 0, 1, :], T), lam(0, 1, T + 1), ALU.mult)
                tt(cut(TDD, T), rep(DT[:, 0, 0, :], T), lam(1, 1, T + 1), ALU.mult)
                V_.tensor_tensor(DT[:, 1:T + 1, 0, :], TA[:, :, :], TB[:, :, :], ALU.add)
                V_.tensor_tensor(DT[:, 1:T + 1, 1, :], TC[:, :, :], TDD[:, :, :], ALU.subtract).then_inc(dt_ready, 1)
                dve.wait_ge(dt_ready, b + 1)
            step.leave(KB)

            for j in range(RING):
                split(j, j)
            with nc.vector.Fori(0, NT // 2) as e:
                splits("v", e, 2 * KT, 0, 2 * KT)

            def norm_chunk(c):
                f = slice(NW * c, NW * c + NW)
                for i, op in enumerate((ALU.mult, ALU.add)):
                    last = V_.tensor_tensor(V[:, :, f], V[:, :, f], LG[:, i, f].unsqueeze(1).to_broadcast([P, 2, NW]), op)
                    if i == 0:
                        step(last)
                if c == NT - 1:
                    last.then_inc(v_ready, 1)

            a = AT["us"]
            dve.wait_ge(acc_free, a["u"])
            dve.wait_ge(ln_in, 48)
            for th in range(2):
                for c in range(NT):
                    last = V_.bn_stats(STAT[:, th, 6 * c:6 * c + 6], V[:, th, NW * c:NW * c + NW])
            step(last)
            splits("us", 0, KT, 0, 2)
            V_.bn_aggr(MV[:, 0, :], STAT[:, 0, :])
            V_.bn_aggr(MV[:, 1, :], STAT[:, 1, :]).then_inc(ln_var, 1)
            splits("us", 0, KT, 2, 2)
            dve.wait_ge(ln_root, 1)
            step(V_.reciprocal(LNR[:, :, :], LNR[:, :, :]))
            for th in range(2):
                last = V_.tensor_scalar(V[:, th, :], V[:, th, :], MV[:, th, 0:1], LNR[:, th, :], ALU.subtract, ALU.mult)
            step(last)
            for c in range(NT):
                splits("us", 0, KT, 4 + c, 1)
                norm_chunk(c)

            def us(n):
                u = n * 2 + a["u"]
                total(u, 0, n + a["cross"], flat3(Z))
                scaled(flat3(Z), z_ready)
                dve.wait_ge(nl_ready, n + (a["nl"] + 1))
                dve.wait_ge(acc_done, n + (a["o"] + 1))
                V_.tensor_tensor(flat3(Z), quad(1, 0), flat3(T1), ALU.mult).then_inc(acc_free, 1)
                dve.wait_ge(acc_free, u + 2)
                dve.wait_ge(operand_hi, n * 2 + (a["q"] + 2))
                blocks = bass.ds(n * QB + KB, QB)
                V_.tensor_tensor(M[:, blocks, TOK:2 * TOK], flat3(Z), M[:, blocks, 0:TOK].bitcast(F32),
                                 ALU.subtract).then_inc(operand_ready, 2)

            us(0)
            with nc.vector.Fori(1, NT) as n:
                splits("us", n, KT, 0, KT)
                us(n)

            def residual_stage(stage, depth, vec):
                a = AT[stage]
                with nc.vector.Fori(0, NT // 2) as e:
                    step.enter(e, 4)
                    for s in range(2):
                        splits(stage, e, 2 * depth, depth * s, depth)
                        n = e * 2 + s
                        xq = X[:, bass.ds(n * (QB * TOK), QB * TOK)].rearrange("p (m t) -> p m t", t=TOK)
                        dve.wait_ge(split_used, n * depth + (a["t"] + depth))
                        step(V_.tensor_tensor(xq, xq, quad(s, TOK), ALU.add))
                        V_.tensor_tensor(xq, xq, quad(s, 0), ALU.add).then_inc(acc_free, 1)
                        dve.wait_ge(acc_free, n + (a["u"] + 1))
                        low_parts(n, vec, H, n * 2 + a["q"])
                        sum_squares(n + a["r"])
                step.leave(NT // 2)

            def gated_quad(stage, n, vec, dst, other):
                a = AT[stage]
                dve.wait_ge(nl_ready, n + (a["nl"] + 1))
                step(V_.tensor_tensor(Z[:, :], T1[:, :], other, ALU.mult))
                xq = X[:, bass.ds(n * (QB * TOK), QB * TOK)]
                V_.tensor_tensor(xq, xq, Z[:, :], ALU.add).then_inc(gated_ready, 1)
                dve.wait_ge(gated_ready, n + (a["g"] + 1))
                if dst is not None:
                    low_parts(n, vec, dst, n * 2 + a["q"])
                sum_squares(n + a["r"])

            def ffn_and_gate(i, k):
                a = AT[f"up{i}"]
                with nc.vector.Fori(0, NU) as n:
                    blocks = bass.ds(n * QB, QB)
                    splits(f"up{i}", n, 2 * KT, 0, KT)
                    total(n * 2 + a["u"], 0, n * 2 + a["cross"], flat3(Z))
                    scaled(flat3(Z), z_ready)
                    step.enter(n, 1)
                    splits(f"up{i}", n, 2 * KT, KT, KT)
                    dve.wait_ge(nl_ready, n + (a["nl"] + 1))
                    total(n * 2 + (a["u"] + 1), 1, n * 2 + (a["cross"] + 1), flat3(Z))
                    scaled(flat3(Z), dve_chain)
                    step.n += 1
                    dve.wait_ge(dve_chain, n + (step.base + 1))
                    V_.tensor_tensor(flat3(Z), flat3(Z), GATED[:, blocks, 1, :], ALU.mult).then_inc(z_ready, 1)
                    dve.wait_ge(z_ready, n * 2 + (a["z"] + 2))
                    dve.wait_ge(operand_hi, n * 2 + (a["q"] + 2))
                    V_.tensor_tensor(M[:, blocks, TOK:2 * TOK], flat3(Z), M[:, blocks, 0:TOK].bitcast(F32),
                                     ALU.subtract).then_inc(operand_ready, 2)
                step.leave(NU)
                residual_stage(f"down{i}", FT, 4 + i)
                a = AT[f"proj{i}"]
                for n in range(NT):
                    splits(f"proj{i}", 0, NT, n, 1)
                    total(a["u"] + n, n % 2, a["cross"] + n,
                          PROJ[:, QB * TOK * n:QB * TOK * (n + 1)].rearrange("p (m t) -> p m t", t=TOK))
                rstd(k)
                a = AT[f"gate{i}"]
                if i == 0:
                    with nc.vector.Fori(0, NT // 2) as e:
                        step.enter(e, 4)
                        for s in range(2):
                            n = e * 2 + s
                            splits("gate0", e, 2 * KT, KT * s, KT)
                            total(n + a["u"], s, n + a["cross"], flat3(Z))
                            scaled(flat3(Z), z_ready)
                            gated_quad("gate0", n, 1, M, PROJ[:, bass.ds(n * (QB * TOK), QB * TOK)])
                    step.leave(NT // 2)
                else:
                    for n in range(NT):
                        splits("gate1", 0, KT, KT * n, KT if n < NT - 1 else KT - RING)
                        total(n + a["u"], n % 2, n + a["cross"], flat3(Z))
                        scaled(flat3(Z), z_ready)
                        gated_quad("gate1", n, None, None, PROJ[:, QB * TOK * n:QB * TOK * (n + 1)])

            residual_stage("out0", KT, 2)
            rstd(2)
            ffn_and_gate(0, 3)
            rstd(4)
            a = AT["win"]
            with nc.vector.Fori(0, NT // 2) as e:
                for s in range(2):
                    n = e * 2 + s
                    splits("win", e, 2 * KT, KT * s, KT)
                    total(n + a["u"], s, n + a["cross"], flat3(Z))
                    scaled(UF[:, bass.ds(n * QB, QB), 1, :], u_ready)

            a = AT["core"]
            u0 = a["u"]

            def scan_duo(d, par, u, s, rounds):
                dve.wait_ge(tab_in[par], rounds * 128)
                dve.wait_ge(acc_done, u + (1 + a["o"] - a["u"]))
                for bl in range(2):
                    cos, sin = TE[par][:, bl, 0, :, :], TE[par][:, bl, 1, :, :]
                    inc = PS[:, QB * s:QB * s + QB, P * bl:P * bl + P].rearrange("p q (r k) -> p q r k", r=2)
                    both = lambda x_: x_.unsqueeze(2).to_broadcast([P, QP, 2, NC])
                    V_.tensor_tensor(CA[:, :, :, :], inc, both(cos), ALU.mult)
                    last = V_.tensor_tensor(CB[:, :, :, :], inc, both(sin), ALU.mult)
                    if bl == 1:
                        last.then_inc(acc_free, 1)
                        dve.wait_ge(acc_free, u + 1)
                    else:
                        step(last)
                    V_.tensor_tensor(CV[:, 0, :, :], CA[:, :, 0, :], CB[:, :, 1, :], ALU.add)
                    step(V_.tensor_tensor(CV[:, 1, :, :], CA[:, :, 1, :], CB[:, :, 0, :], ALU.subtract))
                    dve.wait_ge(rt_ready, d * 2 + (bl + 1))
                    for ri in range(2):
                        last = V_.tensor_tensor_scan(CW[:, ri, :, :].rearrange("p q k -> p (q k)"),
                                                     RT[:, :, :].rearrange("p q k -> p (q k)"),
                                                     CV[:, ri, :, :].rearrange("p q k -> p (q k)"), 0.0, ALU.mult, ALU.add)
                    last.then_inc(rt_used, 1)
                    dve.wait_ge(rt_used, d * 2 + (bl + 1))
                    flat = lambda x_: x_.rearrange("p a b k -> p (a b k)").rearrange("p (r n) -> p r n", r=2)
                    one = lambda x_: x_.rearrange("p q k -> p (q k)").unsqueeze(1).to_broadcast([P, 2, QP * NC])
                    w = CW[:, :, :, :].rearrange("p r q k -> p r (q k)")
                    V_.tensor_tensor(flat(CA[:, :, :, :]), w, one(cos), ALU.mult)
                    step(V_.tensor_tensor(flat(CB[:, :, :, :]), w, one(sin), ALU.mult))
                    part = lambda x_, ri: flat(x_[:, :, :, :])[:, ri, :].rearrange("p (q k) -> p q k", k=NC)[:, :, 0:NC - 1]
                    V_.tensor_tensor(SD[:, par, bl, 0, :, 1:NC], part(CA, 0), part(CB, 1), ALU.subtract)
                    last = V_.tensor_tensor(SD[:, par, bl, 1, :, 1:NC], part(CA, 1), part(CB, 0), ALU.add)
                    if bl == 0:
                        step(last)
                last.then_inc(sd_ready, 1)
                dve.wait_ge(sd_ready, d + 1)

            def outputs(d, u, s):
                dve.wait_ge(acc_done, u + (1 + a["o"] - a["u"]))
                for bl in range(2):
                    k = d * 2 + bl
                    last = V_.scalar_tensor_tensor(Z[:, TOK * bl:TOK * bl + TOK].rearrange("p (k j) -> p k j", j=T),
                                                   UF[:, bass.ds(k, 1), 1, :].rearrange("p b (k j) -> p (b k) j", j=T),
                                                   VEC[:, 7, bass.ds(k, 1)],
                                                   PS[:, QB * s + bl, 0:TOK].rearrange("p (j k) -> p k j", j=T),
                                                   ALU.mult, ALU.add)
                last.then_inc(acc_free, 1)
                dve.wait_ge(operand_hi, d + (a["q"] + 1))
                blocks = bass.ds(d * 2 + KB, 2)
                V_.tensor_tensor(M[:, blocks, TOK:2 * TOK], T1[:, 0:2 * TOK].rearrange("p (b t) -> p b t", t=TOK),
                                 M[:, blocks, 0:TOK].bitcast(F32), ALU.subtract).then_inc(operand_ready, 1)

            dve.wait_ge(core_ready, 1)
            scan_duo(0, 0, u0, 0, 1)
            with nc.vector.Fori(0, DUOS // 2 - 1) as e:
                step.enter(e, 12)
                for par in range(2):
                    d = e * 2 + par
                    scan_duo(d + 1, 1 - par, d * 2 + (u0 + 1), 1, e + (1 + par))
                    outputs(d, d * 2 + (u0 + 2), 0)
            step.leave(DUOS // 2 - 1)
            scan_duo(DUOS - 1, 1, u0 + 2 * DUOS - 3, 1, DUOS // 2)
            outputs(DUOS - 2, u0 + 2 * DUOS - 2, 0)
            outputs(DUOS - 1, u0 + 2 * DUOS - 1, 1)

            a = AT["out1"]
            with nc.vector.Fori(0, NT) as n:
                step.enter(n, 2)
                u = n * 2 + a["u"]
                splits("out1", n, 2 * KT, 0, KT)
                total(u, 0, n * 2 + a["cross"], flat3(VAL))
                splits("out1", n, 2 * KT, KT, KT)
                total(u + 1, 1, n * 2 + (a["cross"] + 1), flat3(Z))
                gated_quad("out1", n, 3, H, VAL[:, :])
            step.leave(NT)
            rstd(5)
            ffn_and_gate(1, 6)
            rstd(7)
            for n in range(NT):
                if n >= 2:
                    dve.wait_ge(acc_done, AT["fin"]["o"] + n)
                for m in range(QB):
                    k = QB * n + m
                    last = V_.tensor_scalar(XF[:, n % 2, m, :], X[:, TOK * k:TOK * k + TOK], VEC[:, 6, k:k + 1], None, ALU.mult)
                last.then_inc(xf_ready, 1)

        @block.tensor
        def _(pe):
            def free(u):
                pe.wait_ge(acc_free, u - 1)

            def products(t0, u, s, depth, operand, ready, q, j0=0):
                free(u)
                for j in range(depth):
                    slot = (j0 + j) % RING
                    pe.wait_ge(ready, q + j + 1)
                    pe.wait_ge(lo_ready, t0 + (j + 1))
                    for kk in range(TK):
                        k = TK * j + kk
                        for m in range(QB):
                            w = slice(NW * kk + P * m, NW * kk + P * m + P)
                            nc.tensor.matmul(PS[:, QB * s + m, :], WHI[:, slot, w], operand(k), start=(k == 0), stop=False)
                            last = nc.tensor.matmul(PS[:, QB * s + m, TOK:2 * TOK], WLO[:, slot, w], operand(k)[:, 0:TOK],
                                                    start=False, stop=(k == TK * depth - 1))
                    last.then_inc(split_used, 1)

            in_h = lambda k: H[:, k, :]
            in_m = lambda k: M[:, k, :]
            in_m2 = lambda k: M[:, KB + k, :]

            pe.wait_ge(small_in, 16 * 13)
            pe.wait_ge(ident_ready, 1)
            pe.wait_ge(ldt_spread, 1)
            nc.tensor.transpose(PS[:, 0, 0:P], NAT[:, :], IDENT[:, :])
            for i in range(3):
                last = nc.tensor.transpose(PS[:, 1 + i, 0:PAIRS], AN[:, i, :], IDENT[0:PAIRS, 0:PAIRS])
            last.then_inc(acc_done, 1)
            pe.wait_ge(x_in, 16)
            for n in range(NT):
                if n >= 1:
                    free(n + 1)
                for m in range(QB):
                    for th in range(2):
                        k = QB * n + m
                        last = nc.tensor.transpose(PS[:, QB * ((n + 1) % 2) + m, P * th:P * th + P],
                                                   XN[:, th, P * k:P * k + P], IDENT[:, :])
                last.then_inc(acc_done, 1)
            pe.wait_ge(ws_masked, 1)
            free(5)
            for h in range(HEADS):
                last = nc.tensor.transpose(PS[:, 4 + h // 4, P * (h % 4):P * (h % 4) + P], WN[:, h, :], IDENT[:, :])
            last.then_inc(acc_done, 1)

            def to_column(u, k):
                free(u)
                pe.wait_ge(rstd_ready, k)
                for th in range(2):
                    last = nc.tensor.matmul(PS[:, 0, th:th + 1], RSTD[0:1, P * th:P * th + P], ONE[0:1, 0:1],
                                            start=True, stop=True)
                last.then_inc(acc_done, 1)

            pe.wait_ge(masks_ready, 1)
            to_column(6, 1)
            free(7)
            for l in range(2):
                for f in range(2):
                    for th in range(2):
                        i = 2 * l + f
                        last = nc.tensor.transpose(PS[:, 4 + i // 2, TOK * (i % 2) + P * th:TOK * (i % 2) + P * th + P],
                                                   PN[:, l, th, P * f:P * f + P], IDENT[:, :])
            last.then_inc(acc_done, 1)

            u0 = AT["build"]["u"]
            with nc.tensor.Fori(0, KB) as b:
                free(b * 2 + u0)
                pe.wait_ge(cm_ready, b + 1)
                for ri in range(2):
                    last = nc.tensor.transpose(PS[:, 0, P * ri:P * ri + P], CM[:, ri, :, :].rearrange("p g s -> p (g s)"),
                                               IDENT[:, :])
                last.then_inc(acc_done, 1)
                free(b * 2 + (u0 + 1))
                pe.wait_ge(qt_ready, b + 1)
                for j in range(T):
                    for ri in range(2):
                        i = 2 * j + ri
                        nc.tensor.transpose(PS[:, 4 + i // 4, P * (i % 4):P * (i % 4) + P], QT[:, j, ri, :], IDENT[:, :])
                pe.wait_ge(dt_ready, b + 1)
                for q in range(QP):
                    r = slice(32 * q, 32 * q + 32)
                    for ri in range(2):
                        last = nc.tensor.matmul(PS[r, 6, 0:P], QT[:, 0, ri, r], DT[:, 0:T, ri, r],
                                                start=(ri == 0), stop=(ri == 1))
                last.then_inc(acc_done, 1)

            a = AT["v"]
            with nc.tensor.Fori(0, NT // 2) as e:
                for s in range(2):
                    free(e * 2 + (a["u"] + s))
                    for j in range(KT):
                        slot = j % RING
                        pe.wait_ge(operand_ready, j + 1)
                        pe.wait_ge(lo_ready, e * (2 * KT) + (a["t"] + KT * s + j + 1))
                        for kk in range(TK):
                            k = TK * j + kk
                            f = slice(NW * kk, NW * kk + NW)
                            for th in range(2):
                                acc = PS[:, QB * s + th, :]
                                hi, lo = M[:, k, P * th:P * th + P], M[:, k, TOK + P * th:TOK + P * th + P]
                                nc.tensor.matmul(acc, hi, WHI[:, slot, f], start=(k == 0), stop=False)
                                nc.tensor.matmul(acc, hi, WLO[:, slot, f], start=False, stop=False)
                                last = nc.tensor.matmul(acc, lo, WHI[:, slot, f], start=False, stop=(k == KB - 1))
                        last.then_inc(split_used, 1)

            a = AT["us"]
            for n in range(NT):
                products(a["t"] + KT * n, a["u"] + 2 * n, 0, KT, in_m, operand_ready, 0)
                free(a["u"] + 2 * n + 1)
                pe.wait_ge(v_ready, 1)
                for m in range(QB):
                    h = QB * n + m
                    for c in range(2):
                        nc.tensor.matmul(PS[:, QB + m, P * c:P * c + P], V[:, c, P * h:P * h + P], WT[:, h, :],
                                         start=(c == 0), stop=False)
                    last = nc.tensor.matmul(PS[:, QB + m, 0:TOK].rearrange("p (c t) -> p c t", c=2), ONE[0:1, :],
                                            BS[0:1, h, :].unsqueeze(1).to_broadcast([1, 2, P]), start=False, stop=True)
                last.then_inc(acc_done, 1)

            def stage(name, depth, operand, ready, q):
                a = AT[name]
                with nc.tensor.Fori(0, NT // 2) as e:
                    for s in range(2):
                        products(e * (2 * depth) + (a["t"] + depth * s), e * 2 + (a["u"] + s), s, depth, operand, ready, q,
                                 j0=depth * s)

            def ffn_and_gate(i):
                a = AT[f"up{i}"]
                with nc.tensor.Fori(0, NU) as n:
                    for s in range(2):
                        products(n * (2 * KT) + (a["t"] + KT * s), n * 2 + (a["u"] + s), s, KT, in_h, operand_ready, a["q"] - KT)
                stage(f"down{i}", FT, in_m, operand_ready, AT[f"down{i}"]["q"] - FT)
                a = AT[f"proj{i}"]
                for n in range(NT):
                    products(a["t"] + n, a["u"] + n, n % 2, 1, lambda k: PT[:, 2 * i + k, :], acc_free, 7, j0=n)
                stage(f"gate{i}", KT, in_h, operand_ready, AT[f"gate{i}"]["q"] - KT)

            stage("out0", KT, in_m2, operand_ready, AT["out0"]["q"] - KT)
            ffn_and_gate(0)
            stage("win", KT, in_m, operand_ready, AT["win"]["q"] - KT)

            a = AT["core"]

            def into_states(d, par, u, s, rounds):
                free(u)
                pe.wait_ge(tab_in[par], rounds * 128)
                pe.wait_ge(ud_ready, d + 1)
                for bl in range(2):
                    for ri in range(2):
                        for j in range(T):
                            for q in range(QP):
                                r = slice(32 * q, 32 * q + 32)
                                c0 = P * bl + NC * ri
                                last = nc.tensor.matmul(PS[:, QB * s + q, c0:c0 + NC], TQ[par][r, bl, T - 1 - j, ri, :],
                                                        UD[r, par, bl, j, :], start=(j == 0), stop=(j == T - 1))
                last.then_inc(acc_done, 1)

            def out_of_states(d, par, u, s):
                free(u)
                pe.wait_ge(sd_ready, d + 1)
                for bl in range(2):
                    for j in range(T):
                        nc.tensor.matmul(PS[:, QB * s + bl, NC * j:TOK], TKK[par][:, bl, j, :],
                                         UD[:, par, bl, 0:T - j, :].rearrange("p j k -> p (j k)"), start=(j == 0), stop=False)
                    for j in range(T):
                        for ri in range(2):
                            for q in range(QP):
                                r = slice(32 * q, 32 * q + 32)
                                last = nc.tensor.matmul(PS[r, QB * s + bl, NC * j:NC * j + NC], TD[par][:, bl, j, ri, r],
                                                        SD[:, par, bl, ri, q, :], start=False, stop=(j == T - 1 and ri == 1))
                last.then_inc(acc_done, 1)

            into_states(0, 0, a["u"], 0, 1)
            with nc.tensor.Fori(0, DUOS // 2 - 1) as e:
                for par in range(2):
                    d = e * 2 + par
                    into_states(d + 1, 1 - par, d * 2 + (a["u"] + 1), 1, e + (1 + par))
                    out_of_states(d, par, d * 2 + (a["u"] + 2), 0)
            into_states(DUOS - 1, 1, a["u"] + 2 * DUOS - 3, 1, DUOS // 2)
            out_of_states(DUOS - 2, 0, a["u"] + 2 * DUOS - 2, 0)
            out_of_states(DUOS - 1, 1, a["u"] + 2 * DUOS - 1, 1)

            a = AT["out1"]
            with nc.tensor.Fori(0, NT) as n:
                for s in range(2):
                    products(n * (2 * KT) + (a["t"] + KT * s), n * 2 + (a["u"] + s), s, KT, in_m2, operand_ready, a["q"] - KT)
            ffn_and_gate(1)

            a = AT["fin"]
            to_column(a["u"], 7)
            for n in range(NT):
                s = (n + 1) % 2
                if n >= 1:
                    pe.wait_ge(acc_free, a["u"] + 1) if n == 1 else pe.wait_ge(out_ready, n - 1)
                pe.wait_ge(xf_ready, n + 1)
                for m in range(QB):
                    for th in range(2):
                        last = nc.tensor.transpose(PS[:, QB * s + th, P * m:P * m + P], XF[:, n % 2, m, P * th:P * th + P],
                                                   IDENT[:, :])
                last.then_inc(acc_done, 1)


INPUTS = ["x", "p", "norm_mix", "norm_ffn", "norm_ple", "norm_final", "gm_w_in", "gm_ln_g", "gm_ln_b", "gm_w_s", "gm_b_s",
          "gm_w_out", "s5_w_in", "s5_a_re", "s5_a_im", "s5_log_dt", "s5_b_re", "s5_b_im", "s5_c_re", "s5_c_im", "s5_d",
          "s5_w_out", "ffn_w1", "ffn_w3", "ffn_w2", "ple_w_gate", "ple_w_proj"]


def kernel(**inputs):
    import numpy as np
    import concourse.bacc as bacc
    from concourse.bass_utils import run_bass_kernel_spmd

    nc = bacc.Bacc("TRN2", target_bir_lowering=False, num_devices=1)
    arrays, args = {}, []
    for name in INPUTS:
        a = np.ascontiguousarray(inputs[name])
        arrays[f"in_{name}"] = a
        args.append(nc.dram_tensor(f"in_{name}", a.shape, mybir.dt.from_np(a.dtype), kind="ExternalInput").ap())
    args.append(nc.dram_tensor("out", (1, TOK, D), F32, kind="ExternalOutput").ap())
    trunk(nc, *args)
    return run_bass_kernel_spmd(nc, [arrays], core_ids=[0]).results[0]["out"]
```

```python
import math
from contextlib import ExitStack

import concourse.bass as bass
from concourse import mybir

F32 = mybir.dt.float32
F32R = mybir.dt.float32r
I32 = mybir.dt.int32
ACT = mybir.ActivationFunctionType
ALU = mybir.AluOpType
AX = mybir.AxisListType
RADD = bass.bass_isa.ReduceOp.add

P = 128
TOK = 256
D = 2048
KB = D // P
DFF = 5632
FB = DFF // P
NW = 512
QB = NW // P
NT = D // NW
TK = 2
KT = KB // TK
FT = FB // TK
NU = DFF // NW
RING = 4
PLE = 256
EPS = 1e-6
HEADS = 16

GROUPS = 128
CH = 16
ST = 64
T = 4
NC = TOK // T
PAIRS = GROUPS // 2
QP = 4
DUOS = KB // 2

STAGES = [
    ("pro", 1, dict(a=5, q=8, r=4)),
    ("set-up", 1, dict(a=3)),
    ("v", NT, dict(t=KT, c=1)),
    ("us", NT, dict(t=KT, c=1, a=1, cross=1, z=1, nl=1, q=2)),
    ("out0", NT, dict(t=KT, c=1, q=2, r=1)),
    ("first", 1, dict(a=1)),
    ("build", KB, dict(a=1)),
    ("up0", NU, dict(t=2 * KT, c=2, cross=2, z=2, nl=1, q=2)),
    ("down0", NT, dict(t=FT, c=1, q=2, r=1)),
    ("proj0", NT, dict(t=1, c=1)),
    ("gate0", NT, dict(t=KT, c=1, cross=1, z=1, nl=1, g=1, q=2, r=1)),
    ("win", NT, dict(t=KT, c=1)),
    ("core", DUOS, dict(q=1)),
    ("value0", 1, dict(cross=-1)),
    ("out1", NT, dict(t=2 * KT, c=2, cross=2, nl=1, g=1, q=2, r=1)),
    ("up1", NU, dict(t=2 * KT, c=2, cross=2, z=2, nl=1, q=2)),
    ("down1", NT, dict(t=FT, c=1, q=2, r=1)),
    ("proj1", NT, dict(t=1, c=1)),
    ("gate1", NT, dict(t=KT, c=1, cross=1, z=1, nl=1, g=1, r=1)),
    ("fin", 1, dict(a=5)),
]

SCAN = [KT * (n + 1) + 3 + 2 * i if n < NT - 1 else KT * NT + 3 + min(i, 2) for n in range(NT) for i in range(QB)]
OUT = [SCAN[2 * d + 1] + 2 if d < DUOS - 2 else KT * NT + 5 for d in range(DUOS)]
HI = [min(OUT[d] + 2, KT * NT - 1 + d) for d in range(DUOS)]
LO = [min(OUT[d] + 3, KT * NT - 1 + d) for d in range(DUOS)]
CORE_TILES = KT * (NT + 1)
MID = 4


def plan():
    at, now = {}, dict(t=0, c=0, a=0, cross=0, z=0, nl=0, g=0, q=0, r=0)
    for name, times, per in STAGES:
        at[name] = dict(now)
        assert now["t"] % RING == 0 and now["c"] % 2 == 0
        for k, v in per.items():
            now[k] += v * times
    at["end"] = now
    return at


AT = plan()


class Chain:

    def __init__(self, eng, sem):
        self.eng, self.sem, self.n, self.base, self.i, self.per = eng, sem, 0, 0, 0, 0

    def __call__(self, ins):
        ins.then_inc(self.sem, 1)
        self.n += 1
        self.eng.wait_ge(self.sem, self.base + self.i * self.per + self.n)

    def enter(self, i, per):
        self.base, self.i, self.per, self.n = self.base + self.n, i, per, 0

    def leave(self, times):
        assert self.n == self.per, (self.n, self.per)
        self.base, self.i, self.n = self.base + self.per * times, 0, 0


def trunk(nc, x, p, norm_mix, norm_ffn, norm_ple, norm_final, gm_w_in, gm_ln_g, gm_ln_b, gm_w_s, gm_b_s,
          gm_w_out, s5_w_in, s5_a_re, s5_a_im, s5_log_dt, s5_b_re, s5_b_im, s5_c_re, s5_c_im, s5_d,
          s5_w_out, ffn_w1, ffn_w3, ffn_w2, ple_w_gate, ple_w_proj, out):
    ctx = ExitStack()
    with ctx:
        def sem(name):
            return ctx.enter_context(nc.semaphore(name))

        KBYTE = 1024
        ARENA = 207 * KBYTE
        base = (nc.sbuf_base + 63) // 64 * 64
        arena = ctx.enter_context(nc.sbuf_tensor("arena", [P, ARENA // 4], F32))
        top = [base]

        def place(name, shape, dt=F32, at=None):
            size = 4
            for s in shape[1:]:
                size *= s
            if at is None:
                at = top[0]
                top[0] += (size + 31) // 32 * 32
                assert top[0] <= base + ARENA, name
            return nc.alloc_sbuf_tensor_at(name, shape, dt, offset=at)

        X = place("X", [P, D // P * TOK])
        h_at = top[0]
        H = place("H", [P, KB, 2 * TOK], F32R)
        m_at = top[0]
        M = place("M", [P, FB, 2 * TOK], F32R)
        RAW = place("RAW", [P, RING, TK * NW])
        WHI = place("WHI", [P, RING, TK * NW], F32R)
        WLO = place("WLO", [P, RING, TK * NW], F32R)
        t1_at = top[0]
        T1 = place("T1", [P, QB * TOK])
        z_at = top[0]
        Z = place("Z", [P, QB * TOK])
        pt_at = top[0]
        PT = place("PT", [P, 2 * (PLE // P), 2 * TOK], F32R)
        IDENT = place("IDENT", [P, P])
        VEC = place("VEC", [P, 8, KB])
        SS = place("SS", [P, TOK])
        SUM = place("SUM", [P, TOK])
        RSTD = place("RSTD", [P, TOK])
        RCOL = place("RCOL", [P, 2])
        ONE = place("ONE", [1, P])
        RHO = place("RHO", [P, PAIRS])
        PAR = place("PAR", [P, 2])
        STAT = place("STAT", [P, 2, 4 * 6])
        MV = place("MV", [P, 2, 2])
        LNR = place("LNR", [P, 2, 1])
        EPSB = place("EPSB", [P, 1])
        BAND = place("BAND", [P, QP])
        DIAG = place("DIAG", [P, 2, 2 * CH])
        ZERO = place("ZERO", [1, P], F32R)
        DG = place("DG", [P, P])

        def h_view(name, shape, off, dt=F32):
            return place(name, shape, dt, at=h_at + off * KBYTE)

        def m_view(name, shape, off, dt=F32):
            return place(name, shape, dt, at=m_at + int(off * KBYTE))

        def shared(whole, lo, name, shape):
            return place(name, shape, F32, at=whole + 4 * lo)

        XN = m_view("XN", [P, 2, D], 32)
        WN = m_view("WN", [P, HEADS, P], 48)
        NAT = m_view("NAT", [P, P], 56)
        AN = m_view("AN", [PAIRS, 3, P], 57)
        LDN = m_view("LDN", [PAIRS, 2], 59)
        PN = m_view("PN", [P, 2, 2, PLE], 60)
        V = h_view("V", [P, 2, D], 0)
        WT = h_view("WT", [P, HEADS, P], 16)
        BS = h_view("BS", [1, HEADS, P], 24)
        LG = m_view("LG", [P, 2, D], 64)
        SV = m_view("SV", [P, QB, TOK], 80)
        PW = m_view("PW", [P, 18, PAIRS], 32)
        SA = m_view("SA", [P, 3, PAIRS], 37)
        PI = m_view("PI", [P, PAIRS], 38, I32)
        LAM = m_view("LAM", [P, 2, T + 1, PAIRS], 84)
        FAC = m_view("FAC", [P, 2, PAIRS], 86.5)
        TURN = m_view("TURN", [P, 2, PAIRS], 87)
        ROT = m_view("ROT", [P, 2, PAIRS, NC], 0)
        ROTP = m_view("ROTP", [P, 6, 2, PAIRS], 64)
        RA = m_view("RA", [P, 2, PAIRS // 2, NC // 2], 68)
        RB = m_view("RB", [P, 2, PAIRS // 2, NC // 2], 76)
        QT = m_view("QT", [P, QP, 2, T, 2 * CH], 64)
        DT = m_view("DT", [P, QP, 2, T + 1, 2 * CH], 68)
        QS = m_view("QS", [P, QP, 2, P], 73)
        QTA = m_view("QTA", [P, QP, T - 1, 2 * CH], 77)
        QTB = m_view("QTB", [P, QP, T - 1, 2 * CH], 78.5)
        DTA = m_view("DTA", [P, QP, 2, 2 * CH], 80)
        DTB = m_view("DTB", [P, QP, 2, 2 * CH], 81)
        BD = m_view("BD", [P, 2, QP, 2, CH], 82)
        CM = m_view("CM", [P, 2, 2, ST], 83)
        KS = m_view("KS", [P, (T - 1) * 2 * CH + P], 87)
        LAMB = m_view("LAMB", [P, 2, T, QP], 87.875)
        TQ = [h_view("TQ0", [P, 2, QP, 2, P], 0), m_view("TQ1", [P, 2, QP, 2, P], 64)]
        TD = [h_view("TD0", [P, 2, QP, 2, P], 8), m_view("TD1", [P, 2, QP, 2, P], 72)]
        TKK = [h_view("TK0", [P, 2, QP, P], 16), m_view("TK1", [P, 2, QP, P], 80)]
        TE = [h_view("TE0", [P, 2, 2, QP, NC], 20), m_view("TE1", [P, 2, 2, QP, NC], 84)]
        CA = h_view("CA", [P, QP, 2, NC], 24)
        CB = h_view("CB", [P, QP, 2, NC], 26)
        CV = h_view("CV", [P, 2, QP, NC], 28)
        RT = [h_view("RT0", [P, QP, NC], 30), h_view("RT1", [P, QP, NC], 31)]
        UC = [m_view(f"UC{n}", [P, QB, T, NC], 32 + 8 * n) for n in range(NT)]
        UP = [m_view(f"UP{n}", [P, QB, QP, NC], 36 + 8 * n) for n in range(NT)]
        YP = shared(t1_at, 0, "YP", [P, 2, QP, NC])
        YG = shared(t1_at, 2 * TOK, "YG", [P, 2, T, NC])
        SD = [shared(at, 2 * TOK * i, f"SD{j}{i}", [P, 2, QP, NC]) for j, at in enumerate((pt_at, z_at)) for i in range(2)]
        VAL = m_view("VAL", [P, QB * TOK], 64)
        GATED = m_view("GATED", [P, FB, 2, TOK], 0)
        PROJ = m_view("PROJ", [P, D // P * TOK], 32)
        ON = m_view("ON", [P, 2, D], 64)
        XF = m_view("XF", [P, 2, QB, TOK], 80)

        PS = ctx.enter_context(nc.psum_tensor("PS", [P, 8, NW], F32))

        tabq = nc.dram_tensor("tabq", (KB, P, QP * 2 * P), F32).ap()
        tabd = nc.dram_tensor("tabd", (KB, P, QP * 2 * P), F32).ap()
        tabk = nc.dram_tensor("tabk", (KB * QP, 2 * CH, (T - 1) * 2 * CH + P), F32).ap()
        tabe = nc.dram_tensor("tabe", (2, P, PAIRS * NC), F32).ap()

        raw_in = [sem(f"raw_in{s}") for s in range(RING)]
        hi_ready = sem("hi_ready")
        lo_ready = sem("lo_ready")
        split_used = sem("split_used")
        acc_free = sem("acc_free")
        aux_done = sem("aux_done")
        aux_free = sem("aux_free")
        cross_copied = sem("cross_copied")
        z_ready = sem("z_ready")
        nl_ready = sem("nl_ready")
        mixed_ready = sem("mixed_ready")
        gated_ready = sem("gated_ready")
        operand_hi = sem("operand_hi")
        operand_ready = sem("operand_ready")
        squares_ready = sem("squares_ready")
        squares_summed = sem("squares_summed")
        square_total = sem("square_total")
        root_ready = sem("root_ready")
        rstd_ready = sem("rstd_ready")
        dve_chain = sem("dve_chain")
        pool_chain = sem("pool_chain")
        x_in = [sem(f"x_in{n}") for n in range(NT)]
        vec_in = sem("vec_in")
        s5_in = sem("s5_in")
        p_in = sem("p_in")
        ws_in = sem("ws_in")
        ws_masked = sem("ws_masked")
        ident_ready = sem("ident_ready")
        masks_ready = sem("masks_ready")
        ldt_spread = sem("ldt_spread")
        p_ready = sem("p_ready")
        ln_in = sem("ln_in")
        v_ready = sem("v_ready")
        ln_var = sem("ln_var")
        ln_root = sem("ln_root")
        angle_ready = sem("angle_ready")
        sine_ready = sem("sine_ready")
        params_ready = sem("params_ready")
        rot_out = sem("rot_out")
        build_clear = sem("build_clear")
        b_in = sem("b_in")
        b_used = sem("b_used")
        c_in = sem("c_in")
        cm_ready = sem("cm_ready")
        q_base = sem("q_base")
        qt_ready = sem("qt_ready")
        dt_ready = sem("dt_ready")
        d_out = sem("d_out")
        qk_out = sem("qk_out")
        tq_in = [sem("tq_in0"), sem("tq_in1")]
        te_in = [sem("te_in0"), sem("te_in1")]
        td_in = [sem("td_in0"), sem("td_in1")]
        core_ready = sem("core_ready")
        up_in = [sem(f"up_in{n}") for n in range(NT)]
        in_done = sem("in_done")
        inc_free = sem("inc_free")
        rt_ready = sem("rt_ready")
        rt_used = sem("rt_used")
        sd_ready = sem("sd_ready")
        out_of = sem("out_of")
        yp_ready = sem("yp_ready")
        yg_in = sem("yg_in")
        xf_ready = sem("xf_ready")
        out_ready = sem("out_ready")
        out_done = sem("out_done")

        block = ctx.enter_context(nc.Block())

        def tile_src(w, k0, col):
            return w.rearrange("(k p) n -> p k n", p=P)[:, k0:k0 + TK, bass.ds(col, NW)]

        def quad(s, lo):
            return PS[:, QB * s:QB * s + QB, lo:lo + TOK]

        def half_quad(s):
            return PS[:, 2 * s:2 * s + 2, :].rearrange("p b (h t) -> p (b h) t", h=2)

        def flat3(t):
            return t[:, :].rearrange("p (m t) -> p m t", t=TOK)

        def tile_at(stage, i, per, j):
            t0 = AT[stage]["t"]
            if isinstance(i, int):
                t = t0 + i * per + j
                return t, t // RING, t % RING
            assert per % RING == 0
            return i * per + (t0 + j), i * (per // RING) + (t0 + j) // RING, (t0 + j) % RING

        @block.sync
        def _(sp):
            def load(src, stage, i, per, j):
                t, _, slot = tile_at(stage, i, per, j)
                if not (isinstance(t, int) and t < RING):
                    sp.wait_ge(lo_ready, t - (RING - 1))
                sp.dma_start(RAW[:, slot, :].rearrange("p (k n) -> p k n", k=TK), src).then_inc(raw_in[slot], 16)

            def column(w, stage, i, per, col, depth, j0=0, done=0):
                for j in range(done, depth):
                    load(tile_src(w, TK * j, col), stage, i, per, j0 + j)

            for n in range(NT):
                sp.dma_start(XN[:, :, NW * n:NW * n + NW],
                             x[0].rearrange("(h p) d -> p h d", p=P)[:, :, NW * n:NW * n + NW]).then_inc(x_in[n], 16)
                load(tile_src(gm_w_in[0], TK * n, D), "v", 0, KT, n)
            for n in range(NT):
                column(gm_w_in[0], "v", n, KT, D + NW * n, KT, done=RING if n == 0 else 0)
            with nc.sync.Fori(0, NT) as n:
                column(gm_w_in[0], "us", n, KT, n * NW, KT)
            with nc.sync.Fori(0, NT) as n:
                column(gm_w_out[0], "out0", n, KT, n * NW, KT)

            a_build = AT["build"]["a"]

            def load_b(b):
                sp.wait_ge(b_used, b)
                for ri, bw in enumerate((s5_b_re, s5_b_im)):
                    for g in range(2):
                        src = bw[0].rearrange("(q g) s c -> g s q c", g=2)[g, :, bass.ds(b * QP, QP), :]
                        sp.dma_start(BD[ST * g:ST * g + ST, ri, :, g, :], src).then_inc(b_in, 16)

            def load_c(b):
                for ri, cw in enumerate((s5_c_re, s5_c_im)):
                    for g in range(2):
                        sp.dma_start(CM[:, ri, g, :],
                                     cw[0].rearrange("g c s -> (g c) s")[bass.ds(b * P, P), :]).then_inc(c_in, 16)

            def store_d(b):
                sp.wait_ge(dt_ready, b + 1)
                sp.dma_start(tabd[bass.ds(b, 1)].rearrange("b p (q n) -> p (b q) n", n=P),
                             DT[:, :, :, 1:T + 1, :].rearrange("p q r j c -> p (q r) (j c)")).then_inc(d_out, 16)

            def store_qk(b):
                sp.wait_ge(aux_free, b + (a_build + 1))
                sp.dma_start(tabq[bass.ds(b, 1)].rearrange("b p n -> p (b n)"),
                             QS[:, :, :, :].rearrange("p q r n -> p (q r n)")).then_inc(qk_out, 16)
                sp.dma_start(tabk[bass.ds(b * QP, QP)].rearrange("q c n -> (q c) n"), KS[:, :]).then_inc(qk_out, 16)

            def build_column(w, n, off, b, more=True):
                for j in range(KT):
                    load(tile_src(w, TK * j, n * NW), "up0", n, 2 * KT, off + j)
                    if j == MID:
                        store_d(b)
                    if j == MID + 2:
                        store_qk(b)
                        if more:
                            load_c(b + 2)
                    if j == MID + 3 and more:
                        load_b(b + 2)

            t = AT["up0"]["t"]
            load(tile_src(ffn_w1[0], 0, 0), "up0", 0, 2 * KT, 0)
            sp.wait_ge(build_clear, 1)
            load_c(0)
            for ri, bw in enumerate((s5_b_re, s5_b_im)):
                for g in range(2):
                    src = bw[0].rearrange("(q g) s c -> g s q c", g=2)[g, :, 0:QP, :]
                    sp.dma_start(BD[ST * g:ST * g + ST, ri, :, g, :], src).then_inc(b_in, 16)
            for j in range(1, KT):
                load(tile_src(ffn_w1[0], TK * j, 0), "up0", 0, 2 * KT, j)
                if j == MID + 2:
                    sp.wait_ge(aux_free, AT["first"]["a"] + 1)
                    load_c(1)
                if j == MID + 3:
                    load_b(1)
            with nc.sync.Fori(0, KB // 2 - 1) as n:
                build_column(ffn_w3[0], n, KT, n * 2)
                build_column(ffn_w1[0], n + 1, 0, n * 2 + 1)
            build_column(ffn_w3[0], KB // 2 - 1, KT, KB - 2, more=False)
            build_column(ffn_w1[0], KB // 2, 0, KB - 1, more=False)
            column(ffn_w3[0], "up0", KB // 2, 2 * KT, KB // 2 * NW, KT, j0=KT)

            def up(i, first):
                with nc.sync.Fori(first, NU) as n:
                    column(ffn_w1[i], f"up{i}", n, 2 * KT, n * NW, KT)
                    column(ffn_w3[i], f"up{i}", n, 2 * KT, n * NW, KT, j0=KT)

            def down_and_gate(i):
                with nc.sync.Fori(0, NT // 2) as e:
                    column(ffn_w2[i], f"down{i}", e, 2 * FT, e * (2 * NW), FT)
                    column(ffn_w2[i], f"down{i}", e, 2 * FT, e * (2 * NW) + NW, FT, j0=FT)
                for n in range(NT):
                    column(ple_w_proj[i], f"proj{i}", n, 1, NW * n, 1)
                with nc.sync.Fori(0, NT) as n:
                    column(ple_w_gate[i], f"gate{i}", n, KT, n * NW, KT)

            up(0, KB // 2 + 1)
            down_and_gate(0)

            def duo(table, d):
                return table[2 * d:2 * d + 2].rearrange("b p n -> p b n")

            def load_tq(d):
                par = d % 2
                if d >= 2:
                    sp.wait_ge(in_done, 2 * (d - 2) + 2)
                sp.dma_start(TQ[par][:, :, :, :, :].rearrange("p b q r n -> p b (q r n)"), duo(tabq, d)).then_inc(tq_in[par], 16)

            def load_te(d):
                par = d % 2
                if d >= 2:
                    sp.wait_ge(sd_ready, 2 * (d - 2) + 2)
                sp.dma_start(TE[par][:, :, :, :, :].rearrange("p r b q k -> p r (b q k)"),
                             tabe.rearrange("r p n -> p r n")[:, :, 2 * QP * NC * d:2 * QP * NC * (d + 1)]).then_inc(te_in[par], 16)

            def load_td(d):
                par = d % 2
                if d >= 2:
                    sp.wait_ge(out_of, d - 1)
                sp.dma_start(TD[par][:, :, :, :, :].rearrange("p b q r n -> p b (q r n)"), duo(tabd, d)).then_inc(td_in[par], 16)
                for i in range(T):
                    sp.dma_start(TKK[par][2 * CH * i:2 * CH * (i + 1), :, :, :].rearrange("c b q n -> c (b q) n"),
                                 tabk[2 * QP * d:2 * QP * (d + 1), :, 2 * CH * i:2 * CH * i + P].rearrange("x c n -> c x n")
                                 ).then_inc(td_in[par], 16)

            sp.wait_ge(rot_out, 32)
            sp.wait_ge(d_out, 16 * KB)
            sp.wait_ge(qk_out, 16 + 32 * KB)
            for g in range(CORE_TILES + KT):
                n, j = g // KT, g % KT
                if n < NT:
                    load(tile_src(s5_w_in[0], TK * j, NW * n), "win", 0, 0, g)
                else:
                    load(tile_src(s5_w_out[0], TK * j, D * (n - NT)), "win", 0, 0, g)
                if g == KT - 1:
                    sp.wait_ge(split_used, AT["win"]["t"])
                for d in range(DUOS):
                    if g == (KT - 1 + 2 * d if d < 2 else SCAN[2 * d - 3] + KT):
                        load_tq(d)
                    if g == (KT - 1 + 2 * d if d < 2 else SCAN[2 * d - 3] + KT + 2):
                        load_te(d)
                        load_td(d)
            with nc.sync.Fori(1, NT) as n:
                column(s5_w_out[0], "out1", n, 2 * KT, n * NW, KT)
                column(s5_w_out[0], "out1", n, 2 * KT, n * NW + D, KT, j0=KT)
            up(1, 0)
            down_and_gate(1)
            for n in range(NT):
                sp.wait_ge(out_ready, n + 1)
                sp.dma_start(out[0, :, NW * n:NW * n + NW].rearrange("(h p) d -> p h d", p=P),
                             ON[:, :, NW * n:NW * n + NW]).then_inc(out_done, 16)
            sp.wait_ge(out_done, 16 * NT)

        @block.gpsimd
        def _(pool):
            step = Chain(pool, pool_chain)
            G_ = nc.gpsimd
            step(G_.memset(IDENT[:, :], 0.0))
            G_.affine_select(out=IDENT[:, :], in_=IDENT[:, :], compare_op=ALU.not_equal, fill=1.0, base=0,
                             pattern=[[-1, P]], channel_multiplier=1).then_inc(ident_ready, 1)
            pool.dma_start(WN[:, :, :], gm_w_s[0].rearrange("h t s -> t h s")).then_inc(ws_in, 16)
            pool.dma_start(BS[0:1, :, :], gm_b_s[0:1, :, :]).then_inc(ln_in, 16)
            pool.dma_start(LG[:, 0, :], gm_ln_g[0].unsqueeze(0).to_broadcast([P, D])).then_inc(ln_in, 16)
            pool.dma_start(LG[:, 1, :], gm_ln_b[0].unsqueeze(0).to_broadcast([P, D])).then_inc(ln_in, 16)
            G_.memset(ONE[0:1, :], 1.0)
            G_.memset(ZERO[0:1, :].bitcast(F32), 0.0)
            G_.memset(EPSB[:, :], EPS)
            G_.memset(DG[:, :], 0.0)
            step(G_.memset(BAND[:, :], 1.0))
            step(G_.affine_select(out=BAND[:, :], in_=BAND[:, :], compare_op=ALU.is_ge, fill=0.0,
                                  base=0, pattern=[[-2 * CH, QP]], channel_multiplier=1))
            step(G_.affine_select(out=BAND[:, :], in_=BAND[:, :], compare_op=ALU.is_ge, fill=0.0,
                                  base=CH - 1, pattern=[[2 * CH, QP]], channel_multiplier=-1))
            step(G_.tensor_tensor(BAND[:, 0:2], BAND[:, 0:2], BAND[:, 2:4], ALU.add))
            step(G_.tensor_tensor(PAR[:, 0:1], BAND[:, 0:1], BAND[:, 1:2], ALU.add))
            G_.tensor_scalar(PAR[:, 1:2], PAR[:, 0:1], -1.0, 1.0, ALU.mult, ALU.add)
            pool.wait_ge(ident_ready, 1)
            two = IDENT[:, :].rearrange("p (a n) -> p a n", a=2)
            step(G_.tensor_tensor(DIAG[:, :, :], two[:, :, 0:2 * CH], two[:, :, 2 * CH:4 * CH], ALU.add))
            G_.tensor_tensor(DIAG[:, 0, :], DIAG[:, 0, :], DIAG[:, 1, :], ALU.add).then_inc(masks_ready, 1)
            pool.wait_ge(ws_in, 16)
            G_.affine_select(out=WN[:, :, :], in_=WN[:, :, :], compare_op=ALU.is_ge, fill=0.0, base=0,
                             pattern=[[0, HEADS], [-1, P]], channel_multiplier=1).then_inc(ws_masked, 1)

            def all_reduce(k):
                pool.wait_ge(squares_summed, AT[k]["r"])
                G_.partition_all_reduce(SUM[:, :], SS[:, :], P, RADD).then_inc(square_total, 1)

            all_reduce("set-up")

            pool.wait_ge(params_ready, 1)
            pool.wait_ge(mixed_ready, NT)
            pool.wait_ge(split_used, AT["out0"]["t"])
            pair_row = lambda i: RA[:, 0, 2 * i:2 * i + 2, :].rearrange("p a b -> p (a b)")
            power = [TURN[:, :, :]] + [ROTP[:, m, :, :] for m in range(1, 6)]
            for m in range(1, 6):
                re, im = power[m - 1][:, 0, :], power[m - 1][:, 1, :]
                G_.tensor_tensor(pair_row(0), re, re, ALU.mult)
                G_.tensor_tensor(pair_row(1), im, im, ALU.mult)
                step(G_.tensor_tensor(pair_row(2), re, im, ALU.mult))
                G_.tensor_tensor(power[m][:, 0, :], pair_row(0), pair_row(1), ALU.subtract)
                step(G_.tensor_tensor(power[m][:, 1, :], pair_row(2), pair_row(2), ALU.add))
            G_.memset(ROT[:, 0, :, 0:1], 1.0)
            step(G_.memset(ROT[:, 1, :, 0:1], 0.0))
            HP = PAIRS // 2
            for m in range(6):
                n = 1 << m
                for h in range(2):
                    pairs = slice(HP * h, HP * h + HP)
                    old = ROT[:, :, pairs, 0:n]
                    turn = lambda ri: power[m][:, ri, pairs].unsqueeze(1).unsqueeze(3).to_broadcast([P, 2, HP, n])
                    G_.tensor_tensor(RA[:, :, :, 0:n], old, turn(0), ALU.mult)
                    step(G_.tensor_tensor(RB[:, :, :, 0:n], old, turn(1), ALU.mult))
                    G_.tensor_tensor(ROT[:, 0, pairs, n:2 * n], RA[:, 0, :, 0:n], RB[:, 1, :, 0:n], ALU.subtract)
                    step(G_.tensor_tensor(ROT[:, 1, pairs, n:2 * n], RA[:, 1, :, 0:n], RB[:, 0, :, 0:n], ALU.add))
            for ri in range(2):
                pool.dma_start(tabe[ri], ROT[:, ri, :, :].rearrange("p q k -> p (q k)")).then_inc(rot_out, 16)

            G_.memset(KS[:, :], 0.0).then_inc(qk_out, 16)
            G_.memset(BD[:, :, :, :, :], 0.0).then_inc(build_clear, 1)

            def spread_c(b):
                pool.wait_ge(c_in, b * 64 + 64)
                G_.tensor_tensor(CM[:, :, :, :], CM[:, :, :, :],
                                 PAR[:, :].unsqueeze(1).unsqueeze(3).to_broadcast([P, 2, 2, ST]), ALU.mult).then_inc(cm_ready, 1)

            def c_powers(b, first=False):
                step(G_.tensor_copy(LAMB[:, :, :, :], LAM[:, :, 1:T + 1, bass.ds(b * QP, QP)]))
                pool.wait_ge(aux_free, b + AT["build"]["a"])
                if not first:
                    pool.wait_ge(d_out, b * 16)
                c = lambda ri: DT[:, :, ri, 0:1, :].to_broadcast([P, QP, 2, 2 * CH])
                for j in (1, 3):
                    lam = lambda ri: LAMB[:, ri, j - 1:j + 1, :].rearrange("p j q -> p q j").unsqueeze(3).to_broadcast(
                        [P, QP, 2, 2 * CH])
                    G_.tensor_tensor(DTA[:, :, :, :], c(0), lam(0), ALU.mult)
                    step(G_.tensor_tensor(DTB[:, :, :, :], c(1), lam(1), ALU.mult))
                    step(G_.tensor_tensor(DT[:, :, 0, j:j + 2, :], DTA[:, :, :, :], DTB[:, :, :, :], ALU.add))
                    G_.tensor_tensor(DTA[:, :, :, :], c(1), lam(0), ALU.mult)
                    step(G_.tensor_tensor(DTB[:, :, :, :], c(0), lam(1), ALU.mult))
                    last = G_.tensor_tensor(DT[:, :, 1, j:j + 2, :], DTA[:, :, :, :], DTB[:, :, :, :], ALU.subtract)
                    if j == 1:
                        step(last)
                last.then_inc(dt_ready, 1)
                pool.wait_ge(dt_ready, b + 1)

            spread_c(0)
            c_powers(0, first=True)
            spread_c(1)
            all_reduce("up0")
            with nc.gpsimd.Fori(1, KB - 1) as b:
                step.enter(b - 1, 8)
                c_powers(b)
                spread_c(b + 1)
            step.leave(KB - 2)
            c_powers(KB - 1)
            all_reduce("proj0")
            all_reduce("win")

            def decay(b, par):
                G_.tensor_copy(RT[par][:, :, 1:NC],
                               RHO[:, bass.ds(b * QP, QP)].unsqueeze(2).to_broadcast([P, QP, NC - 1])).then_inc(rt_ready, 1)

            pool.wait_ge(split_used, AT["win"]["t"])
            for par in range(2):
                G_.memset(RT[par][:, :, 0:1], 0.0)
            for i in range(4):
                last = G_.memset(SD[i][:, :, :, 0:1], 0.0)
            last.then_inc(core_ready, 1)
            for par in range(2):
                decay(par, par)
            with nc.gpsimd.Fori(1, KB // 2) as e:
                for par in range(2):
                    pool.wait_ge(rt_used, e * 2 + (par - 1))
                    decay(e * 2 + par, par)

            all_reduce("up1")
            all_reduce("proj1")
            all_reduce("fin")

        @block.scalar
        def _(act):
            A_ = nc.scalar

            def section(stage, i, per, j):
                t, rnd, slot = tile_at(stage, i, per, j + RING)
                if isinstance(t, int) and t >= AT["end"]["t"]:
                    return
                act.wait_ge(raw_in[slot], rnd * 16 + 16)
                act.wait_ge(split_used, t - (RING - 1))
                A_.activation(WHI[:, slot, :], RAW[:, slot, :], ACT.Copy).then_inc(hi_ready, 1)

            def sections(stage, i, per, j0, count):
                for j in range(j0, j0 + count):
                    section(stage, i, per, j)

            def cross(c, s, r, t_end):
                act.wait_ge(split_used, t_end)
                act.wait_ge(acc_free, c)
                act.wait_ge(squares_summed, r)
                A_.activation(flat3(T1), quad(s, TOK), ACT.Copy).then_inc(cross_copied, 1)

            def high_parts(n, vec, dst, signal, value):
                act.wait_ge(signal, value)
                for m in range(QB):
                    k = n * QB + m
                    last = A_.activation(dst[:, bass.ds(k, 1), 0:TOK].rearrange("p k t -> p (k t)"),
                                         X[:, bass.ds(k * TOK, TOK)], ACT.Identity, scale=VEC[:, vec, bass.ds(k, 1)])
                last.then_inc(operand_hi, 2)

            def squares(n, r, signal, value):
                act.wait_ge(signal, value)
                if not (isinstance(r, int) and r == 0):
                    act.wait_ge(squares_summed, r)
                A_.activation(T1[:, :], X[:, bass.ds(n * (QB * TOK), QB * TOK)], ACT.Square).then_inc(squares_ready, 1)

            def root(k):
                act.wait_ge(square_total, k)
                A_.activation(SUM[:, :], SUM[:, :], ACT.Sqrt, scale=1.0 / D, bias=EPSB[:, 0:1]).then_inc(root_ready, 1)

            vectors = [norm_mix[0], norm_mix[1], norm_ffn[0], norm_ffn[1], norm_ple[0], norm_ple[1], norm_final, s5_d[0]]
            for i, v in enumerate(vectors):
                act.dma_start(NAT[KB * i:KB * i + KB, :], v.rearrange("(k p) -> k p", p=P)).then_inc(vec_in, 16)
            act.dma_start(AN[:, 0, :], s5_a_re[0].rearrange("(q g) s -> q (g s)", g=2)).then_inc(s5_in, 16)
            act.dma_start(AN[:, 1, :], s5_a_im[0].rearrange("(q g) s -> q (g s)", g=2)).then_inc(s5_in, 16)
            act.dma_start(LDN[:, :], s5_log_dt[0].rearrange("(q g) -> q g", g=2)).then_inc(s5_in, 16)
            for l in range(2):
                act.dma_start(PN[:, l, :, :], p[l, 0].rearrange("(h p) d -> p h d", p=P)).then_inc(p_in, 16)
            act.wait_ge(aux_done, 1)
            A_.activation(VEC[:, :, :].rearrange("p v k -> p (v k)"), PS[:, 4, 0:P], ACT.Copy).then_inc(aux_free, 1)
            for n in range(NT):
                act.wait_ge(raw_in[n], 16)
                A_.activation(WHI[:, n, :], RAW[:, n, :], ACT.Copy).then_inc(hi_ready, 1)
                high_parts(n, 0, M, aux_free, n + 2)
                squares(n, n, aux_free, n + 2)

            setup = AT["set-up"]["a"]
            for n in range(NT):
                sections("v", n, KT, RING if n else 0, KT - RING if n else 2)
                if n == 0:
                    root(1)
                    sections("v", n, KT, 2, 1)
                    act.wait_ge(aux_done, setup + 1)
                    for h in range(2):
                        A_.activation(PT[:, 2 * h:2 * h + 2, 0:TOK], PS[:, 5 + h, :].rearrange("p (k t) -> p k t", t=TOK),
                                     ACT.Copy)
                    A_.activation(SA[:, :, :], PS[:, 4, 0:3 * PAIRS].rearrange("p (v k) -> p v k", v=3), ACT.Copy).then_inc(p_ready, 1)
                    sections("v", n, KT, 3, 3)
                    act.wait_ge(aux_done, setup + 2)
                    A_.activation(WT[:, :, :].rearrange("p h t -> p (h t)"),
                                  PS[:, 4:8, :].rearrange("p b n -> p (b n)"), ACT.Copy).then_inc(aux_free, 1)
                    sections("v", n, KT, 6, 1)
                    act.wait_ge(aux_done, setup + 3)
                    A_.activation(RCOL[:, :], PS[:, 4, 0:2], ACT.Copy).then_inc(aux_free, 1)
                    act.wait_ge(aux_free, setup + 3)
                    sections("v", n, KT, 7, 1)
                if n == 1:
                    act.wait_ge(angle_ready, 1)
                    A_.activation(PW[:, 8:10, :], PW[:, 8:10, :], ACT.Sin).then_inc(sine_ready, 1)
                act.wait_ge(split_used, AT["v"]["t"] + KT * (n + 1))
                for th in range(2):
                    last = A_.activation(V[:, th, NW * n:NW * n + NW], PS[:, QB * (n % 2) + th, :],
                                         ACT.Gelu_apprx_tanh, scale=RCOL[:, th:th + 1])
                last.then_inc(acc_free, 1)
                sections("v", n, KT, KT, 2)
                if n == NT - 1:
                    act.wait_ge(ln_var, 1)
                    A_.activation(LNR[:, :, :], MV[:, :, 1:2], ACT.Sqrt, bias=EPSB[:, 0:1]).then_inc(ln_root, 1)
                sections("v", n, KT, KT + 2, 2)

            a = AT["us"]
            for n in range(NT):
                sections("us", n, KT, RING, 3)
                act.wait_ge(aux_done, a["a"] + n + 1)
                A_.activation(SV[:, :, :], quad(1 - n % 2, 0), ACT.Copy).then_inc(aux_free, 1)
                sections("us", n, KT, RING + 3, 1)
                cross(a["c"] + n, n % 2, a["r"], a["t"] + KT * (n + 1))
                sections("us", n, KT, KT, 1)
                act.wait_ge(z_ready, a["z"] + n + 1)
                A_.activation(T1[:, :], Z[:, :], ACT.Gelu_apprx_tanh).then_inc(nl_ready, 1)
                sections("us", n, KT, KT + 1, 1)
                act.wait_ge(mixed_ready, n + 1)
                A_.activation(M[:, KB + QB * n:KB + QB * n + QB, 0:TOK], flat3(Z), ACT.Copy).then_inc(operand_hi, 2)
                sections("us", n, KT, KT + 2, 2)

            def residual_end(stage, i, per, j, n, vec):
                a = AT[stage]
                section(stage, i, per, j)
                high_parts(n, vec, H, acc_free, n + (a["c"] + 1))
                section(stage, i, per, j + 1)
                squares(n, n + a["r"], acc_free, n + (a["c"] + 1))
                sections(stage, i, per, j + 2, 2)

            def gated_end(stage, i, per, j, n, vec, dst, signal, value):
                a = AT[stage]
                section(stage, i, per, j)
                act.wait_ge(signal, value)
                A_.activation(T1[:, :], Z[:, :], ACT.Sigmoid).then_inc(nl_ready, 1)
                section(stage, i, per, j + 1)
                if dst is not None:
                    high_parts(n, vec, dst, gated_ready, n + (a["g"] + 1))
                squares(n, n + a["r"], gated_ready, n + (a["g"] + 1))
                sections(stage, i, per, j + 2, 2)

            a_build = AT["build"]["a"]

            def tables_out(b, q, s, c=True):
                if c:
                    act.wait_ge(aux_done, b + (a_build + 1))
                    for ri in range(2):
                        last = A_.activation(DT[:, :, ri, 0, :],
                                             PS[:, QB * s, P * ri:P * ri + P].rearrange("p (q c) -> p q c", q=QP),
                                             ACT.Copy, scale=(-1.0 if ri else 1.0))
                    if not q:
                        last.then_inc(aux_free, 1)
                if q:
                    act.wait_ge(aux_done, b + (a_build + 1))
                    act.wait_ge(qk_out, b * 32 + 16)
                    A_.activation(QS[:, :, :, :].rearrange("p q r n -> p (q r n)"),
                                  PS[:, QB * s + 1:QB * s + 3, :].rearrange("p b n -> p (b n)"), ACT.Copy)
                    A_.activation(KS[:, (T - 1) * 2 * CH:], PS[:, QB * s + 3, 0:P], ACT.Copy).then_inc(aux_free, 1)

            for n in range(NT):
                sections("out0", n, KT, RING, 1)
                if n == NT - 1:
                    tables_out(-1, False, 0)
                sections("out0", n, KT, RING + 1, 3)
                residual_end("out0", n, KT, KT, n, 2)
            root(2)

            def up_step(i, n, b=None, more=True):
                a, stage = AT[f"up{i}"], f"up{i}"
                sections(stage, n, 2 * KT, RING, 1)
                if b is not None:
                    tables_out(b, True, 1)
                sections(stage, n, 2 * KT, RING + 1, 3)
                cross(n * 2 + a["c"], 0, a["r"], n * (2 * KT) + (a["t"] + KT))
                section(stage, n, 2 * KT, KT)
                act.wait_ge(z_ready, n * 2 + (a["z"] + 1))
                A_.activation(GATED[:, bass.ds(n * QB, QB), 1, :], flat3(Z), ACT.Silu).then_inc(nl_ready, 1)
                sections(stage, n, 2 * KT, KT + 1, RING)
                if b is not None:
                    tables_out(b + 1, True, 0, c=more)
                sections(stage, n, 2 * KT, KT + RING + 1, 3)
                cross(n * 2 + (a["c"] + 1), 1, a["r"], n * (2 * KT) + (a["t"] + 2 * KT))
                sections(stage, n, 2 * KT, 2 * KT, 2)
                act.wait_ge(z_ready, n * 2 + (a["z"] + 2))
                A_.activation(M[:, bass.ds(n * QB, QB), 0:TOK], flat3(Z), ACT.Copy).then_inc(operand_hi, 2)
                sections(stage, n, 2 * KT, 2 * KT + 2, 2)

            def up_loop(i, first):
                with nc.scalar.Fori(first, NU) as n:
                    up_step(i, n)

            def down(i):
                a = AT[f"proj{i}"]

                def proj(n):
                    act.wait_ge(split_used, a["t"] + n + 1)
                    A_.activation(PROJ[:, QB * TOK * n:QB * TOK * (n + 1)].rearrange("p (m t) -> p m t", t=TOK),
                                  half_quad(n), ACT.Copy).then_inc(acc_free, 1)

                d, stage = AT[f"down{i}"], f"down{i}"
                for n in range(NT):
                    sections(stage, n, FT, RING, FT - RING)
                    if n < NT - 1:
                        residual_end(stage, n, FT, FT, n, 4 + i)
                section(stage, n, FT, FT)
                high_parts(n, 4 + i, H, acc_free, d["c"] + n + 1)
                proj(0)
                section(stage, n, FT, FT + 1)
                proj(1)
                squares(n, n + d["r"], acc_free, d["c"] + n + 1)
                section(stage, n, FT, FT + 2)
                proj(2)
                section(stage, n, FT, FT + 3)
                proj(3)
                sections(stage, n, FT, FT + NT, 1)
                root(3 * i + 3)
                sections(stage, n, FT, FT + NT + 1, RING - 1)

            act.wait_ge(rot_out, 32)
            with nc.scalar.Fori(0, KB // 2 - 1) as n:
                up_step(0, n, b=n * 2)
            up_step(0, KB // 2 - 1, b=KB - 2, more=False)
            act.wait_ge(d_out, 16 * KB)
            act.wait_ge(qk_out, 32 * KB + 16)
            up_loop(0, KB // 2)
            down(0)
            a = AT["gate0"]
            with nc.scalar.Fori(0, NT // 2) as e:
                for s in range(2):
                    n = e * 2 + s
                    sections("gate0", e, 2 * KT, KT * s + RING, KT - RING)
                    cross(n + a["c"], s, n + a["r"], n * KT + (a["t"] + KT))
                    gated_end("gate0", e, 2 * KT, KT * (s + 1), n, 1, M, z_ready, n + (a["z"] + 1))
            root(4)

            def send_u(n):
                act.wait_ge(acc_free, AT["win"]["c"] + n + 1)
                for q in range(QP):
                    for j in range(T):
                        i = T - 1 - j
                        act.dma_start(UP[n][2 * CH * i:2 * CH * (i + 1), :, q, :],
                                      UC[n][2 * CH * q:2 * CH * (q + 1), :, j, :]).then_inc(up_in[n], 16)

            def core_gelu(d):
                act.wait_ge(out_of, d + 1)
                if d:
                    act.wait_ge(yg_in, 256 * d)
                A_.activation(YP[:, :, :, :].rearrange("p b q k -> p (b q k)"), PS[:, 6 + d % 2, :],
                              ACT.Gelu_apprx_tanh).then_inc(yp_ready, 1)
                act.wait_ge(yp_ready, d + 1)
                if d:
                    act.wait_ge(operand_ready, a_core["q"] + d)
                for q in range(QP):
                    for j in range(T):
                        act.dma_start(YG[2 * CH * q:2 * CH * (q + 1), :, j, :],
                                      YP[2 * CH * j:2 * CH * (j + 1), :, q, :]).then_inc(yg_in, 16)

            def core_hi(d):
                act.wait_ge(yg_in, 256 * (d + 1))
                A_.activation(M[:, KB + 2 * d:KB + 2 * d + 2, 0:TOK].rearrange("p b (k j) -> p b k j", j=T),
                              YG[:, :, :, :].rearrange("p b j k -> p b k j"), ACT.Copy).then_inc(operand_hi, 1)

            a_core = AT["core"]
            for g in range(RING, CORE_TILES):
                section("win", 0, 0, g)
                if g % KT == 0:
                    send_u(g // KT - 1)
                for d in range(DUOS):
                    if g == OUT[d]:
                        core_gelu(d)
                    if g == HI[d]:
                        core_hi(d)

            a = AT["out1"]

            def out1_step(n, value=True):
                if value:
                    sections("out1", n, 2 * KT, RING, KT - RING)
                    cross(n * 2 + a["c"], 0, n + a["r"], n * (2 * KT) + (a["t"] + KT))
                sections("out1", n, 2 * KT, KT, KT)
                cross(n * 2 + (a["c"] + 1), 1, n + a["r"], n * (2 * KT) + (a["t"] + 2 * KT))
                gated_end("out1", n, 2 * KT, 2 * KT, n, 3, H, acc_free, n * 2 + (a["c"] + 2))

            out1_step(0, value=False)
            with nc.scalar.Fori(1, NT) as n:
                out1_step(n)
            root(5)
            up_loop(1, 0)
            down(1)
            a = AT["gate1"]
            for n in range(NT):
                sections("gate1", n, KT, RING, KT - RING)
                cross(n + a["c"], n % 2, n + a["r"], a["t"] + KT * (n + 1))
                gated_end("gate1", n, KT, KT, n, None, None, z_ready, n + (a["z"] + 1))
            root(7)
            a0 = AT["fin"]["a"]
            act.wait_ge(aux_done, a0 + 1)
            A_.activation(RCOL[:, :], PS[:, 0, 0:2], ACT.Copy).then_inc(aux_free, 1)
            act.wait_ge(aux_free, a0 + 1)
            for n in range(NT):
                act.wait_ge(aux_done, a0 + n + 2)
                for th in range(2):
                    last = A_.activation(ON[:, th, NW * n:NW * n + NW], PS[:, QB * ((n + 1) % 2) + th, :],
                                         ACT.Identity, scale=RCOL[:, th:th + 1])
                last.then_inc(out_ready, 1)

        @block.vector
        def _(dve):
            step = Chain(dve, dve_chain)
            V_ = nc.vector

            def section(stage, i, per, j):
                t, _, slot = tile_at(stage, i, per, j + RING)
                if isinstance(t, int) and t >= AT["end"]["t"]:
                    return
                dve.wait_ge(hi_ready, t + 1)
                V_.tensor_tensor(WLO[:, slot, :], RAW[:, slot, :], WHI[:, slot, :].bitcast(F32), ALU.subtract).then_inc(lo_ready, 1)

            def sections(stage, i, per, j0, count):
                for j in range(j0, j0 + count):
                    section(stage, i, per, j)

            def total(c, s, count, dst):
                dve.wait_ge(cross_copied, count + 1)
                V_.tensor_tensor(dst, quad(s, 0), flat3(T1), ALU.add).then_inc(acc_free, 1)
                dve.wait_ge(acc_free, c + 1)

            def scaled(dst, signal):
                V_.tensor_tensor(dst, flat3(Z), RSTD[:, :].unsqueeze(1).to_broadcast([P, QB, TOK]), ALU.mult).then_inc(signal, 1)

            def low_parts(n, vec, dst, q):
                dve.wait_ge(operand_hi, q + 2)
                for m in range(QB):
                    k = n * QB + m
                    last = V_.scalar_tensor_tensor(dst[:, bass.ds(k, 1), TOK:2 * TOK].rearrange("p k t -> p (k t)"),
                                                   X[:, bass.ds(k * TOK, TOK)], VEC[:, vec, bass.ds(k, 1)],
                                                   dst[:, bass.ds(k, 1), 0:TOK].rearrange("p k t -> p (k t)").bitcast(F32),
                                                   ALU.mult, ALU.subtract)
                last.then_inc(operand_ready, 2)

            def sum_squares(r):
                dve.wait_ge(squares_ready, r + 1)
                step(V_.tensor_reduce(Z[:, 0:TOK], T1[:, :].rearrange("p (m t) -> p t m", t=TOK), AX.X, ALU.add))
                if not (isinstance(r, int) and r == 0):
                    dve.wait_ge(squares_summed, r)
                V_.tensor_tensor(SS[:, :], SS[:, :], Z[:, 0:TOK], ALU.add).then_inc(squares_summed, 1)

            def rstd(k):
                dve.wait_ge(root_ready, k)
                V_.reciprocal(RSTD[:, :], SUM[:, :]).then_inc(rstd_ready, 1)
                dve.wait_ge(rstd_ready, k)
                step(V_.memset(SS[:, :], 0.0))

            dve.wait_ge(s5_in, 48)
            V_.tensor_copy(AN[:, 2, :].rearrange("q (g s) -> q g s", g=2),
                           LDN[:, :].unsqueeze(2).to_broadcast([PAIRS, 2, ST])).then_inc(ldt_spread, 1)
            step(V_.memset(SS[:, :], 0.0))
            for n in range(NT):
                dve.wait_ge(hi_ready, n + 1)
                V_.tensor_tensor(WLO[:, n, :], RAW[:, n, :], WHI[:, n, :].bitcast(F32), ALU.subtract).then_inc(lo_ready, 1)
                dve.wait_ge(aux_done, n + 2)
                dve.wait_ge(aux_free, n + 1)
                V_.tensor_copy(X[:, QB * TOK * n:QB * TOK * (n + 1)].rearrange("p (m t) -> p m t", t=TOK),
                               quad(n % 2, 0)).then_inc(aux_free, 1)
                dve.wait_ge(aux_free, n + 2)
                low_parts(n, 0, M, 2 * n)
                sum_squares(n)
            sections("v", 0, 0, 0, 2)
            rstd(1)
            sections("v", 0, 0, 2, 2)
            dve.wait_ge(p_ready, 1)
            for h in range(2):
                last = V_.tensor_tensor(PT[:, 2 * h:2 * h + 2, TOK:2 * TOK], PS[:, 5 + h, :].rearrange("p (k t) -> p k t", t=TOK),
                                        PT[:, 2 * h:2 * h + 2, 0:TOK].bitcast(F32), ALU.subtract)
            last.then_inc(aux_free, 1)
            sections("v", 0, 0, RING, KT - RING)

            def stats(n):
                dve.wait_ge(acc_free, AT["v"]["c"] + n + 1)
                for th in range(2):
                    last = V_.bn_stats(STAT[:, th, 6 * n:6 * n + 6], V[:, th, NW * n:NW * n + NW])
                step(last)

            def norm_quad(n):
                f = slice(NW * n, NW * n + NW)
                for th in range(2):
                    last = V_.tensor_scalar(V[:, th, f], V[:, th, f], MV[:, th, 0:1], LNR[:, th, :], ALU.subtract, ALU.mult)
                step(last)
                step(V_.tensor_tensor(V[:, :, f], V[:, :, f], LG[:, 0, f].unsqueeze(1).to_broadcast([P, 2, NW]), ALU.mult))
                V_.tensor_tensor(V[:, :, f], V[:, :, f], LG[:, 1, f].unsqueeze(1).to_broadcast([P, 2, NW]),
                                 ALU.add).then_inc(v_ready, 1)

            W = lambda i: PW[:, i, :]
            LOG2E, MAGIC = 1.4426950408889634, 12582912.0

            def tt(o, a, b, op):
                step(V_.tensor_tensor(o, a, b, op))

            def ts(o, a, s1, s2, op0, op1):
                step(V_.tensor_scalar(o, a, s1, s2, op0, op1))

            def stt(o, a, s, b, op0, op1):
                step(V_.scalar_tensor_tensor(o, a, s, b, op0, op1))

            pauses = [KT]

            def pause():
                j = pauses[0]
                section("v", 0, 0, j)
                if j % KT == 0:
                    stats(j // KT - 1)
                pauses[0] += 1

            def exponential(dst, src, minus_one):
                c, k, r, q = W(10), W(11), W(12), W(13)
                ts(c, src, -88.5, 89.0, ALU.max, ALU.min)
                ts(k, c, LOG2E, MAGIC, ALU.mult, ALU.add)
                ts(k, k, MAGIC, -127.0, ALU.subtract, ALU.max)
                stt(r, k, -0.693359375, c, ALU.mult, ALU.add)
                stt(r, k, 2.12194440e-4, r, ALU.mult, ALU.add)
                pause()
                ts(q, r, 1.0 / math.factorial(8), 0.0, ALU.mult, ALU.add)
                for n in range(7, 0, -1):
                    stt(q, q, 1.0 / math.factorial(n), r, ALU.add, ALU.mult)
                pause()
                ts(PI[:, :], k, 127.0, 8388608.0, ALU.add, ALU.mult)
                two_k = PI[:, :].bitcast(F32)
                tt(q, q, two_k, ALU.mult)
                if minus_one:
                    ts(c, two_k, -1.0, 0.0, ALU.add, ALU.add)
                    tt(dst, q, c, ALU.add)
                else:
                    tt(dst, q, two_k, ALU.add)

            a_re, a_im, dt = SA[:, 0, :], SA[:, 1, :], SA[:, 2, :]
            exponential(dt, dt, False)
            tt(W(0), a_re, dt, ALU.mult)
            pause()
            tt(W(2), a_im, dt, ALU.mult)
            ts(W(3), W(2), 0.5 / math.pi, MAGIC, ALU.mult, ALU.add)
            ts(W(3), W(3), MAGIC, 0.0, ALU.subtract, ALU.add)
            stt(W(2), W(3), -6.28125, W(2), ALU.mult, ALU.add)
            stt(W(2), W(3), -0.00193500518798828125, W(2), ALU.mult, ALU.add)
            stt(W(2), W(3), -3.0199159819567521e-7, W(2), ALU.mult, ALU.add)
            ts(W(8), W(2), 0.5, 0.0, ALU.mult, ALU.add)
            stt(W(9), W(8), -1.0, W(8), ALU.mult, ALU.max)
            V_.tensor_scalar(W(9), W(9), -1.0, math.pi / 2, ALU.mult, ALU.add).then_inc(angle_ready, 1)
            exponential(W(1), W(0), True)
            pause()
            pause()
            dve.wait_ge(sine_ready, 1)
            sn, cm1, im, re, r1 = W(2), W(3), W(4), W(5), W(6)
            tt(sn, W(8), W(9), ALU.mult)
            ts(sn, sn, 2.0, 0.0, ALU.mult, ALU.add)
            tt(cm1, W(8), W(8), ALU.mult)
            ts(cm1, cm1, -2.0, 0.0, ALU.mult, ALU.add)
            ts(r1, W(1), 1.0, 0.0, ALU.add, ALU.add)
            tt(im, r1, sn, ALU.mult)
            ts(re, cm1, 1.0, 0.0, ALU.add, ALU.add)
            ts(W(14), re, 1.0, 0.0, ALU.mult, ALU.add)
            ts(W(15), sn, 1.0, 0.0, ALU.mult, ALU.add)
            pause()
            tt(re, re, W(1), ALU.mult)
            tt(re, re, cm1, ALU.add)
            ts(LAM[:, 0, 1, :], re, 1.0, 0.0, ALU.add, ALU.add)
            ts(LAM[:, 1, 1, :], im, 1.0, 0.0, ALU.mult, ALU.add)
            pause()
            tt(W(7), a_re, a_re, ALU.mult)
            tt(W(8), a_im, a_im, ALU.mult)
            tt(W(7), W(7), W(8), ALU.add)
            step(V_.reciprocal(W(7), W(7)))
            tt(W(8), re, a_re, ALU.mult)
            tt(W(9), im, a_im, ALU.mult)
            tt(W(8), W(8), W(9), ALU.add)
            tt(FAC[:, 0, :], W(8), W(7), ALU.mult)
            pause()
            tt(W(8), im, a_re, ALU.mult)
            tt(W(9), re, a_im, ALU.mult)
            tt(W(8), W(8), W(9), ALU.subtract)
            tt(FAC[:, 1, :], W(8), W(7), ALU.mult)
            tt(W(7), r1, r1, ALU.mult)
            tt(RHO[:, :], W(7), W(7), ALU.mult)

            def product(out_re, out_im, x_re, x_im, y_re, y_im, sc):
                V_.tensor_tensor(sc[0], x_re, y_re, ALU.mult)
                V_.tensor_tensor(sc[1], x_im, y_im, ALU.mult)
                V_.tensor_tensor(sc[2], x_re, y_im, ALU.mult)
                tt(sc[3], x_im, y_re, ALU.mult)
                V_.tensor_tensor(out_re, sc[0], sc[1], ALU.subtract)
                tt(out_im, sc[2], sc[3], ALU.add)

            sc = [W(10), W(11), W(12), W(13)]
            for j in range(2, T + 1):
                pause()
                product(LAM[:, 0, j, :], LAM[:, 1, j, :], LAM[:, 0, j - 1, :], LAM[:, 1, j - 1, :],
                        LAM[:, 0, 1, :], LAM[:, 1, 1, :], sc)
            pause()
            product(W(16), W(17), W(14), W(15), W(14), W(15), sc)
            product(TURN[:, 0, :], TURN[:, 1, :], W(16), W(17), W(16), W(17), sc)
            V_.memset(W(16), 0.0).then_inc(params_ready, 1)
            while pauses[0] < KT * NT:
                pause()

            section("us", 0, 0, 0)
            stats(NT - 1)
            section("us", 0, 0, 1)
            V_.bn_aggr(MV[:, 0, :], STAT[:, 0, :])
            V_.bn_aggr(MV[:, 1, :], STAT[:, 1, :]).then_inc(ln_var, 1)
            section("us", 0, 0, 2)
            dve.wait_ge(ln_in, 48)
            dve.wait_ge(ln_root, 1)
            step(V_.reciprocal(LNR[:, :, :], LNR[:, :, :]))
            norm_quad(0)
            section("us", 0, 0, 3)

            a = AT["us"]
            for n in range(NT):
                sections("us", n, KT, RING, 2)
                if n < NT - 1:
                    norm_quad(n + 1)
                sections("us", n, KT, RING + 2, 2)
                total(a["c"] + n, n % 2, a["cross"] + n, flat3(Z))
                scaled(flat3(Z), z_ready)
                section("us", n, KT, KT)
                dve.wait_ge(nl_ready, a["nl"] + n + 1)
                dve.wait_ge(aux_free, a["a"] + n + 1)
                V_.tensor_tensor(flat3(Z), SV[:, :, :], flat3(T1), ALU.mult).then_inc(mixed_ready, 1)
                section("us", n, KT, KT + 1)
                dve.wait_ge(mixed_ready, n + 1)
                dve.wait_ge(operand_hi, a["q"] + 2 * n + 2)
                blocks = slice(KB + QB * n, KB + QB * n + QB)
                V_.tensor_tensor(M[:, blocks, TOK:2 * TOK], flat3(Z), M[:, blocks, 0:TOK].bitcast(F32),
                                 ALU.subtract).then_inc(operand_ready, 2)
                sections("us", n, KT, KT + 2, 2)

            a_build = AT["build"]["a"]

            def b_scaled(b, first=False):
                dve.wait_ge(b_in, b * 64 + 64)
                if not first:
                    dve.wait_ge(aux_done, b + a_build)
                pairs = bass.ds(b * QP, QP)
                bb = lambda ri: BD[:, ri, :, :, :].rearrange("p q g c -> p q (g c)")
                fac = lambda ri: FAC[:, ri, pairs].unsqueeze(2).to_broadcast([P, QP, 2 * CH])
                V_.tensor_tensor(QTA[:, :, 0, :], bb(0), fac(0), ALU.mult)
                V_.tensor_tensor(QTB[:, :, 0, :], bb(1), fac(1), ALU.mult)
                V_.tensor_tensor(QTA[:, :, 1, :], bb(0), fac(1), ALU.mult)
                V_.tensor_tensor(QTB[:, :, 1, :], bb(1), fac(0), ALU.mult).then_inc(b_used, 1)
                V_.tensor_scalar(DG[:, 0:2 * CH], DIAG[:, 0, :], VEC[:, 7, bass.ds(b, 1)], None, ALU.mult)
                dve.wait_ge(b_used, b + 1)
                V_.tensor_tensor(QT[:, :, 0, 0, :], QTA[:, :, 0, :], QTB[:, :, 0, :], ALU.subtract)
                V_.tensor_tensor(QT[:, :, 1, 0, :], QTA[:, :, 1, :], QTB[:, :, 1, :], ALU.add).then_inc(q_base, 1)

            def b_powers(b):
                dve.wait_ge(q_base, b + 1)
                pairs = bass.ds(b * QP, QP)
                shape = [P, QP, T - 1, 2 * CH]
                base_ = lambda ri: QT[:, :, ri, 0:1, :].to_broadcast(shape)
                lam = lambda ri: LAM[:, ri, 1:T, pairs].rearrange("p j q -> p q j").unsqueeze(3).to_broadcast(shape)
                V_.tensor_tensor(QTA[:, :, :, :], base_(0), lam(0), ALU.mult)
                step(V_.tensor_tensor(QTB[:, :, :, :], base_(1), lam(1), ALU.mult))
                step(V_.tensor_tensor(QT[:, :, 0, 1:T, :], QTA[:, :, :, :], QTB[:, :, :, :], ALU.subtract))
                V_.tensor_tensor(QTA[:, :, :, :], base_(0), lam(1), ALU.mult)
                step(V_.tensor_tensor(QTB[:, :, :, :], base_(1), lam(0), ALU.mult))
                V_.tensor_tensor(QT[:, :, 1, 1:T, :], QTA[:, :, :, :], QTB[:, :, :, :], ALU.add).then_inc(qt_ready, 1)
                dve.wait_ge(qt_ready, b + 1)

            def residual_end(stage, i, per, j, n, vec, t_end):
                a = AT[stage]
                xq = X[:, bass.ds(n * (QB * TOK), QB * TOK)].rearrange("p (m t) -> p m t", t=TOK)
                dve.wait_ge(split_used, t_end)
                step(V_.tensor_tensor(xq, xq, quad(n % 2, TOK), ALU.add))
                V_.tensor_tensor(xq, xq, quad(n % 2, 0), ALU.add).then_inc(acc_free, 1)
                section(stage, i, per, j)
                dve.wait_ge(acc_free, n + (a["c"] + 1))
                low_parts(n, vec, H, n * 2 + a["q"])
                section(stage, i, per, j + 1)
                sum_squares(n + a["r"])
                sections(stage, i, per, j + 2, 2)

            def gated_end(stage, i, per, j, n, vec, dst, other):
                a = AT[stage]
                section(stage, i, per, j)
                dve.wait_ge(nl_ready, n + (a["nl"] + 1))
                step(V_.tensor_tensor(Z[:, :], T1[:, :], other, ALU.mult))
                xq = X[:, bass.ds(n * (QB * TOK), QB * TOK)]
                V_.tensor_tensor(xq, xq, Z[:, :], ALU.add).then_inc(gated_ready, 1)
                section(stage, i, per, j + 1)
                dve.wait_ge(gated_ready, n + (a["g"] + 1))
                if dst is not None:
                    low_parts(n, vec, dst, n * 2 + a["q"])
                sum_squares(n + a["r"])
                sections(stage, i, per, j + 2, 2)

            for n in range(NT):
                sections("out0", n, KT, RING, 2)
                if n == NT - 1:
                    b_scaled(0, first=True)
                sections("out0", n, KT, RING + 2, 1)
                if n == NT - 1:
                    b_powers(0)
                sections("out0", n, KT, RING + 3, 1)
                residual_end("out0", n, KT, KT, n, 2, AT["out0"]["t"] + KT * (n + 1))
            rstd(2)

            def up_step(i, n, b=None, more=True):
                a, stage = AT[f"up{i}"], f"up{i}"
                blocks = bass.ds(n * QB, QB)

                def second_half(j0, b):
                    sections(stage, n, 2 * KT, j0 + RING, 2)
                    if b is not None:
                        b_scaled(b)
                    sections(stage, n, 2 * KT, j0 + RING + 2, 1)
                    if b is not None:
                        b_powers(b)
                    sections(stage, n, 2 * KT, j0 + RING + 3, 1)

                second_half(0, None if b is None else b + 1)
                total(n * 2 + a["c"], 0, n * 2 + a["cross"], flat3(Z))
                scaled(flat3(Z), z_ready)
                sections(stage, n, 2 * KT, KT, RING)
                second_half(KT, None if b is None or not more else b + 2)
                dve.wait_ge(nl_ready, n + (a["nl"] + 1))
                total(n * 2 + (a["c"] + 1), 1, n * 2 + (a["cross"] + 1), flat3(Z))
                step(V_.tensor_tensor(flat3(Z), flat3(Z), RSTD[:, :].unsqueeze(1).to_broadcast([P, QB, TOK]), ALU.mult))
                V_.tensor_tensor(flat3(Z), flat3(Z), GATED[:, blocks, 1, :], ALU.mult).then_inc(z_ready, 1)
                sections(stage, n, 2 * KT, 2 * KT, 2)
                dve.wait_ge(z_ready, n * 2 + (a["z"] + 2))
                dve.wait_ge(operand_hi, n * 2 + (a["q"] + 2))
                V_.tensor_tensor(M[:, blocks, TOK:2 * TOK], flat3(Z), M[:, blocks, 0:TOK].bitcast(F32),
                                 ALU.subtract).then_inc(operand_ready, 2)
                sections(stage, n, 2 * KT, 2 * KT + 2, 2)

            def up_loop(i, first):
                with nc.vector.Fori(first, NU) as n:
                    step.enter(n - first if first else n, 1)
                    up_step(i, n)
                step.leave(NU - first)

            def down(i):
                for n in range(NT):
                    sections(f"down{i}", n, FT, RING, FT - RING)
                    residual_end(f"down{i}", n, FT, FT, n, 4 + i, AT[f"down{i}"]["t"] + FT * (n + 1))
                sections(f"down{i}", n, FT, FT + NT, 1)
                rstd(3 * i + 3)
                sections(f"down{i}", n, FT, FT + NT + 1, RING - 1)

            with nc.vector.Fori(0, KB // 2 - 1) as n:
                step.enter(n, 7)
                up_step(0, n, b=n * 2)
            step.leave(KB // 2 - 1)
            up_step(0, KB // 2 - 1, b=KB - 2, more=False)
            up_loop(0, KB // 2)
            down(0)
            a = AT["gate0"]
            with nc.vector.Fori(0, NT // 2) as e:
                step.enter(e, 4)
                for s in range(2):
                    n = e * 2 + s
                    sections("gate0", e, 2 * KT, KT * s + RING, KT - RING)
                    total(n + a["c"], s, n + a["cross"], flat3(Z))
                    scaled(flat3(Z), z_ready)
                    gated_end("gate0", e, 2 * KT, KT * (s + 1), n, 1, M, PROJ[:, bass.ds(n * (QB * TOK), QB * TOK)])
            step.leave(NT // 2)
            rstd(4)

            def core_u(n):
                dve.wait_ge(split_used, AT["win"]["t"] + KT * (n + 1))
                V_.tensor_tensor(UC[n][:, :, :, :], half_quad(n % 2).rearrange("p m (k j) -> p m j k", j=T),
                                 RSTD[:, :].rearrange("p (k j) -> p j k", j=T).unsqueeze(1).to_broadcast([P, QB, T, NC]),
                                 ALU.mult).then_inc(acc_free, 1)

            def core_scan(b):
                d, par, bl = b // 2, b // 2 % 2, b % 2
                dve.wait_ge(te_in[par], 16 * (d // 2 + 1))
                dve.wait_ge(in_done, b + 1)
                cos, sin = TE[par][:, 0, bl, :, :], TE[par][:, 1, bl, :, :]
                inc = PS[:, 4 + bl, :].rearrange("p (q r k) -> p q r k", q=QP, r=2)
                both = lambda x_: x_.unsqueeze(2).to_broadcast([P, QP, 2, NC])
                V_.tensor_tensor(CA[:, :, :, :], inc, both(cos), ALU.mult)
                V_.tensor_tensor(CB[:, :, :, :], inc, both(sin), ALU.mult).then_inc(inc_free, 1)
                dve.wait_ge(inc_free, b + 1)
                V_.tensor_tensor(CV[:, 0, :, :], CA[:, :, 0, :], CB[:, :, 1, :], ALU.add)
                step(V_.tensor_tensor(CV[:, 1, :, :], CA[:, :, 1, :], CB[:, :, 0, :], ALU.subtract))
                dve.wait_ge(rt_ready, b + 1)
                flat = lambda x_: x_.rearrange("p a b k -> p (a b k)").rearrange("p (r n) -> p r n", r=2)
                w, w_cos, w_sin = flat(CB[:, :, :, :]), flat(CV[:, :, :, :]), flat(CA[:, :, :, :])
                for ri in range(2):
                    last = V_.tensor_tensor_scan(w[:, ri, :], RT[bl][:, :, :].rearrange("p q k -> p (q k)"),
                                                 CV[:, ri, :, :].rearrange("p q k -> p (q k)"), 0.0, ALU.mult, ALU.add)
                last.then_inc(rt_used, 1)
                dve.wait_ge(rt_used, b + 1)
                one = lambda x_: x_.rearrange("p q k -> p (q k)").unsqueeze(1).to_broadcast([P, 2, QP * NC])
                V_.tensor_tensor(w_cos, w, one(cos), ALU.mult)
                step(V_.tensor_tensor(w_sin, w, one(sin), ALU.mult))
                if d >= 2:
                    dve.wait_ge(out_of, d - 1)
                part = lambda x_, ri: x_[:, ri, :].rearrange("p (q k) -> p q k", k=NC)[:, :, 0:NC - 1]
                V_.tensor_tensor(SD[b % 4][:, 0, :, 1:NC], part(w_cos, 0), part(w_sin, 1), ALU.subtract)
                V_.tensor_tensor(SD[b % 4][:, 1, :, 1:NC], part(w_cos, 1), part(w_sin, 0), ALU.add).then_inc(sd_ready, 1)
                dve.wait_ge(sd_ready, b + 1)

            def core_lo(d):
                dve.wait_ge(operand_hi, AT["core"]["q"] + d + 1)
                blocks = slice(KB + 2 * d, KB + 2 * d + 2)
                V_.tensor_tensor(M[:, blocks, TOK:2 * TOK].rearrange("p b (k j) -> p b k j", j=T),
                                 YG[:, :, :, :].rearrange("p b j k -> p b k j"),
                                 M[:, blocks, 0:TOK].bitcast(F32).rearrange("p b (k j) -> p b k j", j=T),
                                 ALU.subtract).then_inc(operand_ready, 1)

            for g in range(RING, CORE_TILES):
                section("win", 0, 0, g)
                if g % KT == KT - 1 and g < KT * NT:
                    core_u(g // KT)
                if g == SCAN[0]:
                    dve.wait_ge(core_ready, 1)
                for b in range(KB):
                    if g == SCAN[b]:
                        core_scan(b)
                for d in range(DUOS):
                    if g == LO[d]:
                        core_lo(d)
            a = AT["out1"]
            dve.wait_ge(split_used, AT["win"]["t"] + CORE_TILES)
            V_.tensor_copy(flat3(VAL), half_quad(0)).then_inc(acc_free, 1)

            def out1_step(n, value=True):
                c = n * 2 + a["c"]
                if value:
                    sections("out1", n, 2 * KT, RING, KT - RING)
                    total(c, 0, n * 2 + a["cross"], flat3(VAL))
                sections("out1", n, 2 * KT, KT, KT)
                total(c + 1, 1, n * 2 + (a["cross"] + 1), flat3(Z))
                gated_end("out1", n, 2 * KT, 2 * KT, n, 3, H, VAL[:, :])

            out1_step(0, value=False)
            with nc.vector.Fori(1, NT) as n:
                step.enter(n - 1, 2)
                out1_step(n)
            step.leave(NT - 1)
            rstd(5)
            up_loop(1, 0)
            down(1)
            a = AT["gate1"]
            for n in range(NT):
                sections("gate1", n, KT, RING, KT - RING)
                total(n + a["c"], n % 2, n + a["cross"], flat3(Z))
                scaled(flat3(Z), z_ready)
                gated_end("gate1", n, KT, KT, n, None, None, PROJ[:, QB * TOK * n:QB * TOK * (n + 1)])
            rstd(7)
            for n in range(NT):
                if n >= 2:
                    dve.wait_ge(aux_done, AT["fin"]["a"] + n)
                for m in range(QB):
                    k = QB * n + m
                    last = V_.tensor_scalar(XF[:, n % 2, m, :], X[:, TOK * k:TOK * k + TOK], VEC[:, 6, k:k + 1], None, ALU.mult)
                last.then_inc(xf_ready, 1)

        @block.tensor
        def _(pe):
            T_ = nc.tensor

            def free(c):
                if not (isinstance(c, int) and c < 2):
                    pe.wait_ge(acc_free, c - 1)

            def products(stage, i, per, j0, c, s, depth, operand, ready, q, after=None):
                free(c)
                for j in range(depth):
                    t, _, slot = tile_at(stage, i, per, j0 + j)
                    pe.wait_ge(ready, q + j + 1)
                    pe.wait_ge(lo_ready, t + 1)
                    for kk in range(TK):
                        k = TK * j + kk
                        for m in range(QB):
                            w = slice(NW * kk + P * m, NW * kk + P * m + P)
                            T_.matmul(PS[:, QB * s + m, :], WHI[:, slot, w], operand(k), start=(k == 0), stop=False)
                            last = T_.matmul(PS[:, QB * s + m, TOK:2 * TOK], WLO[:, slot, w], operand(k)[:, 0:TOK],
                                             start=False, stop=(k == TK * depth - 1))
                    last.then_inc(split_used, 1)
                    if after is not None:
                        after(j)

            def tile_in_place(t, s, j, depth, operand):
                slot = t % RING
                if j == 0:
                    for h in range(2):
                        T_.matmul(PS[:, 2 * s + h, :].rearrange("p (a n) -> p a n", n=P), ZERO[0:1, :],
                                  ZERO[0:1, :].unsqueeze(1).to_broadcast([1, QB, P]), start=True, stop=False)
                pe.wait_ge(lo_ready, t + 1)
                for kk in range(TK):
                    k = TK * j + kk
                    for m in range(QB):
                        w = slice(NW * kk + P * m, NW * kk + P * m + P)
                        dst = PS[:, 2 * s + m // 2, TOK * (m % 2):TOK * (m % 2) + TOK]
                        T_.matmul(dst, WHI[:, slot, w], operand(k)[:, 0:TOK], start=False, stop=False)
                        T_.matmul(dst, WHI[:, slot, w], operand(k)[:, TOK:2 * TOK], start=False, stop=False)
                        last = T_.matmul(dst, WLO[:, slot, w], operand(k)[:, 0:TOK], start=False, stop=(k == TK * depth - 1 and m % 2 == 1))
                last.then_inc(split_used, 1)

            in_h = lambda k: H[:, k, :]
            in_m = lambda k: M[:, k, :]
            in_m2 = lambda k: M[:, KB + k, :]

            pe.wait_ge(ident_ready, 1)
            pe.wait_ge(vec_in, 16 * 8)
            T_.transpose(PS[:, 4, 0:P], NAT[:, :], IDENT[:, :]).then_inc(aux_done, 1)
            for n in range(NT):
                pe.wait_ge(x_in[n], 16)
                if n >= 1:
                    pe.wait_ge(aux_free, n)
                for m in range(QB):
                    for th in range(2):
                        k = QB * n + m
                        last = T_.transpose(PS[:, QB * (n % 2) + m, P * th:P * th + P], XN[:, th, P * k:P * k + P], IDENT[:, :])
                last.then_inc(aux_done, 1)

            def set_up(j):
                a0 = AT["set-up"]["a"]
                if j == 2:
                    pe.wait_ge(aux_free, a0)
                    pe.wait_ge(s5_in, 48)
                    pe.wait_ge(ldt_spread, 1)
                    pe.wait_ge(p_in, 32)
                    for i in range(3):
                        T_.transpose(PS[:, 4, PAIRS * i:PAIRS * i + PAIRS], AN[:, i, :], IDENT[0:PAIRS, 0:PAIRS])
                    for l in range(2):
                        for f in range(2):
                            for th in range(2):
                                at = TOK * f + P * th
                                last = T_.transpose(PS[:, 5 + l, at:at + P], PN[:, l, th, P * f:P * f + P], IDENT[:, :])
                    last.then_inc(aux_done, 1)
                if j == 5:
                    pe.wait_ge(aux_free, a0 + 1)
                    pe.wait_ge(ws_masked, 1)
                    for h in range(HEADS):
                        last = T_.transpose(PS[:, 4 + h // 4, P * (h % 4):P * (h % 4) + P], WN[:, h, :], IDENT[:, :])
                    last.then_inc(aux_done, 1)
                if j == 6:
                    pe.wait_ge(masks_ready, 1)
                    to_column(4, a0 + 2, 1)

            def to_column(bank, a, k):
                pe.wait_ge(aux_free, a)
                pe.wait_ge(rstd_ready, k)
                for th in range(2):
                    last = T_.matmul(PS[:, bank, th:th + 1], RSTD[0:1, P * th:P * th + P], ONE[0:1, 0:1], start=True, stop=True)
                last.then_inc(aux_done, 1)

            for n in range(NT):
                s = n % 2
                if n < 2:
                    pe.wait_ge(aux_free, AT["set-up"]["a"] - 1 if n == 0 else AT["us"]["a"])
                free(n)
                for j in range(KT):
                    t, _, slot = tile_at("v", n, KT, j)
                    pe.wait_ge(operand_ready, j + 1)
                    pe.wait_ge(lo_ready, t + 1)
                    for kk in range(TK):
                        k = TK * j + kk
                        f = slice(NW * kk, NW * kk + NW)
                        for th in range(2):
                            acc = PS[:, QB * s + th, :]
                            hi, lo = M[:, k, P * th:P * th + P], M[:, k, TOK + P * th:TOK + P * th + P]
                            T_.matmul(acc, hi, WHI[:, slot, f], start=(k == 0), stop=False)
                            T_.matmul(acc, hi, WLO[:, slot, f], start=False, stop=False)
                            last = T_.matmul(acc, lo, WHI[:, slot, f], start=False, stop=(k == KB - 1))
                    last.then_inc(split_used, 1)
                    if n == 0:
                        set_up(j)

            a = AT["us"]
            for n in range(NT):
                def mix(j):
                    if j != RING + 2:
                        return
                    s = 1 - n % 2
                    free(a["c"] + n + 1)
                    pe.wait_ge(v_ready, n + 1)
                    pe.wait_ge(ln_in, 48)
                    for m in range(QB):
                        h = QB * n + m
                        for c in range(2):
                            T_.matmul(PS[:, QB * s + m, P * c:P * c + P], V[:, c, P * h:P * h + P], WT[:, h, :],
                                      start=(c == 0), stop=False)
                        last = T_.matmul(PS[:, QB * s + m, 0:TOK].rearrange("p (c t) -> p c t", c=2), ONE[0:1, :],
                                         BS[0:1, h, :].unsqueeze(1).to_broadcast([1, 2, P]), start=False, stop=True)
                    last.then_inc(aux_done, 1)

                pe.wait_ge(aux_free, a["a"] + n)
                products("us", n, KT, 0, a["c"] + n, n % 2, KT, in_m, operand_ready, 0, after=mix)

            def tables(b, s, c, q=True, more=True):
                free(c + 1)
                if more:
                    pe.wait_ge(cm_ready, b + 2)
                    for ri in range(2):
                        last = T_.transpose(PS[:, QB * s, P * ri:P * ri + P], CM[:, ri, :, :].rearrange("p g s -> p (g s)"),
                                            IDENT[:, :])
                if q:
                    pe.wait_ge(qt_ready, b + 1)
                    for i in range(2 * QP):
                        T_.transpose(PS[:, QB * s + 1 + i // 4, P * (i % 4):P * (i % 4) + P],
                                     QT[:, i // 2, i % 2, :, :].rearrange("p j c -> p (j c)"), IDENT[:, :])
                    pe.wait_ge(dt_ready, b + 1)
                    T_.matmul(PS[:, QB * s + 3, 0:P], IDENT[:, :], DG[:, :], start=True, stop=False)
                    for k in range(QP):
                        r = slice(32 * k, 32 * k + 32)
                        for ri in range(2):
                            last = T_.matmul(PS[r, QB * s + 3, 0:P], QT[:, k, ri, 0, :],
                                             DT[:, k, ri, 0:T, :].rearrange("p j c -> p (j c)"), start=False, stop=(ri == 1))
                last.then_inc(aux_done, 1)

            a = AT["out0"]
            pe.wait_ge(aux_free, AT["first"]["a"])
            for n in range(NT):
                after = (lambda j: tables(-1, 0, a["c"] + NT - 1, q=False) if j == MID else None) if n == NT - 1 else None
                products("out0", n, KT, 0, a["c"] + n, n % 2, KT, in_m2, operand_ready, a["q"] - KT, after=after)

            def up_step(i, n, b=None, more=True):
                a, stage = AT[f"up{i}"], f"up{i}"
                for s in range(2):
                    c = n * 2 + (a["c"] + s)
                    after = None
                    if b is not None:
                        pe.wait_ge(aux_free, b + (AT["build"]["a"] + s))
                        after = lambda j: tables(b + s, 1 - s, c, more=(s == 0 or more)) if j == MID else None
                    products(stage, n, 2 * KT, KT * s, c, s, KT, in_h, operand_ready, a["q"] - KT, after=after)

            def up_loop(i, first):
                with nc.tensor.Fori(first, NU) as n:
                    up_step(i, n)

            def down_and_gate(i):
                a = AT[f"down{i}"]
                with nc.tensor.Fori(0, NT // 2) as e:
                    for s in range(2):
                        products(f"down{i}", e, 2 * FT, FT * s, e * 2 + (a["c"] + s), s, FT, in_m, operand_ready, a["q"] - FT)
                a = AT[f"proj{i}"]
                for n in range(NT):
                    pe.wait_ge(acc_free, a["c"] - 1 + n // 2)
                    tile_in_place(a["t"] + n, n, 0, 1, lambda k: PT[:, 2 * i + k, :])
                a = AT[f"gate{i}"]
                with nc.tensor.Fori(0, NT // 2) as e:
                    for s in range(2):
                        products(f"gate{i}", e, 2 * KT, KT * s, e * 2 + (a["c"] + s), s, KT, in_h, operand_ready, a["q"] - KT)

            with nc.tensor.Fori(0, KB // 2 - 1) as n:
                up_step(0, n, b=n * 2)
            up_step(0, KB // 2 - 1, b=KB - 2, more=False)
            pe.wait_ge(aux_free, AT["build"]["a"] + KB)
            up_loop(0, KB // 2)
            down_and_gate(0)

            def into_states(b):
                d, par, bl, n = b // 2, b // 2 % 2, b % 2, b // QB
                if b == 0:
                    pe.wait_ge(acc_free, AT["win"]["c"])
                if bl == 0:
                    pe.wait_ge(tq_in[par], 16 * (d // 2 + 1))
                pe.wait_ge(up_in[n], 256)
                if b >= 2:
                    pe.wait_ge(inc_free, b - 1)
                for q in range(QP):
                    for ri in range(2):
                        c0 = P * q + NC * ri
                        last = T_.matmul(PS[:, 4 + bl, c0:c0 + NC], TQ[par][:, bl, q, ri, :], UP[n][:, b % QB, q, :],
                                         start=True, stop=True)
                last.then_inc(in_done, 1)

            def out_of_states(d):
                par = d % 2
                pe.wait_ge(td_in[par], 80 * (d // 2 + 1))
                pe.wait_ge(sd_ready, 2 * d + 2)
                if d >= 2:
                    pe.wait_ge(yp_ready, d - 1)
                for bl in range(2):
                    b = 2 * d + bl
                    for q in range(QP):
                        dst = PS[:, 6 + par, TOK * bl + NC * q:TOK * bl + NC * q + NC]
                        T_.matmul(dst, TKK[par][:, bl, q, :], UP[b // QB][:, b % QB, q, :], start=True, stop=False)
                        for ri in range(2):
                            last = T_.matmul(dst, TD[par][:, bl, q, ri, :], SD[b % 4][:, ri, q, :], start=False, stop=(ri == 1))
                last.then_inc(out_of, 1)

            a = AT["win"]
            for g in range(CORE_TILES):
                n, j = g // KT, g % KT
                if j == 0:
                    free(a["c"] + n)
                if n < NT:
                    pe.wait_ge(operand_ready, a["q"] - KT + j + 1)
                    tile_in_place(a["t"] + g, n % 2, j, KT, in_m)
                else:
                    pe.wait_ge(operand_ready, a["q"] + j + 1)
                    tile_in_place(a["t"] + g, n % 2, j, KT, in_m2)
                for b in range(KB):
                    if g == SCAN[b]:
                        into_states(b)
                for d in range(DUOS):
                    if g == OUT[d]:
                        out_of_states(d)

            a = AT["out1"]
            pe.wait_ge(yp_ready, DUOS)
            pe.wait_ge(inc_free, KB)

            def out1_column(n, s):
                products("out1", n, 2 * KT, KT * s, n * 2 + (a["c"] + s), s, KT, in_m2, operand_ready, a["q"] - KT)

            out1_column(0, 1)
            with nc.tensor.Fori(1, NT) as n:
                for s in range(2):
                    out1_column(n, s)
            up_loop(1, 0)
            down_and_gate(1)

            a0 = AT["fin"]["a"]
            pe.wait_ge(acc_free, AT["fin"]["c"])
            to_column(0, a0, 7)
            for n in range(NT):
                s = (n + 1) % 2
                if n == 1:
                    pe.wait_ge(aux_free, a0 + 1)
                if n >= 2:
                    pe.wait_ge(out_ready, n - 1)
                pe.wait_ge(xf_ready, n + 1)
                for m in range(QB):
                    for th in range(2):
                        last = T_.transpose(PS[:, QB * s + th, P * m:P * m + P], XF[:, n % 2, m, P * th:P * th + P], IDENT[:, :])
                last.then_inc(aux_done, 1)


INPUTS = ["x", "p", "norm_mix", "norm_ffn", "norm_ple", "norm_final", "gm_w_in", "gm_ln_g", "gm_ln_b", "gm_w_s", "gm_b_s",
          "gm_w_out", "s5_w_in", "s5_a_re", "s5_a_im", "s5_log_dt", "s5_b_re", "s5_b_im", "s5_c_re", "s5_c_im", "s5_d",
          "s5_w_out", "ffn_w1", "ffn_w3", "ffn_w2", "ple_w_gate", "ple_w_proj"]


def kernel(**inputs):
    import numpy as np
    import concourse.bacc as bacc
    from concourse.bass_utils import run_bass_kernel_spmd

    nc = bacc.Bacc("TRN2", target_bir_lowering=False, num_devices=1)
    arrays, args = {}, []
    for name in INPUTS:
        a = np.ascontiguousarray(inputs[name])
        arrays[f"in_{name}"] = a
        args.append(nc.dram_tensor(f"in_{name}", a.shape, mybir.dt.from_np(a.dtype), kind="ExternalInput").ap())
    args.append(nc.dram_tensor("out", (1, TOK, D), F32, kind="ExternalOutput").ap())
    trunk(nc, *args)
    return run_bass_kernel_spmd(nc, [arrays], core_ids=[0]).results[0]["out"]
```

```python
import math
from contextlib import ExitStack

import concourse.bass as bass
from concourse import mybir

F32 = mybir.dt.float32
F32R = mybir.dt.float32r
I32 = mybir.dt.int32
ACT = mybir.ActivationFunctionType
ALU = mybir.AluOpType
AX = mybir.AxisListType
RADD = bass.bass_isa.ReduceOp.add

P = 128
TOK = 256
D = 2048
KB = D // P
DFF = 5632
FB = DFF // P
NW = 512
QB = NW // P
NT = D // NW
TK = 2
KT = KB // TK
FT = FB // TK
NU = DFF // NW
RING = 4
PLE = 256
EPS = 1e-6
HEADS = 16

GROUPS = 128
CH = 16
ST = 64
T = 4
NC = TOK // T
PAIRS = GROUPS // 2
QP = 4
DUOS = KB // 2

STAGES = [
    ("pro", 1, dict(a=5, q=8, r=4)),
    ("set-up", 1, dict(a=3)),
    ("v", NT, dict(t=KT, c=1)),
    ("us", NT, dict(t=KT, c=1, a=1, cross=1, z=1, nl=1, q=2)),
    ("out0", NT, dict(t=KT, c=1, q=2, r=1)),
    ("first", 1, dict(a=1)),
    ("build", KB, dict(a=1)),
    ("up0", NU, dict(t=2 * KT, c=2, cross=2, z=2, nl=1, q=2)),
    ("down0", NT, dict(t=FT, c=1, q=2, r=1)),
    ("proj0", NT, dict(t=1, c=1)),
    ("gate0", NT, dict(t=KT, c=1, cross=1, z=1, nl=1, g=1, q=2, r=1)),
    ("win", NT, dict(t=KT, c=1)),
    ("core", DUOS, dict(q=1)),
    ("pair0", 1, dict(cross=-2)),
    ("out1", NT, dict(t=2 * KT, c=2, cross=2, nl=1, g=1, q=2, r=1)),
    ("up1", NU, dict(t=2 * KT, c=2, cross=2, z=2, nl=1, q=2)),
    ("down1", NT, dict(t=FT, c=1, q=2, r=1)),
    ("proj1", NT, dict(t=1, c=1)),
    ("gate1", NT, dict(t=KT, c=1, cross=1, z=1, nl=1, g=1, r=1)),
    ("fin", 1, dict(a=5)),
]

CORE_ORDER = [(n, j) for n in range(NT) for j in range(KT)]
CORE_ORDER += [(NT + h, j) for js in ((0, 1, 2, 3), (4, 5), (6,), (7,)) for h in range(2) for j in js]
CORE_TILES = len(CORE_ORDER)
SCAN = [KT * (n + 1) + 4 + (2 * i if n < NT - 1 else i + i // 2) for n in range(NT) for i in range(QB)]
OUT = [SCAN[2 * d + 1] + 2 for d in range(DUOS)]
NEED = [CORE_ORDER.index((NT, d)) for d in range(DUOS)]
HI = [min(OUT[d] + 2, NEED[d] - 1) for d in range(DUOS)]
LO = [min(OUT[d] + 3, NEED[d] - 1) for d in range(DUOS)]
MID = 4


def plan():
    at, now = {}, dict(t=0, c=0, a=0, cross=0, z=0, nl=0, g=0, q=0, r=0)
    for name, times, per in STAGES:
        at[name] = dict(now)
        assert now["t"] % RING == 0 and now["c"] % 2 == 0
        for k, v in per.items():
            now[k] += v * times
    at["end"] = now
    return at


AT = plan()


class Chain:

    def __init__(self, eng, sem):
        self.eng, self.sem, self.n, self.base, self.i, self.per = eng, sem, 0, 0, 0, 0

    def __call__(self, ins):
        ins.then_inc(self.sem, 1)
        self.n += 1
        self.eng.wait_ge(self.sem, self.base + self.i * self.per + self.n)

    def enter(self, i, per):
        self.base, self.i, self.per, self.n = self.base + self.n, i, per, 0

    def leave(self, times):
        assert self.n == self.per, (self.n, self.per)
        self.base, self.i, self.n = self.base + self.per * times, 0, 0


def trunk(nc, x, p, norm_mix, norm_ffn, norm_ple, norm_final, gm_w_in, gm_ln_g, gm_ln_b, gm_w_s, gm_b_s,
          gm_w_out, s5_w_in, s5_a_re, s5_a_im, s5_log_dt, s5_b_re, s5_b_im, s5_c_re, s5_c_im, s5_d,
          s5_w_out, ffn_w1, ffn_w3, ffn_w2, ple_w_gate, ple_w_proj, out):
    ctx = ExitStack()
    with ctx:
        def sem(name):
            return ctx.enter_context(nc.semaphore(name))

        KBYTE = 1024
        ARENA = 207 * KBYTE
        base = (nc.sbuf_base + 63) // 64 * 64
        arena = ctx.enter_context(nc.sbuf_tensor("arena", [P, ARENA // 4], F32))
        top = [base]

        def place(name, shape, dt=F32, at=None):
            size = 4
            for s in shape[1:]:
                size *= s
            if at is None:
                at = top[0]
                top[0] += (size + 31) // 32 * 32
                assert top[0] <= base + ARENA, name
            return nc.alloc_sbuf_tensor_at(name, shape, dt, offset=at)

        X = place("X", [P, D // P * TOK])
        h_at = top[0]
        H = place("H", [P, KB, 2 * TOK], F32R)
        m_at = top[0]
        M = place("M", [P, FB, 2 * TOK], F32R)
        RAW = place("RAW", [P, RING, TK * NW])
        WHI = place("WHI", [P, RING, TK * NW], F32R)
        WLO = place("WLO", [P, RING, TK * NW], F32R)
        t1_at = top[0]
        T1 = place("T1", [P, QB * TOK])
        z_at = top[0]
        Z = place("Z", [P, QB * TOK])
        pt_at = top[0]
        PT = place("PT", [P, 2 * (PLE // P), 2 * TOK], F32R)
        IDENT = place("IDENT", [P, P])
        VEC = place("VEC", [P, 8, KB])
        SS = place("SS", [P, TOK])
        SUM = place("SUM", [P, TOK])
        RSTD = place("RSTD", [P, TOK])
        RCOL = place("RCOL", [P, 2])
        ONE = place("ONE", [1, P])
        RHO = place("RHO", [P, PAIRS])
        PAR = place("PAR", [P, 2])
        STAT = place("STAT", [P, 2, 4 * 6])
        MV = place("MV", [P, 2, 2])
        LNR = place("LNR", [P, 2, 1])
        EPSB = place("EPSB", [P, 1])
        BAND = place("BAND", [P, QP])
        DIAG = place("DIAG", [P, 2, 2 * CH])
        ZERO = place("ZERO", [1, P], F32R)
        DG = place("DG", [P, P])

        def h_view(name, shape, off, dt=F32):
            return place(name, shape, dt, at=h_at + off * KBYTE)

        def m_view(name, shape, off, dt=F32):
            return place(name, shape, dt, at=m_at + int(off * KBYTE))

        def shared(whole, lo, name, shape):
            return place(name, shape, F32, at=whole + 4 * lo)

        XN = m_view("XN", [P, 2, D], 32)
        WN = m_view("WN", [P, HEADS, P], 48)
        NAT = m_view("NAT", [P, P], 56)
        AN = m_view("AN", [PAIRS, 3, P], 57)
        LDN = m_view("LDN", [PAIRS, 2], 59)
        PN = m_view("PN", [P, 2, 2, PLE], 60)
        V = h_view("V", [P, 2, D], 0)
        WT = h_view("WT", [P, HEADS, P], 16)
        BS = h_view("BS", [1, HEADS, P], 24)
        LG = m_view("LG", [P, 2, D], 64)
        SV = m_view("SV", [P, QB, TOK], 80)
        PW = m_view("PW", [P, 18, PAIRS], 32)
        SA = m_view("SA", [P, 3, PAIRS], 37)
        PI = m_view("PI", [P, PAIRS], 38, I32)
        LAM = m_view("LAM", [P, 2, T + 1, PAIRS], 84)
        FAC = m_view("FAC", [P, 2, PAIRS], 86.5)
        TURN = m_view("TURN", [P, 2, PAIRS], 87)
        ROT = m_view("ROT", [P, 2, PAIRS, NC], 0)
        ROTP = m_view("ROTP", [P, 6, 2, PAIRS], 64)
        RA = [m_view(f"RA{i}", [P, 2, PAIRS // 4, NC // 2], 68 + 8 * i) for i in range(2)]
        RB = [m_view(f"RB{i}", [P, 2, PAIRS // 4, NC // 2], 72 + 8 * i) for i in range(2)]
        QT = m_view("QT", [P, QP, 2, T, 2 * CH], 64)
        DT = m_view("DT", [P, QP, 2, T + 1, 2 * CH], 68)
        QS = m_view("QS", [P, QP, 2, P], 73)
        QTA = m_view("QTA", [P, QP, T - 1, 2 * CH], 77)
        QTB = m_view("QTB", [P, QP, T - 1, 2 * CH], 78.5)
        DTA = m_view("DTA", [P, QP, 2, 2 * CH], 80)
        DTB = m_view("DTB", [P, QP, 2, 2 * CH], 81)
        BD = m_view("BD", [P, 2, QP, 2, CH], 82)
        CM = m_view("CM", [P, 2, 2, ST], 83)
        KS = m_view("KS", [P, (T - 1) * 2 * CH + P], 87)
        LAMB = m_view("LAMB", [P, 2, T, QP], 87.875)
        TQ = [h_view("TQ0", [P, 2, QP, 2, P], 0), m_view("TQ1", [P, 2, QP, 2, P], 64)]
        TD = [h_view("TD0", [P, 2, QP, 2, P], 8), m_view("TD1", [P, 2, QP, 2, P], 72)]
        TKK = [h_view("TK0", [P, 2, QP, P], 16), m_view("TK1", [P, 2, QP, P], 80)]
        TE = [h_view("TE0", [P, 2, 2, QP, NC], 20), m_view("TE1", [P, 2, 2, QP, NC], 84)]
        CA = h_view("CA", [P, QP, 2, NC], 24)
        CB = h_view("CB", [P, QP, 2, NC], 26)
        CV = h_view("CV", [P, 2, QP, NC], 28)
        RT = [h_view("RT0", [P, QP, NC], 30), h_view("RT1", [P, QP, NC], 31)]
        UC = [m_view(f"UC{n}", [P, QB, T, NC], 32 + 8 * n) for n in range(NT)]
        UP = [m_view(f"UP{n}", [P, QB, QP, NC], 36 + 8 * n) for n in range(NT)]
        YP = shared(t1_at, 0, "YP", [P, 2, QP, NC])
        YG = shared(t1_at, 2 * TOK, "YG", [P, 2, T, NC])
        SD = [shared(at, 2 * TOK * i, f"SD{j}{i}", [P, 2, QP, NC]) for j, at in enumerate((pt_at, z_at)) for i in range(2)]
        VAL = m_view("VAL", [P, QB * TOK], 64)
        GATED = m_view("GATED", [P, FB, 2, TOK], 0)
        PROJ = m_view("PROJ", [P, D // P * TOK], 32)
        ON = m_view("ON", [P, 2, D], 64)
        XF = m_view("XF", [P, 2, QB, TOK], 80)

        PS = ctx.enter_context(nc.psum_tensor("PS", [P, 8, NW], F32))

        tabq = nc.dram_tensor("tabq", (KB, P, QP * 2 * P), F32).ap()
        tabd = nc.dram_tensor("tabd", (KB, P, QP * 2 * P), F32).ap()
        tabk = nc.dram_tensor("tabk", (KB * QP, 2 * CH, (T - 1) * 2 * CH + P), F32).ap()
        ud = nc.dram_tensor("ud", (NT, QP, 2 * CH, QB, T, NC), F32).ap()
        yd = nc.dram_tensor("yd", (DUOS, T, 2 * CH, 2, QP, NC), F32).ap()
        tabe = nc.dram_tensor("tabe", (2, P, PAIRS * NC), F32).ap()

        raw_in = [sem(f"raw_in{s}") for s in range(RING)]
        hi_ready = sem("hi_ready")
        lo_ready = sem("lo_ready")
        split_used = sem("split_used")
        acc_free = sem("acc_free")
        aux_done = sem("aux_done")
        aux_free = sem("aux_free")
        cross_copied = sem("cross_copied")
        z_ready = sem("z_ready")
        nl_ready = sem("nl_ready")
        mixed_ready = sem("mixed_ready")
        gated_ready = sem("gated_ready")
        operand_hi = sem("operand_hi")
        operand_ready = sem("operand_ready")
        squares_ready = sem("squares_ready")
        squares_summed = sem("squares_summed")
        square_total = sem("square_total")
        root_ready = sem("root_ready")
        rstd_ready = sem("rstd_ready")
        dve_chain = sem("dve_chain")
        pool_chain = sem("pool_chain")
        x_in = [sem(f"x_in{n}") for n in range(NT)]
        vec_in = sem("vec_in")
        s5_in = sem("s5_in")
        p_in = sem("p_in")
        ws_in = sem("ws_in")
        ws_masked = sem("ws_masked")
        ident_ready = sem("ident_ready")
        masks_ready = sem("masks_ready")
        ldt_spread = sem("ldt_spread")
        p_ready = sem("p_ready")
        ln_in = sem("ln_in")
        v_ready = sem("v_ready")
        ln_var = sem("ln_var")
        ln_root = sem("ln_root")
        angle_ready = sem("angle_ready")
        sine_ready = sem("sine_ready")
        params_ready = sem("params_ready")
        turns_ready = sem("turns_ready")
        rot_half = sem("rot_half")
        rot_out = sem("rot_out")
        build_clear = sem("build_clear")
        b_in = sem("b_in")
        b_used = sem("b_used")
        c_in = sem("c_in")
        cm_ready = sem("cm_ready")
        q_base = sem("q_base")
        qt_ready = sem("qt_ready")
        dt_ready = sem("dt_ready")
        d_out = sem("d_out")
        qk_out = sem("qk_out")
        tq_in = [sem("tq_in0"), sem("tq_in1")]
        te_in = [sem("te_in0"), sem("te_in1")]
        td_in = [sem("td_in0"), sem("td_in1")]
        core_ready = sem("core_ready")
        up_in = [sem(f"up_in{n}") for n in range(NT)]
        in_done = sem("in_done")
        inc_free = sem("inc_free")
        rt_ready = sem("rt_ready")
        rt_used = sem("rt_used")
        sd_ready = sem("sd_ready")
        out_of = sem("out_of")
        yp_ready = sem("yp_ready")
        ud_in = sem("ud_in")
        yd_in = sem("yd_in")
        yg_in = sem("yg_in")
        xf_ready = sem("xf_ready")
        out_v = sem("out_v")
        out_s = sem("out_s")
        out_done = sem("out_done")

        block = ctx.enter_context(nc.Block())

        def double_rotation(eng, step, m, part, ra, rb):
            n, size = 1 << m, PAIRS // 4
            pairs = slice(size * part, size * part + size)
            old = ROT[:, :, pairs, 0:n]
            turn = lambda ri: ROTP[:, m, ri, pairs].unsqueeze(1).unsqueeze(3).to_broadcast([P, 2, size, n])
            eng.tensor_tensor(ra[:, :, :, 0:n], old, turn(0), ALU.mult)
            step(eng.tensor_tensor(rb[:, :, :, 0:n], old, turn(1), ALU.mult))
            eng.tensor_tensor(ROT[:, 0, pairs, n:2 * n], ra[:, 0, :, 0:n], rb[:, 1, :, 0:n], ALU.subtract)
            step(eng.tensor_tensor(ROT[:, 1, pairs, n:2 * n], ra[:, 1, :, 0:n], rb[:, 0, :, 0:n], ALU.add))

        def table_set(d):
            return (d + 1) % 2

        def tile_src(w, k0, col):
            return w.rearrange("(k p) n -> p k n", p=P)[:, k0:k0 + TK, bass.ds(col, NW)]

        def quad(s, lo):
            return PS[:, QB * s:QB * s + QB, lo:lo + TOK]

        def half_quad(s):
            return PS[:, 2 * s:2 * s + 2, :].rearrange("p b (h t) -> p (b h) t", h=2)

        def flat3(t):
            return t[:, :].rearrange("p (m t) -> p m t", t=TOK)

        def tile_at(stage, i, per, j):
            t0 = AT[stage]["t"]
            if isinstance(i, int):
                t = t0 + i * per + j
                return t, t // RING, t % RING
            assert per % RING == 0
            return i * per + (t0 + j), i * (per // RING) + (t0 + j) // RING, (t0 + j) % RING

        @block.sync
        def _(sp):
            def load(src, stage, i, per, j):
                t, _, slot = tile_at(stage, i, per, j)
                if not (isinstance(t, int) and t < RING):
                    sp.wait_ge(lo_ready, t - (RING - 1))
                sp.dma_start(RAW[:, slot, :].rearrange("p (k n) -> p k n", k=TK), src).then_inc(raw_in[slot], 16)

            def column(w, stage, i, per, col, depth, j0=0, done=0):
                for j in range(done, depth):
                    load(tile_src(w, TK * j, col), stage, i, per, j0 + j)

            def load_x(n):
                sp.dma_start(XN[:, :, NW * n:NW * n + NW],
                             x[0].rearrange("(h p) d -> p h d", p=P)[:, :, NW * n:NW * n + NW]).then_inc(x_in[n], 16)

            load_x(0)
            sp.wait_ge(vec_in, 16 * 5)
            for n in range(NT):
                if n < NT - 1:
                    load_x(n + 1)
                load(tile_src(gm_w_in[0], TK * n, D), "v", 0, KT, n)
            for n in range(NT):
                column(gm_w_in[0], "v", n, KT, D + NW * n, KT, done=RING if n == 0 else 0)
            with nc.sync.Fori(0, NT) as n:
                column(gm_w_in[0], "us", n, KT, n * NW, KT)
            with nc.sync.Fori(0, NT) as n:
                column(gm_w_out[0], "out0", n, KT, n * NW, KT)

            a_build = AT["build"]["a"]

            def load_b(b):
                sp.wait_ge(b_used, b)
                for ri, bw in enumerate((s5_b_re, s5_b_im)):
                    for g in range(2):
                        src = bw[0].rearrange("(q g) s c -> g s q c", g=2)[g, :, bass.ds(b * QP, QP), :]
                        sp.dma_start(BD[ST * g:ST * g + ST, ri, :, g, :], src).then_inc(b_in, 16)

            def load_c(b):
                for ri, cw in enumerate((s5_c_re, s5_c_im)):
                    for g in range(2):
                        sp.dma_start(CM[:, ri, g, :],
                                     cw[0].rearrange("g c s -> (g c) s")[bass.ds(b * P, P), :]).then_inc(c_in, 16)

            def store_d(b):
                sp.wait_ge(dt_ready, b + 1)
                sp.dma_start(tabd[bass.ds(b, 1)].rearrange("b p (q n) -> p (b q) n", n=P),
                             DT[:, :, :, 1:T + 1, :].rearrange("p q r j c -> p (q r) (j c)")).then_inc(d_out, 16)

            def store_qk(b):
                sp.wait_ge(aux_free, b + (a_build + 1))
                sp.dma_start(tabq[bass.ds(b, 1)].rearrange("b p n -> p (b n)"),
                             QS[:, :, :, :].rearrange("p q r n -> p (q r n)")).then_inc(qk_out, 16)
                sp.dma_start(tabk[bass.ds(b * QP, QP)].rearrange("q c n -> (q c) n"), KS[:, :]).then_inc(qk_out, 16)

            def build_column(w, n, off, b, more=True):
                for j in range(KT):
                    load(tile_src(w, TK * j, n * NW), "up0", n, 2 * KT, off + j)
                    if j == MID:
                        store_d(b)
                    if j == MID + 2:
                        store_qk(b)
                        if more:
                            load_c(b + 2)
                    if j == MID + 3 and more:
                        load_b(b + 2)

            load(tile_src(ffn_w1[0], 0, 0), "up0", 0, 2 * KT, 0)
            sp.wait_ge(build_clear, 1)
            load_c(0)
            for ri, bw in enumerate((s5_b_re, s5_b_im)):
                for g in range(2):
                    src = bw[0].rearrange("(q g) s c -> g s q c", g=2)[g, :, 0:QP, :]
                    sp.dma_start(BD[ST * g:ST * g + ST, ri, :, g, :], src).then_inc(b_in, 16)
            for j in range(KT):
                if j:
                    load(tile_src(ffn_w1[0], TK * j, 0), "up0", 0, 2 * KT, j)
                ri, part = j // 4, j % 4
                size = PAIRS // 4 * NC
                sp.dma_start(tabe[ri, :, size * part:size * part + size],
                             ROT[:, ri, PAIRS // 4 * part:PAIRS // 4 * (part + 1), :].rearrange("p q k -> p (q k)")
                             ).then_inc(rot_out, 16)
                if j == MID + 3:
                    sp.wait_ge(aux_free, AT["first"]["a"] + 1)
                    load_c(1)
                    load_b(1)
            with nc.sync.Fori(0, KB // 2 - 1) as n:
                build_column(ffn_w3[0], n, KT, n * 2)
                build_column(ffn_w1[0], n + 1, 0, n * 2 + 1)
            build_column(ffn_w3[0], KB // 2 - 1, KT, KB - 2, more=False)
            build_column(ffn_w1[0], KB // 2, 0, KB - 1, more=False)
            column(ffn_w3[0], "up0", KB // 2, 2 * KT, KB // 2 * NW, KT, j0=KT)

            def up(i, first):
                with nc.sync.Fori(first, NU) as n:
                    column(ffn_w1[i], f"up{i}", n, 2 * KT, n * NW, KT)
                    column(ffn_w3[i], f"up{i}", n, 2 * KT, n * NW, KT, j0=KT)

            def down_and_gate(i):
                with nc.sync.Fori(0, NT // 2) as e:
                    column(ffn_w2[i], f"down{i}", e, 2 * FT, e * (2 * NW), FT)
                    column(ffn_w2[i], f"down{i}", e, 2 * FT, e * (2 * NW) + NW, FT, j0=FT)
                for n in range(NT):
                    column(ple_w_proj[i], f"proj{i}", n, 1, NW * n, 1)
                with nc.sync.Fori(0, NT) as n:
                    column(ple_w_gate[i], f"gate{i}", n, KT, n * NW, KT)

            up(0, KB // 2 + 1)
            down_and_gate(0)

            def duo(table, d):
                return table[2 * d:2 * d + 2].rearrange("b p n -> p b n")

            def load_tq(d):
                par = table_set(d)
                if d >= 2:
                    sp.wait_ge(in_done, 2 * (d - 2) + 2)
                sp.dma_start(TQ[par][:, :, :, :, :].rearrange("p b q r n -> p b (q r n)"), duo(tabq, d)).then_inc(tq_in[par], 16)

            def load_te(d):
                par = table_set(d)
                if d >= 2:
                    sp.wait_ge(sd_ready, 2 * (d - 2) + 2)
                sp.dma_start(TE[par][:, :, :, :, :].rearrange("p r b q k -> p r (b q k)"),
                             tabe.rearrange("r p n -> p r n")[:, :, 2 * QP * NC * d:2 * QP * NC * (d + 1)]).then_inc(te_in[par], 16)

            def load_td(d):
                par = table_set(d)
                if d >= 2:
                    sp.wait_ge(out_of, d - 1)
                sp.dma_start(TD[par][:, :, :, :, :].rearrange("p b q r n -> p b (q r n)"), duo(tabd, d)).then_inc(td_in[par], 16)

            def load_tk(d):
                par = table_set(d)
                for i in range(T):
                    sp.dma_start(TKK[par][2 * CH * i:2 * CH * (i + 1), :, :, :].rearrange("c b q n -> c (b q) n"),
                                 tabk[2 * QP * d:2 * QP * (d + 1), :, 2 * CH * i:2 * CH * i + P].rearrange("x c n -> c x n")
                                 ).then_inc(td_in[par], 16)

            def permute_u(n):
                sp.wait_ge(acc_free, AT["win"]["c"] + n + 1)
                sp.dma_start(ud[n].rearrange("q c m j k -> (q c) (m j k)"),
                             UC[n][:, :, :, :].rearrange("p m j k -> p (m j k)")).then_inc(ud_in, 16)
                sp.wait_ge(ud_in, 16 * (n + 1))
                for i in range(T):
                    sp.dma_start(UP[n][2 * CH * i:2 * CH * (i + 1), :, :, :],
                                 ud[n].rearrange("q c m j k -> j c m q k")[T - 1 - i]).then_inc(up_in[n], 16)

            def store_y(d):
                sp.wait_ge(yp_ready, d + 1)
                sp.dma_start(yd[d].rearrange("j c b q k -> (j c) (b q k)"),
                             YP[:, :, :, :].rearrange("p b q k -> p (b q k)")).then_inc(yd_in, 16)

            def permute_y(d):
                sp.wait_ge(yd_in, 16 * (d + 1))
                if d:
                    sp.wait_ge(operand_ready, AT["core"]["q"] + d)
                for q in range(QP):
                    sp.dma_start(YG[2 * CH * q:2 * CH * (q + 1), :, :, :],
                                 yd[d].rearrange("j c b q k -> q c b j k")[q]).then_inc(yg_in, 16)

            sp.wait_ge(rot_out, 16 * 8)
            sp.wait_ge(d_out, 16 * KB)
            sp.wait_ge(qk_out, 16 + 32 * KB)
            sp.wait_ge(split_used, AT["proj0"]["t"])
            for g in range(CORE_TILES + KT):
                n, j = CORE_ORDER[g] if g < CORE_TILES else (NT + 2, g - CORE_TILES)
                if g % KT == 0 and 2 <= g // KT < NT + 2:
                    permute_u(g // KT - 2)
                if n < NT:
                    src = tile_src(s5_w_in[0], TK * j, NW * n)
                else:
                    src = tile_src(s5_w_out[0], TK * j, D * ((n - NT) % 2) + NW * ((n - NT) // 2))
                load(src, "win", 0, 0, g)
                if g == KT:
                    sp.wait_ge(split_used, AT["win"]["t"])
                for d in range(DUOS):
                    since = g - (KT * d if d < 2 else SCAN[2 * d - 3] + KT + 1)
                    if since == 0:
                        load_tq(d)
                    if since == 1:
                        load_te(d)
                    if since == 2:
                        load_td(d)
                    if since == 3:
                        load_tk(d)
                for d in range(DUOS):
                    if g == OUT[d] + KT:
                        store_y(d)
                    if g == OUT[d] + KT + (1 if d < DUOS - 1 else 0):
                        permute_y(d)
            column(s5_w_out[0], "out1", 1, 2 * KT, NW + D, KT, j0=KT)
            with nc.sync.Fori(2, NT) as n:
                column(s5_w_out[0], "out1", n, 2 * KT, n * NW, KT)
                column(s5_w_out[0], "out1", n, 2 * KT, n * NW + D, KT, j0=KT)
            up(1, 0)
            down_and_gate(1)
            for th in range(2):
                for half, ready in enumerate((out_v, out_s)):
                    sp.wait_ge(ready, th + 1)
                    f = slice(D // 2 * half, D // 2 * (half + 1))
                    sp.dma_start(out[0, P * th:P * th + P, f], ON[:, th, f]).then_inc(out_done, 16)
            sp.wait_ge(out_done, 16 * NT)

        @block.gpsimd
        def _(pool):
            step = Chain(pool, pool_chain)
            G_ = nc.gpsimd
            step(G_.memset(IDENT[:, :], 0.0))
            G_.affine_select(out=IDENT[:, :], in_=IDENT[:, :], compare_op=ALU.not_equal, fill=1.0, base=0,
                             pattern=[[-1, P]], channel_multiplier=1).then_inc(ident_ready, 1)
            G_.memset(ONE[0:1, :], 1.0)
            G_.memset(ZERO[0:1, :].bitcast(F32), 0.0)
            G_.memset(EPSB[:, :], EPS)
            G_.memset(DG[:, :], 0.0)
            step(G_.memset(BAND[:, :], 1.0))
            step(G_.affine_select(out=BAND[:, :], in_=BAND[:, :], compare_op=ALU.is_ge, fill=0.0,
                                  base=0, pattern=[[-2 * CH, QP]], channel_multiplier=1))
            step(G_.affine_select(out=BAND[:, :], in_=BAND[:, :], compare_op=ALU.is_ge, fill=0.0,
                                  base=CH - 1, pattern=[[2 * CH, QP]], channel_multiplier=-1))
            step(G_.tensor_tensor(BAND[:, 0:2], BAND[:, 0:2], BAND[:, 2:4], ALU.add))
            step(G_.tensor_tensor(PAR[:, 0:1], BAND[:, 0:1], BAND[:, 1:2], ALU.add))
            G_.tensor_scalar(PAR[:, 1:2], PAR[:, 0:1], -1.0, 1.0, ALU.mult, ALU.add)
            pool.wait_ge(ident_ready, 1)
            two = IDENT[:, :].rearrange("p (a n) -> p a n", a=2)
            step(G_.tensor_tensor(DIAG[:, :, :], two[:, :, 0:2 * CH], two[:, :, 2 * CH:4 * CH], ALU.add))
            G_.tensor_tensor(DIAG[:, 0, :], DIAG[:, 0, :], DIAG[:, 1, :], ALU.add).then_inc(masks_ready, 1)
            pool.wait_ge(x_in[1], 16)
            pool.dma_start(AN[:, 0, :], s5_a_re[0].rearrange("(q g) s -> q (g s)", g=2)).then_inc(s5_in, 16)
            pool.dma_start(AN[:, 1, :], s5_a_im[0].rearrange("(q g) s -> q (g s)", g=2)).then_inc(s5_in, 16)
            pool.dma_start(LDN[:, :], s5_log_dt[0].rearrange("(q g) -> q g", g=2)).then_inc(s5_in, 16)
            pool.wait_ge(x_in[NT - 1], 16)
            for l in range(2):
                pool.dma_start(PN[:, l, :, :], p[l, 0].rearrange("(h p) d -> p h d", p=P)).then_inc(p_in, 16)
            pool.dma_start(WN[:, :, :], gm_w_s[0].rearrange("h t s -> t h s")).then_inc(ws_in, 16)
            pool.wait_ge(ws_in, 16)
            G_.affine_select(out=WN[:, :, :], in_=WN[:, :, :], compare_op=ALU.is_ge, fill=0.0, base=0,
                             pattern=[[0, HEADS], [-1, P]], channel_multiplier=1).then_inc(ws_masked, 1)

            def all_reduce(k):
                pool.wait_ge(squares_summed, AT[k]["r"])
                G_.partition_all_reduce(SUM[:, :], SS[:, :], P, RADD).then_inc(square_total, 1)

            all_reduce("set-up")
            for i, v in enumerate((gm_ln_g, gm_ln_b)):
                pool.wait_ge(acc_free, AT["v"]["c"] + i + 1)
                pool.dma_start(LG[:, i, :], v[0].unsqueeze(0).to_broadcast([P, D])).then_inc(ln_in, 16)
            pool.dma_start(BS[0:1, :, :], gm_b_s[0:1, :, :]).then_inc(ln_in, 16)

            pool.wait_ge(params_ready, 1)
            pool.wait_ge(mixed_ready, NT)
            pool.wait_ge(split_used, AT["out0"]["t"])
            pair_row = lambda i: RA[0][:, 0, 2 * i:2 * i + 2, :].rearrange("p a b -> p (a b)")
            step(G_.tensor_copy(ROTP[:, 0, :, :], TURN[:, :, :]))
            power = [ROTP[:, m, :, :] for m in range(6)]
            for m in range(1, 6):
                re, im = power[m - 1][:, 0, :], power[m - 1][:, 1, :]
                G_.tensor_tensor(pair_row(0), re, re, ALU.mult)
                G_.tensor_tensor(pair_row(1), im, im, ALU.mult)
                step(G_.tensor_tensor(pair_row(2), re, im, ALU.mult))
                G_.tensor_tensor(power[m][:, 0, :], pair_row(0), pair_row(1), ALU.subtract)
                step(G_.tensor_tensor(power[m][:, 1, :], pair_row(2), pair_row(2), ALU.add))
            G_.memset(ROT[:, 0, :, 0:1], 1.0)
            G_.memset(ROT[:, 1, :, 0:1], 0.0).then_inc(turns_ready, 1)
            pool.wait_ge(turns_ready, 1)
            for m in range(6):
                for h in range(2):
                    double_rotation(G_, step, m, h, RA[0], RB[0])
            pool.wait_ge(rot_half, 1)
            double_rotation(G_, step, 5, 2, RA[0], RB[0])
            pool.wait_ge(rot_half, 2)

            G_.memset(KS[:, :], 0.0).then_inc(qk_out, 16)
            G_.memset(BD[:, :, :, :, :], 0.0).then_inc(build_clear, 1)

            def spread_c(b):
                pool.wait_ge(c_in, b * 64 + 64)
                G_.tensor_tensor(CM[:, :, :, :], CM[:, :, :, :],
                                 PAR[:, :].unsqueeze(1).unsqueeze(3).to_broadcast([P, 2, 2, ST]), ALU.mult).then_inc(cm_ready, 1)

            def c_powers(b, first=False):
                step(G_.tensor_copy(LAMB[:, :, :, :], LAM[:, :, 1:T + 1, bass.ds(b * QP, QP)]))
                pool.wait_ge(aux_free, b + AT["build"]["a"])
                if not first:
                    pool.wait_ge(d_out, b * 16)
                c = lambda ri: DT[:, :, ri, 0:1, :].to_broadcast([P, QP, 2, 2 * CH])
                for j in (1, 3):
                    lam = lambda ri: LAMB[:, ri, j - 1:j + 1, :].rearrange("p j q -> p q j").unsqueeze(3).to_broadcast(
                        [P, QP, 2, 2 * CH])
                    G_.tensor_tensor(DTA[:, :, :, :], c(0), lam(0), ALU.mult)
                    step(G_.tensor_tensor(DTB[:, :, :, :], c(1), lam(1), ALU.mult))
                    step(G_.tensor_tensor(DT[:, :, 0, j:j + 2, :], DTA[:, :, :, :], DTB[:, :, :, :], ALU.add))
                    G_.tensor_tensor(DTA[:, :, :, :], c(1), lam(0), ALU.mult)
                    step(G_.tensor_tensor(DTB[:, :, :, :], c(0), lam(1), ALU.mult))
                    last = G_.tensor_tensor(DT[:, :, 1, j:j + 2, :], DTA[:, :, :, :], DTB[:, :, :, :], ALU.subtract)
                    if j == 1:
                        step(last)
                last.then_inc(dt_ready, 1)
                pool.wait_ge(dt_ready, b + 1)

            spread_c(0)
            c_powers(0, first=True)
            spread_c(1)
            all_reduce("up0")
            with nc.gpsimd.Fori(1, KB - 1) as b:
                step.enter(b - 1, 8)
                c_powers(b)
                spread_c(b + 1)
            step.leave(KB - 2)
            c_powers(KB - 1)
            all_reduce("proj0")
            all_reduce("win")

            def decay(b, par):
                G_.tensor_copy(RT[par][:, :, 1:NC],
                               RHO[:, bass.ds(b * QP, QP)].unsqueeze(2).to_broadcast([P, QP, NC - 1])).then_inc(rt_ready, 1)

            pool.wait_ge(split_used, AT["win"]["t"])
            for par in range(2):
                G_.memset(RT[par][:, :, 0:1], 0.0)
            for i in range(4):
                last = G_.memset(SD[i][:, :, :, 0:1], 0.0)
            last.then_inc(core_ready, 1)
            for par in range(2):
                decay(par, par)
            with nc.gpsimd.Fori(1, KB // 2) as e:
                for par in range(2):
                    pool.wait_ge(rt_used, e * 2 + (par - 1))
                    decay(e * 2 + par, par)

            all_reduce("up1")
            all_reduce("proj1")
            all_reduce("fin")

        @block.scalar
        def _(act):
            A_ = nc.scalar

            def section(stage, i, per, j):
                t, rnd, slot = tile_at(stage, i, per, j + RING)
                if isinstance(t, int) and t >= AT["end"]["t"]:
                    return
                act.wait_ge(raw_in[slot], rnd * 16 + 16)
                act.wait_ge(split_used, t - (RING - 1))
                A_.activation(WHI[:, slot, :], RAW[:, slot, :], ACT.Copy).then_inc(hi_ready, 1)

            def sections(stage, i, per, j0, count):
                for j in range(j0, j0 + count):
                    section(stage, i, per, j)

            def cross(c, s, r, t_end):
                act.wait_ge(split_used, t_end)
                act.wait_ge(acc_free, c)
                act.wait_ge(squares_summed, r)
                A_.activation(flat3(T1), quad(s, TOK), ACT.Copy).then_inc(cross_copied, 1)

            def high_parts(n, vec, dst, signal, value):
                act.wait_ge(signal, value)
                for m in range(QB):
                    k = n * QB + m
                    last = A_.activation(dst[:, bass.ds(k, 1), 0:TOK].rearrange("p k t -> p (k t)"),
                                         X[:, bass.ds(k * TOK, TOK)], ACT.Identity, scale=VEC[:, vec, bass.ds(k, 1)])
                last.then_inc(operand_hi, 2)

            def squares(n, r, signal, value):
                act.wait_ge(signal, value)
                if not (isinstance(r, int) and r == 0):
                    act.wait_ge(squares_summed, r)
                A_.activation(T1[:, :], X[:, bass.ds(n * (QB * TOK), QB * TOK)], ACT.Square).then_inc(squares_ready, 1)

            def root(k):
                act.wait_ge(square_total, k)
                A_.activation(SUM[:, :], SUM[:, :], ACT.Sqrt, scale=1.0 / D, bias=EPSB[:, 0:1]).then_inc(root_ready, 1)

            rows = 0
            for v in (norm_mix, norm_ffn, norm_ple, norm_final, s5_d):
                v = v.rearrange("(k p) -> k p", p=P) if len(v.shape) == 1 else v.rearrange("l (k p) -> (l k) p", p=P)
                act.dma_start(NAT[rows:rows + v.shape[0], :], v).then_inc(vec_in, 16)
                rows += v.shape[0]
            act.wait_ge(aux_done, 1)
            A_.activation(VEC[:, :, :].rearrange("p v k -> p (v k)"), PS[:, 4, 0:P], ACT.Copy).then_inc(aux_free, 1)
            for n in range(NT):
                high_parts(n, 0, M, aux_free, n + 2)
                act.wait_ge(raw_in[n], 16)
                A_.activation(WHI[:, n, :], RAW[:, n, :], ACT.Copy).then_inc(hi_ready, 1)
            for n in range(NT):
                squares(n, n, aux_free, n + 2)
                section("v", 0, 0, n)

            setup = AT["set-up"]["a"]
            for n in range(NT):
                if n == 0:
                    act.wait_ge(aux_done, setup + 1)
                    for h in range(2):
                        A_.activation(PT[:, 2 * h:2 * h + 2, 0:TOK], PS[:, 5 + h, :].rearrange("p (k t) -> p k t", t=TOK), ACT.Copy)
                    A_.activation(SA[:, :, :], PS[:, 4, 0:3 * PAIRS].rearrange("p (v k) -> p v k", v=3),
                                  ACT.Copy).then_inc(p_ready, 1)
                    sections("v", n, KT, RING, 2)
                    act.wait_ge(aux_done, setup + 2)
                    A_.activation(WT[:, :, :].rearrange("p h t -> p (h t)"),
                                  PS[:, 4:8, :].rearrange("p b n -> p (b n)"), ACT.Copy).then_inc(aux_free, 1)
                    root(1)
                    sections("v", n, KT, RING + 2, RING)
                    act.wait_ge(aux_done, setup + 3)
                    A_.activation(RCOL[:, :], PS[:, 2, 0:2], ACT.Copy).then_inc(aux_free, 1)
                    act.wait_ge(aux_free, setup + 3)
                else:
                    sections("v", n, KT, RING, KT - RING)
                if n == 1:
                    act.wait_ge(angle_ready, 1)
                    A_.activation(PW[:, 8:10, :], PW[:, 8:10, :], ACT.Sin).then_inc(sine_ready, 1)
                act.wait_ge(split_used, AT["v"]["t"] + KT * (n + 1))
                for th in range(2):
                    last = A_.activation(V[:, th, NW * n:NW * n + NW], PS[:, QB * (n % 2) + th, :],
                                         ACT.Gelu_apprx_tanh, scale=RCOL[:, th:th + 1])
                last.then_inc(acc_free, 1)
                if n > 0:
                    sections("v", n, KT, KT, 2)
                if n == NT - 1:
                    act.wait_ge(ln_var, 1)
                    A_.activation(LNR[:, :, :], MV[:, :, 1:2], ACT.Sqrt, bias=EPSB[:, 0:1]).then_inc(ln_root, 1)
                sections("v", n, KT, KT + 2, 2)

            a = AT["us"]
            for n in range(NT):
                sections("us", n, KT, RING, 3)
                act.wait_ge(aux_done, a["a"] + n + 1)
                A_.activation(SV[:, :, :], quad(1 - n % 2, 0), ACT.Copy).then_inc(aux_free, 1)
                sections("us", n, KT, RING + 3, 1)
                cross(a["c"] + n, n % 2, a["r"], a["t"] + KT * (n + 1))
                sections("us", n, KT, KT, 1)
                act.wait_ge(z_ready, a["z"] + n + 1)
                A_.activation(T1[:, :], Z[:, :], ACT.Gelu_apprx_tanh).then_inc(nl_ready, 1)
                sections("us", n, KT, KT + 1, 1)
                act.wait_ge(mixed_ready, n + 1)
                A_.activation(M[:, KB + QB * n:KB + QB * n + QB, 0:TOK], flat3(Z), ACT.Copy).then_inc(operand_hi, 2)
                sections("us", n, KT, KT + 2, 2)

            def residual_end(stage, i, per, j, n, vec):
                a = AT[stage]
                section(stage, i, per, j)
                high_parts(n, vec, H, acc_free, n + (a["c"] + 1))
                section(stage, i, per, j + 1)
                squares(n, n + a["r"], acc_free, n + (a["c"] + 1))
                sections(stage, i, per, j + 2, 2)

            def gated_end(stage, i, per, j, n, vec, dst, signal, value):
                a = AT[stage]
                section(stage, i, per, j)
                act.wait_ge(signal, value)
                A_.activation(T1[:, :], Z[:, :], ACT.Sigmoid).then_inc(nl_ready, 1)
                section(stage, i, per, j + 1)
                if dst is not None:
                    high_parts(n, vec, dst, gated_ready, n + (a["g"] + 1))
                squares(n, n + a["r"], gated_ready, n + (a["g"] + 1))
                sections(stage, i, per, j + 2, 2)

            a_build = AT["build"]["a"]

            def tables_out(b, q, s, c=True):
                if c:
                    act.wait_ge(aux_done, b + (a_build + 1))
                    for ri in range(2):
                        last = A_.activation(DT[:, :, ri, 0, :],
                                             PS[:, QB * s, P * ri:P * ri + P].rearrange("p (q c) -> p q c", q=QP),
                                             ACT.Copy, scale=(-1.0 if ri else 1.0))
                    if not q:
                        last.then_inc(aux_free, 1)
                if q:
                    act.wait_ge(aux_done, b + (a_build + 1))
                    act.wait_ge(qk_out, b * 32 + 16)
                    A_.activation(QS[:, :, :, :].rearrange("p q r n -> p (q r n)"),
                                  PS[:, QB * s + 1:QB * s + 3, :].rearrange("p b n -> p (b n)"), ACT.Copy)
                    A_.activation(KS[:, (T - 1) * 2 * CH:], PS[:, QB * s + 3, 0:P], ACT.Copy).then_inc(aux_free, 1)

            for n in range(NT):
                sections("out0", n, KT, RING, 3)
                if n == NT - 1:
                    tables_out(-1, False, 0)
                sections("out0", n, KT, RING + 3, 1)
                residual_end("out0", n, KT, KT, n, 2)
            root(2)

            def up_step(i, n, b=None, more=True):
                a, stage = AT[f"up{i}"], f"up{i}"
                sections(stage, n, 2 * KT, RING, 1)
                if b is not None:
                    tables_out(b, True, 1)
                sections(stage, n, 2 * KT, RING + 1, 3)
                cross(n * 2 + a["c"], 0, a["r"], n * (2 * KT) + (a["t"] + KT))
                section(stage, n, 2 * KT, KT)
                act.wait_ge(z_ready, n * 2 + (a["z"] + 1))
                A_.activation(GATED[:, bass.ds(n * QB, QB), 1, :], flat3(Z), ACT.Silu).then_inc(nl_ready, 1)
                sections(stage, n, 2 * KT, KT + 1, RING)
                if b is not None:
                    tables_out(b + 1, True, 0, c=more)
                sections(stage, n, 2 * KT, KT + RING + 1, 3)
                cross(n * 2 + (a["c"] + 1), 1, a["r"], n * (2 * KT) + (a["t"] + 2 * KT))
                sections(stage, n, 2 * KT, 2 * KT, 2)
                act.wait_ge(z_ready, n * 2 + (a["z"] + 2))
                A_.activation(M[:, bass.ds(n * QB, QB), 0:TOK], flat3(Z), ACT.Copy).then_inc(operand_hi, 2)
                sections(stage, n, 2 * KT, 2 * KT + 2, 2)

            def up_loop(i, first):
                with nc.scalar.Fori(first, NU) as n:
                    up_step(i, n)

            def down(i):
                a = AT[f"proj{i}"]

                def proj(n):
                    act.wait_ge(split_used, a["t"] + n + 1)
                    A_.activation(PROJ[:, QB * TOK * n:QB * TOK * (n + 1)].rearrange("p (m t) -> p m t", t=TOK),
                                  half_quad(n), ACT.Copy).then_inc(acc_free, 1)

                d, stage = AT[f"down{i}"], f"down{i}"
                for n in range(NT):
                    sections(stage, n, FT, RING, FT - RING)
                    if n < NT - 1:
                        residual_end(stage, n, FT, FT, n, 4 + i)
                section(stage, n, FT, FT)
                high_parts(n, 4 + i, H, acc_free, d["c"] + n + 1)
                proj(0)
                section(stage, n, FT, FT + 1)
                proj(1)
                squares(n, n + d["r"], acc_free, d["c"] + n + 1)
                section(stage, n, FT, FT + 2)
                proj(2)
                section(stage, n, FT, FT + 3)
                proj(3)
                sections(stage, n, FT, FT + NT, 1)
                root(3 * i + 3)
                sections(stage, n, FT, FT + NT + 1, RING - 1)

            act.wait_ge(rot_out, 16 * 8)
            with nc.scalar.Fori(0, KB // 2 - 1) as n:
                up_step(0, n, b=n * 2)
            up_step(0, KB // 2 - 1, b=KB - 2, more=False)
            act.wait_ge(d_out, 16 * KB)
            act.wait_ge(qk_out, 32 * KB + 16)
            up_loop(0, KB // 2)
            down(0)
            a = AT["gate0"]
            with nc.scalar.Fori(0, NT // 2) as e:
                for s in range(2):
                    n = e * 2 + s
                    sections("gate0", e, 2 * KT, KT * s + RING, KT - RING)
                    cross(n + a["c"], s, n + a["r"], n * KT + (a["t"] + KT))
                    gated_end("gate0", e, 2 * KT, KT * (s + 1), n, 1, M, z_ready, n + (a["z"] + 1))
            root(4)

            def core_gelu(d):
                act.wait_ge(out_of, d + 1)
                if d:
                    act.wait_ge(yd_in, 16 * d)
                A_.activation(YP[:, :, :, :].rearrange("p b q k -> p (b q k)"), PS[:, 6 + d % 2, :],
                              ACT.Gelu_apprx_tanh).then_inc(yp_ready, 1)

            def core_hi(d):
                act.wait_ge(yg_in, 64 * (d + 1))
                A_.activation(M[:, KB + 2 * d:KB + 2 * d + 2, 0:TOK].rearrange("p b (k j) -> p b k j", j=T),
                              YG[:, :, :, :].rearrange("p b j k -> p b k j"), ACT.Copy).then_inc(operand_hi, 1)

            a_core = AT["core"]
            for g in range(RING, CORE_TILES):
                section("win", 0, 0, g)
                for d in range(DUOS):
                    if g == OUT[d]:
                        core_gelu(d)
                    if g == HI[d]:
                        core_hi(d)

            a = AT["out1"]

            def out1_step(n):
                sections("out1", n, 2 * KT, RING, KT - RING)
                cross(n * 2 + a["c"], 0, n + a["r"], n * (2 * KT) + (a["t"] + KT))
                sections("out1", n, 2 * KT, KT, KT)
                cross(n * 2 + (a["c"] + 1), 1, n + a["r"], n * (2 * KT) + (a["t"] + 2 * KT))
                gated_end("out1", n, 2 * KT, 2 * KT, n, 3, H, acc_free, n * 2 + (a["c"] + 2))

            gated_end("out1", 0, 2 * KT, 2 * KT, 0, 3, H, acc_free, a["c"] + 2)
            with nc.scalar.Fori(1, NT) as n:
                out1_step(n)
            root(5)
            up_loop(1, 0)
            down(1)
            a, a0 = AT["gate1"], AT["fin"]["a"]

            def take_out(n):
                act.wait_ge(aux_done, a0 + n + 1)
                for th in range(2):
                    last = A_.activation(ON[:, th, NW * n:NW * n + NW], PS[:, QB * (n % 2) + th, :], ACT.Copy)
                last.then_inc(aux_free, 1)

            for n in range(NT):
                sections("gate1", n, KT, RING, 2)
                if n:
                    take_out(n - 1)
                sections("gate1", n, KT, RING + 2, 2)
                cross(n + a["c"], n % 2, n + a["r"], a["t"] + KT * (n + 1))
                gated_end("gate1", n, KT, KT, n, None, None, z_ready, n + (a["z"] + 1))
            take_out(NT - 1)
            root(7)
            act.wait_ge(aux_done, a0 + NT + 1)
            A_.activation(RCOL[:, :], PS[:, 4, 0:2], ACT.Copy).then_inc(aux_free, 1)
            act.wait_ge(aux_free, a0 + NT + 1)
            for th in range(2):
                A_.activation(ON[:, th, D // 2:], ON[:, th, D // 2:], ACT.Copy, scale=RCOL[:, th:th + 1]).then_inc(out_s, 1)

        @block.vector
        def _(dve):
            step = Chain(dve, dve_chain)
            V_ = nc.vector

            def section(stage, i, per, j):
                t, _, slot = tile_at(stage, i, per, j + RING)
                if isinstance(t, int) and t >= AT["end"]["t"]:
                    return
                dve.wait_ge(hi_ready, t + 1)
                V_.tensor_tensor(WLO[:, slot, :], RAW[:, slot, :], WHI[:, slot, :].bitcast(F32), ALU.subtract).then_inc(lo_ready, 1)

            def sections(stage, i, per, j0, count):
                for j in range(j0, j0 + count):
                    section(stage, i, per, j)

            def total(c, s, count, dst):
                dve.wait_ge(cross_copied, count + 1)
                V_.tensor_tensor(dst, quad(s, 0), flat3(T1), ALU.add).then_inc(acc_free, 1)
                dve.wait_ge(acc_free, c + 1)

            def scaled(dst, signal):
                V_.tensor_tensor(dst, flat3(Z), RSTD[:, :].unsqueeze(1).to_broadcast([P, QB, TOK]), ALU.mult).then_inc(signal, 1)

            def low_parts(n, vec, dst, q):
                dve.wait_ge(operand_hi, q + 2)
                for m in range(QB):
                    k = n * QB + m
                    last = V_.scalar_tensor_tensor(dst[:, bass.ds(k, 1), TOK:2 * TOK].rearrange("p k t -> p (k t)"),
                                                   X[:, bass.ds(k * TOK, TOK)], VEC[:, vec, bass.ds(k, 1)],
                                                   dst[:, bass.ds(k, 1), 0:TOK].rearrange("p k t -> p (k t)").bitcast(F32),
                                                   ALU.mult, ALU.subtract)
                last.then_inc(operand_ready, 2)

            def sum_squares(r):
                dve.wait_ge(squares_ready, r + 1)
                step(V_.tensor_reduce(Z[:, 0:TOK], T1[:, :].rearrange("p (m t) -> p t m", t=TOK), AX.X, ALU.add))
                if not (isinstance(r, int) and r == 0):
                    dve.wait_ge(squares_summed, r)
                V_.tensor_tensor(SS[:, :], SS[:, :], Z[:, 0:TOK], ALU.add).then_inc(squares_summed, 1)

            def rstd(k):
                dve.wait_ge(root_ready, k)
                V_.reciprocal(RSTD[:, :], SUM[:, :]).then_inc(rstd_ready, 1)
                dve.wait_ge(rstd_ready, k)
                step(V_.memset(SS[:, :], 0.0))

            def take_x(n):
                dve.wait_ge(aux_done, n + 2)
                dve.wait_ge(aux_free, n + 1)
                V_.tensor_copy(X[:, QB * TOK * n:QB * TOK * (n + 1)].rearrange("p (m t) -> p m t", t=TOK),
                               quad(n % 2, 0)).then_inc(aux_free, 1)

            step(V_.memset(SS[:, :], 0.0))
            take_x(0)
            for n in range(NT):
                if n < NT - 1:
                    take_x(n + 1)
                dve.wait_ge(aux_free, n + 2)
                low_parts(n, 0, M, 2 * n)
                dve.wait_ge(hi_ready, n + 1)
                V_.tensor_tensor(WLO[:, n, :], RAW[:, n, :], WHI[:, n, :].bitcast(F32), ALU.subtract).then_inc(lo_ready, 1)
            dve.wait_ge(s5_in, 48)
            V_.tensor_copy(AN[:, 2, :].rearrange("q (g s) -> q g s", g=2),
                           LDN[:, :].unsqueeze(2).to_broadcast([PAIRS, 2, ST])).then_inc(ldt_spread, 1)
            for n in range(NT):
                sum_squares(n)
                section("v", 0, 0, n)
            dve.wait_ge(p_ready, 1)
            for h in range(2):
                last = V_.tensor_tensor(PT[:, 2 * h:2 * h + 2, TOK:2 * TOK], PS[:, 5 + h, :].rearrange("p (k t) -> p k t", t=TOK),
                                        PT[:, 2 * h:2 * h + 2, 0:TOK].bitcast(F32), ALU.subtract)
            last.then_inc(aux_free, 1)
            sections("v", 0, 0, RING, 2)
            rstd(1)
            sections("v", 0, 0, RING + 2, KT - RING - 2)

            def stats(n):
                dve.wait_ge(acc_free, AT["v"]["c"] + n + 1)
                for th in range(2):
                    last = V_.bn_stats(STAT[:, th, 6 * n:6 * n + 6], V[:, th, NW * n:NW * n + NW])
                step(last)

            def norm_quad(n):
                f = slice(NW * n, NW * n + NW)
                for th in range(2):
                    last = V_.tensor_scalar(V[:, th, f], V[:, th, f], MV[:, th, 0:1], LNR[:, th, :], ALU.subtract, ALU.mult)
                step(last)
                step(V_.tensor_tensor(V[:, :, f], V[:, :, f], LG[:, 0, f].unsqueeze(1).to_broadcast([P, 2, NW]), ALU.mult))
                V_.tensor_tensor(V[:, :, f], V[:, :, f], LG[:, 1, f].unsqueeze(1).to_broadcast([P, 2, NW]),
                                 ALU.add).then_inc(v_ready, 1)

            W = lambda i: PW[:, i, :]
            LOG2E, MAGIC = 1.4426950408889634, 12582912.0

            def tt(o, a, b, op):
                step(V_.tensor_tensor(o, a, b, op))

            def ts(o, a, s1, s2, op0, op1):
                step(V_.tensor_scalar(o, a, s1, s2, op0, op1))

            def stt(o, a, s, b, op0, op1):
                step(V_.scalar_tensor_tensor(o, a, s, b, op0, op1))

            pauses = [KT]

            def pause():
                j = pauses[0]
                section("v", 0, 0, j)
                if j % KT == 2:
                    stats(j // KT - 1)
                pauses[0] += 1

            def exponential(dst, src, minus_one):
                c, k, r, q = W(10), W(11), W(12), W(13)
                ts(c, src, -88.5, 89.0, ALU.max, ALU.min)
                ts(k, c, LOG2E, MAGIC, ALU.mult, ALU.add)
                ts(k, k, MAGIC, -127.0, ALU.subtract, ALU.max)
                stt(r, k, -0.693359375, c, ALU.mult, ALU.add)
                stt(r, k, 2.12194440e-4, r, ALU.mult, ALU.add)
                pause()
                ts(q, r, 1.0 / math.factorial(8), 0.0, ALU.mult, ALU.add)
                for n in range(7, 0, -1):
                    stt(q, q, 1.0 / math.factorial(n), r, ALU.add, ALU.mult)
                pause()
                ts(PI[:, :], k, 127.0, 8388608.0, ALU.add, ALU.mult)
                two_k = PI[:, :].bitcast(F32)
                tt(q, q, two_k, ALU.mult)
                if minus_one:
                    ts(c, two_k, -1.0, 0.0, ALU.add, ALU.add)
                    tt(dst, q, c, ALU.add)
                else:
                    tt(dst, q, two_k, ALU.add)

            a_re, a_im, dt = SA[:, 0, :], SA[:, 1, :], SA[:, 2, :]
            exponential(dt, dt, False)
            tt(W(0), a_re, dt, ALU.mult)
            pause()
            tt(W(2), a_im, dt, ALU.mult)
            ts(W(3), W(2), 0.5 / math.pi, MAGIC, ALU.mult, ALU.add)
            ts(W(3), W(3), MAGIC, 0.0, ALU.subtract, ALU.add)
            stt(W(2), W(3), -6.28125, W(2), ALU.mult, ALU.add)
            stt(W(2), W(3), -0.00193500518798828125, W(2), ALU.mult, ALU.add)
            stt(W(2), W(3), -3.0199159819567521e-7, W(2), ALU.mult, ALU.add)
            ts(W(8), W(2), 0.5, 0.0, ALU.mult, ALU.add)
            stt(W(9), W(8), -1.0, W(8), ALU.mult, ALU.max)
            V_.tensor_scalar(W(9), W(9), -1.0, math.pi / 2, ALU.mult, ALU.add).then_inc(angle_ready, 1)
            exponential(W(1), W(0), True)
            pause()
            pause()
            dve.wait_ge(sine_ready, 1)
            sn, cm1, im, re, r1 = W(2), W(3), W(4), W(5), W(6)
            tt(sn, W(8), W(9), ALU.mult)
            ts(sn, sn, 2.0, 0.0, ALU.mult, ALU.add)
            tt(cm1, W(8), W(8), ALU.mult)
            ts(cm1, cm1, -2.0, 0.0, ALU.mult, ALU.add)
            ts(r1, W(1), 1.0, 0.0, ALU.add, ALU.add)
            tt(im, r1, sn, ALU.mult)
            ts(re, cm1, 1.0, 0.0, ALU.add, ALU.add)
            ts(W(14), re, 1.0, 0.0, ALU.mult, ALU.add)
            ts(W(15), sn, 1.0, 0.0, ALU.mult, ALU.add)
            pause()
            tt(re, re, W(1), ALU.mult)
            tt(re, re, cm1, ALU.add)
            ts(LAM[:, 0, 1, :], re, 1.0, 0.0, ALU.add, ALU.add)
            ts(LAM[:, 1, 1, :], im, 1.0, 0.0, ALU.mult, ALU.add)
            pause()
            tt(W(7), a_re, a_re, ALU.mult)
            tt(W(8), a_im, a_im, ALU.mult)
            tt(W(7), W(7), W(8), ALU.add)
            step(V_.reciprocal(W(7), W(7)))
            tt(W(8), re, a_re, ALU.mult)
            tt(W(9), im, a_im, ALU.mult)
            tt(W(8), W(8), W(9), ALU.add)
            tt(FAC[:, 0, :], W(8), W(7), ALU.mult)
            pause()
            tt(W(8), im, a_re, ALU.mult)
            tt(W(9), re, a_im, ALU.mult)
            tt(W(8), W(8), W(9), ALU.subtract)
            tt(FAC[:, 1, :], W(8), W(7), ALU.mult)
            tt(W(7), r1, r1, ALU.mult)
            tt(RHO[:, :], W(7), W(7), ALU.mult)

            def product(out_re, out_im, x_re, x_im, y_re, y_im, sc):
                V_.tensor_tensor(sc[0], x_re, y_re, ALU.mult)
                V_.tensor_tensor(sc[1], x_im, y_im, ALU.mult)
                V_.tensor_tensor(sc[2], x_re, y_im, ALU.mult)
                tt(sc[3], x_im, y_re, ALU.mult)
                V_.tensor_tensor(out_re, sc[0], sc[1], ALU.subtract)
                tt(out_im, sc[2], sc[3], ALU.add)

            sc = [W(10), W(11), W(12), W(13)]
            for j in range(2, T + 1):
                pause()
                product(LAM[:, 0, j, :], LAM[:, 1, j, :], LAM[:, 0, j - 1, :], LAM[:, 1, j - 1, :],
                        LAM[:, 0, 1, :], LAM[:, 1, 1, :], sc)
            pause()
            product(W(16), W(17), W(14), W(15), W(14), W(15), sc)
            product(TURN[:, 0, :], TURN[:, 1, :], W(16), W(17), W(16), W(17), sc)
            V_.memset(W(16), 0.0).then_inc(params_ready, 1)
            while pauses[0] < KT * NT:
                pause()

            section("us", 0, 0, 0)
            stats(NT - 1)
            section("us", 0, 0, 1)
            V_.bn_aggr(MV[:, 0, :], STAT[:, 0, :])
            V_.bn_aggr(MV[:, 1, :], STAT[:, 1, :]).then_inc(ln_var, 1)
            section("us", 0, 0, 2)
            dve.wait_ge(ln_in, 48)
            dve.wait_ge(ln_root, 1)
            step(V_.reciprocal(LNR[:, :, :], LNR[:, :, :]))
            norm_quad(0)
            section("us", 0, 0, 3)

            a = AT["us"]
            for n in range(NT):
                sections("us", n, KT, RING, 2)
                if n < NT - 1:
                    norm_quad(n + 1)
                sections("us", n, KT, RING + 2, 2)
                total(a["c"] + n, n % 2, a["cross"] + n, flat3(Z))
                scaled(flat3(Z), z_ready)
                section("us", n, KT, KT)
                dve.wait_ge(nl_ready, a["nl"] + n + 1)
                dve.wait_ge(aux_free, a["a"] + n + 1)
                V_.tensor_tensor(flat3(Z), SV[:, :, :], flat3(T1), ALU.mult).then_inc(mixed_ready, 1)
                section("us", n, KT, KT + 1)
                dve.wait_ge(mixed_ready, n + 1)
                dve.wait_ge(operand_hi, a["q"] + 2 * n + 2)
                blocks = slice(KB + QB * n, KB + QB * n + QB)
                V_.tensor_tensor(M[:, blocks, TOK:2 * TOK], flat3(Z), M[:, blocks, 0:TOK].bitcast(F32),
                                 ALU.subtract).then_inc(operand_ready, 2)
                sections("us", n, KT, KT + 2, 2)

            a_build = AT["build"]["a"]

            def b_scaled(b, first=False):
                dve.wait_ge(b_in, b * 64 + 64)
                if not first:
                    dve.wait_ge(aux_done, b + a_build)
                pairs = bass.ds(b * QP, QP)
                bb = lambda ri: BD[:, ri, :, :, :].rearrange("p q g c -> p q (g c)")
                fac = lambda ri: FAC[:, ri, pairs].unsqueeze(2).to_broadcast([P, QP, 2 * CH])
                V_.tensor_tensor(QTA[:, :, 0, :], bb(0), fac(0), ALU.mult)
                V_.tensor_tensor(QTB[:, :, 0, :], bb(1), fac(1), ALU.mult)
                V_.tensor_tensor(QTA[:, :, 1, :], bb(0), fac(1), ALU.mult)
                V_.tensor_tensor(QTB[:, :, 1, :], bb(1), fac(0), ALU.mult).then_inc(b_used, 1)
                V_.tensor_scalar(DG[:, 0:2 * CH], DIAG[:, 0, :], VEC[:, 7, bass.ds(b, 1)], None, ALU.mult)
                dve.wait_ge(b_used, b + 1)
                V_.tensor_tensor(QT[:, :, 0, 0, :], QTA[:, :, 0, :], QTB[:, :, 0, :], ALU.subtract)
                V_.tensor_tensor(QT[:, :, 1, 0, :], QTA[:, :, 1, :], QTB[:, :, 1, :], ALU.add).then_inc(q_base, 1)

            def b_powers(b):
                dve.wait_ge(q_base, b + 1)
                pairs = bass.ds(b * QP, QP)
                shape = [P, QP, T - 1, 2 * CH]
                base_ = lambda ri: QT[:, :, ri, 0:1, :].to_broadcast(shape)
                lam = lambda ri: LAM[:, ri, 1:T, pairs].rearrange("p j q -> p q j").unsqueeze(3).to_broadcast(shape)
                V_.tensor_tensor(QTA[:, :, :, :], base_(0), lam(0), ALU.mult)
                step(V_.tensor_tensor(QTB[:, :, :, :], base_(1), lam(1), ALU.mult))
                step(V_.tensor_tensor(QT[:, :, 0, 1:T, :], QTA[:, :, :, :], QTB[:, :, :, :], ALU.subtract))
                V_.tensor_tensor(QTA[:, :, :, :], base_(0), lam(1), ALU.mult)
                step(V_.tensor_tensor(QTB[:, :, :, :], base_(1), lam(0), ALU.mult))
                V_.tensor_tensor(QT[:, :, 1, 1:T, :], QTA[:, :, :, :], QTB[:, :, :, :], ALU.add).then_inc(qt_ready, 1)
                dve.wait_ge(qt_ready, b + 1)

            def residual_end(stage, i, per, j, n, vec, t_end):
                a = AT[stage]
                xq = X[:, bass.ds(n * (QB * TOK), QB * TOK)].rearrange("p (m t) -> p m t", t=TOK)
                dve.wait_ge(split_used, t_end)
                step(V_.tensor_tensor(xq, xq, quad(n % 2, TOK), ALU.add))
                V_.tensor_tensor(xq, xq, quad(n % 2, 0), ALU.add).then_inc(acc_free, 1)
                section(stage, i, per, j)
                dve.wait_ge(acc_free, n + (a["c"] + 1))
                low_parts(n, vec, H, n * 2 + a["q"])
                section(stage, i, per, j + 1)
                sum_squares(n + a["r"])
                sections(stage, i, per, j + 2, 2)

            def final_quad(n):
                if n >= 2:
                    dve.wait_ge(aux_done, AT["fin"]["a"] + n - 1)
                for m in range(QB):
                    k = QB * n + m
                    last = V_.tensor_scalar(XF[:, n % 2, m, :], X[:, TOK * k:TOK * k + TOK], VEC[:, 6, k:k + 1], None, ALU.mult)
                last.then_inc(xf_ready, 1)

            def gated_end(stage, i, per, j, n, vec, dst, other):
                a = AT[stage]
                section(stage, i, per, j)
                dve.wait_ge(nl_ready, n + (a["nl"] + 1))
                step(V_.tensor_tensor(Z[:, :], T1[:, :], other, ALU.mult))
                xq = X[:, bass.ds(n * (QB * TOK), QB * TOK)]
                V_.tensor_tensor(xq, xq, Z[:, :], ALU.add).then_inc(gated_ready, 1)
                section(stage, i, per, j + 1)
                dve.wait_ge(gated_ready, n + (a["g"] + 1))
                if dst is not None:
                    low_parts(n, vec, dst, n * 2 + a["q"])
                else:
                    final_quad(n)
                sum_squares(n + a["r"])
                sections(stage, i, per, j + 2, 2)

            def rotation(levels):
                for m in levels:
                    for part in (2, 3):
                        double_rotation(V_, step, m, part, RA[1], RB[1])

            for n in range(NT):
                sections("out0", n, KT, RING, 1)
                if n == 0:
                    dve.wait_ge(turns_ready, 1)
                    rotation([0, 1])
                if n == 1:
                    rotation([4])
                    V_.memset(RA[1][:, 0, 0, 0:1], 0.0).then_inc(rot_half, 1)
                sections("out0", n, KT, RING + 1, 1)
                if n == 0:
                    rotation([2, 3])
                if n == NT - 1:
                    b_scaled(0, first=True)
                sections("out0", n, KT, RING + 2, 1)
                if n == NT - 1:
                    b_powers(0)
                sections("out0", n, KT, RING + 3, 1)
                if n == 1:
                    dve.wait_ge(rot_half, 1)
                    double_rotation(V_, step, 5, 3, RA[1], RB[1])
                    V_.memset(RA[1][:, 0, 0, 0:1], 0.0).then_inc(rot_half, 1)
                residual_end("out0", n, KT, KT, n, 2, AT["out0"]["t"] + KT * (n + 1))
            rstd(2)

            def up_step(i, n, b=None, more=True):
                a, stage = AT[f"up{i}"], f"up{i}"
                blocks = bass.ds(n * QB, QB)

                def second_half(j0, b):
                    sections(stage, n, 2 * KT, j0 + RING, 2)
                    if b is not None:
                        b_scaled(b)
                    sections(stage, n, 2 * KT, j0 + RING + 2, 1)
                    if b is not None:
                        b_powers(b)
                    sections(stage, n, 2 * KT, j0 + RING + 3, 1)

                second_half(0, None if b is None else b + 1)
                total(n * 2 + a["c"], 0, n * 2 + a["cross"], flat3(Z))
                scaled(flat3(Z), z_ready)
                sections(stage, n, 2 * KT, KT, RING)
                second_half(KT, None if b is None or not more else b + 2)
                dve.wait_ge(nl_ready, n + (a["nl"] + 1))
                total(n * 2 + (a["c"] + 1), 1, n * 2 + (a["cross"] + 1), flat3(Z))
                step(V_.tensor_tensor(flat3(Z), flat3(Z), RSTD[:, :].unsqueeze(1).to_broadcast([P, QB, TOK]), ALU.mult))
                V_.tensor_tensor(flat3(Z), flat3(Z), GATED[:, blocks, 1, :], ALU.mult).then_inc(z_ready, 1)
                sections(stage, n, 2 * KT, 2 * KT, 2)
                dve.wait_ge(z_ready, n * 2 + (a["z"] + 2))
                dve.wait_ge(operand_hi, n * 2 + (a["q"] + 2))
                V_.tensor_tensor(M[:, blocks, TOK:2 * TOK], flat3(Z), M[:, blocks, 0:TOK].bitcast(F32),
                                 ALU.subtract).then_inc(operand_ready, 2)
                sections(stage, n, 2 * KT, 2 * KT + 2, 2)

            def up_loop(i, first):
                with nc.vector.Fori(first, NU) as n:
                    step.enter(n - first if first else n, 1)
                    up_step(i, n)
                step.leave(NU - first)

            def down(i):
                for n in range(NT):
                    sections(f"down{i}", n, FT, RING, FT - RING)
                    residual_end(f"down{i}", n, FT, FT, n, 4 + i, AT[f"down{i}"]["t"] + FT * (n + 1))
                sections(f"down{i}", n, FT, FT + NT, 1)
                rstd(3 * i + 3)
                sections(f"down{i}", n, FT, FT + NT + 1, RING - 1)

            with nc.vector.Fori(0, KB // 2 - 1) as n:
                step.enter(n, 7)
                up_step(0, n, b=n * 2)
            step.leave(KB // 2 - 1)
            up_step(0, KB // 2 - 1, b=KB - 2, more=False)
            up_loop(0, KB // 2)
            down(0)
            a = AT["gate0"]
            with nc.vector.Fori(0, NT // 2) as e:
                step.enter(e, 4)
                for s in range(2):
                    n = e * 2 + s
                    sections("gate0", e, 2 * KT, KT * s + RING, KT - RING)
                    total(n + a["c"], s, n + a["cross"], flat3(Z))
                    scaled(flat3(Z), z_ready)
                    gated_end("gate0", e, 2 * KT, KT * (s + 1), n, 1, M, PROJ[:, bass.ds(n * (QB * TOK), QB * TOK)])
            step.leave(NT // 2)
            rstd(4)

            def core_u(n):
                dve.wait_ge(split_used, AT["win"]["t"] + KT * (n + 1))
                V_.tensor_tensor(UC[n][:, :, :, :], half_quad(n % 2).rearrange("p m (k j) -> p m j k", j=T),
                                 RSTD[:, :].rearrange("p (k j) -> p j k", j=T).unsqueeze(1).to_broadcast([P, QB, T, NC]),
                                 ALU.mult).then_inc(acc_free, 1)

            def core_scan(b):
                d, par, bl = b // 2, table_set(b // 2), b % 2
                dve.wait_ge(te_in[par], 16 * (d // 2 + 1))
                dve.wait_ge(in_done, b + 1)
                cos, sin = TE[par][:, 0, bl, :, :], TE[par][:, 1, bl, :, :]
                inc = PS[:, 4 + bl, :].rearrange("p (q r k) -> p q r k", q=QP, r=2)
                both = lambda x_: x_.unsqueeze(2).to_broadcast([P, QP, 2, NC])
                V_.tensor_tensor(CA[:, :, :, :], inc, both(cos), ALU.mult)
                V_.tensor_tensor(CB[:, :, :, :], inc, both(sin), ALU.mult).then_inc(inc_free, 1)
                dve.wait_ge(inc_free, b + 1)
                V_.tensor_tensor(CV[:, 0, :, :], CA[:, :, 0, :], CB[:, :, 1, :], ALU.add)
                step(V_.tensor_tensor(CV[:, 1, :, :], CA[:, :, 1, :], CB[:, :, 0, :], ALU.subtract))
                dve.wait_ge(rt_ready, b + 1)
                flat = lambda x_: x_.rearrange("p a b k -> p (a b k)").rearrange("p (r n) -> p r n", r=2)
                w, w_cos, w_sin = flat(CB[:, :, :, :]), flat(CV[:, :, :, :]), flat(CA[:, :, :, :])
                for ri in range(2):
                    last = V_.tensor_tensor_scan(w[:, ri, :], RT[bl][:, :, :].rearrange("p q k -> p (q k)"),
                                                 CV[:, ri, :, :].rearrange("p q k -> p (q k)"), 0.0, ALU.mult, ALU.add)
                last.then_inc(rt_used, 1)
                dve.wait_ge(rt_used, b + 1)
                one = lambda x_: x_.rearrange("p q k -> p (q k)").unsqueeze(1).to_broadcast([P, 2, QP * NC])
                V_.tensor_tensor(w_cos, w, one(cos), ALU.mult)
                step(V_.tensor_tensor(w_sin, w, one(sin), ALU.mult))
                if d >= 2:
                    dve.wait_ge(out_of, d - 1)
                part = lambda x_, ri: x_[:, ri, :].rearrange("p (q k) -> p q k", k=NC)[:, :, 0:NC - 1]
                V_.tensor_tensor(SD[b % 4][:, 0, :, 1:NC], part(w_cos, 0), part(w_sin, 1), ALU.subtract)
                V_.tensor_tensor(SD[b % 4][:, 1, :, 1:NC], part(w_cos, 1), part(w_sin, 0), ALU.add).then_inc(sd_ready, 1)
                dve.wait_ge(sd_ready, b + 1)

            def core_lo(d):
                dve.wait_ge(operand_hi, AT["core"]["q"] + d + 1)
                blocks = slice(KB + 2 * d, KB + 2 * d + 2)
                V_.tensor_tensor(M[:, blocks, TOK:2 * TOK].rearrange("p b (k j) -> p b k j", j=T),
                                 YG[:, :, :, :].rearrange("p b j k -> p b k j"),
                                 M[:, blocks, 0:TOK].bitcast(F32).rearrange("p b (k j) -> p b k j", j=T),
                                 ALU.subtract).then_inc(operand_ready, 1)

            dve.wait_ge(core_ready, 1)
            for g in range(RING, CORE_TILES):
                for h in range(2):
                    if CORE_ORDER[g] == (NT + h, KT - 1):
                        dve.wait_ge(split_used, AT["win"]["t"] + g + 1)
                        V_.tensor_copy(flat3(Z if h else VAL), half_quad(h)).then_inc(acc_free, 1)
                section("win", 0, 0, g)
                if g % KT == KT - 1 and g < KT * NT:
                    core_u(g // KT)
                for b in range(KB):
                    if g == SCAN[b]:
                        core_scan(b)
                for d in range(DUOS):
                    if g == LO[d]:
                        core_lo(d)
            a = AT["out1"]
            gated_end("out1", 0, 2 * KT, 2 * KT, 0, 3, H, VAL[:, :])

            def out1_step(n):
                c = n * 2 + a["c"]
                sections("out1", n, 2 * KT, RING, KT - RING)
                total(c, 0, n * 2 + a["cross"], flat3(VAL))
                sections("out1", n, 2 * KT, KT, KT)
                total(c + 1, 1, n * 2 + (a["cross"] + 1), flat3(Z))
                gated_end("out1", n, 2 * KT, 2 * KT, n, 3, H, VAL[:, :])

            with nc.vector.Fori(1, NT) as n:
                step.enter(n - 1, 2)
                out1_step(n)
            step.leave(NT - 1)
            rstd(5)
            up_loop(1, 0)
            down(1)
            a, a0 = AT["gate1"], AT["fin"]["a"]

            for n in range(NT):
                sections("gate1", n, KT, RING, KT - RING)
                total(n + a["c"], n % 2, n + a["cross"], flat3(Z))
                scaled(flat3(Z), z_ready)
                gated_end("gate1", n, KT, KT, n, None, None, PROJ[:, QB * TOK * n:QB * TOK * (n + 1)])
            rstd(7)
            dve.wait_ge(aux_free, a0 + NT + 1)
            for th in range(2):
                V_.tensor_scalar(ON[:, th, 0:D // 2], ON[:, th, 0:D // 2], RCOL[:, th:th + 1], None, ALU.mult).then_inc(out_v, 1)

        @block.tensor
        def _(pe):
            T_ = nc.tensor

            def free(c):
                if not (isinstance(c, int) and c < 2):
                    pe.wait_ge(acc_free, c - 1)

            def products(stage, i, per, j0, c, s, depth, operand, ready, q, after=None):
                free(c)
                for j in range(depth):
                    t, _, slot = tile_at(stage, i, per, j0 + j)
                    pe.wait_ge(ready, q + j + 1)
                    pe.wait_ge(lo_ready, t + 1)
                    for kk in range(TK):
                        k = TK * j + kk
                        for m in range(QB):
                            w = slice(NW * kk + P * m, NW * kk + P * m + P)
                            T_.matmul(PS[:, QB * s + m, :], WHI[:, slot, w], operand(k), start=(k == 0), stop=False)
                            last = T_.matmul(PS[:, QB * s + m, TOK:2 * TOK], WLO[:, slot, w], operand(k)[:, 0:TOK],
                                             start=False, stop=(k == TK * depth - 1))
                    last.then_inc(split_used, 1)
                    if after is not None:
                        after(j)

            def tile_in_place(t, s, j, depth, operand):
                slot = t % RING
                if j == 0:
                    for h in range(2):
                        T_.matmul(PS[:, 2 * s + h, :].rearrange("p (a n) -> p a n", n=P), ZERO[0:1, :],
                                  ZERO[0:1, :].unsqueeze(1).to_broadcast([1, QB, P]), start=True, stop=False)
                pe.wait_ge(lo_ready, t + 1)
                for kk in range(TK):
                    k = TK * j + kk
                    for m in range(QB):
                        w = slice(NW * kk + P * m, NW * kk + P * m + P)
                        dst = PS[:, 2 * s + m // 2, TOK * (m % 2):TOK * (m % 2) + TOK]
                        T_.matmul(dst, WHI[:, slot, w], operand(k)[:, 0:TOK], start=False, stop=False)
                        T_.matmul(dst, WHI[:, slot, w], operand(k)[:, TOK:2 * TOK], start=False, stop=False)
                        last = T_.matmul(dst, WLO[:, slot, w], operand(k)[:, 0:TOK], start=False,
                                         stop=(k == TK * depth - 1 and m % 2 == 1))
                last.then_inc(split_used, 1)

            in_h = lambda k: H[:, k, :]
            in_m = lambda k: M[:, k, :]
            in_m2 = lambda k: M[:, KB + k, :]

            pe.wait_ge(ident_ready, 1)
            pe.wait_ge(vec_in, 16 * 5)
            T_.transpose(PS[:, 4, 0:P], NAT[:, :], IDENT[:, :]).then_inc(aux_done, 1)
            for n in range(NT):
                pe.wait_ge(x_in[n], 16)
                if n >= 1:
                    pe.wait_ge(aux_free, n)
                for m in range(QB):
                    for th in range(2):
                        k = QB * n + m
                        last = T_.transpose(PS[:, QB * (n % 2) + m, P * th:P * th + P], XN[:, th, P * k:P * k + P], IDENT[:, :])
                last.then_inc(aux_done, 1)

            def set_up(j):
                a0 = AT["set-up"]["a"]
                if j == 3:
                    pe.wait_ge(aux_free, a0)
                    pe.wait_ge(s5_in, 48)
                    pe.wait_ge(ldt_spread, 1)
                    pe.wait_ge(p_in, 32)
                    for i in range(3):
                        T_.transpose(PS[:, 4, PAIRS * i:PAIRS * i + PAIRS], AN[:, i, :], IDENT[0:PAIRS, 0:PAIRS])
                    for l in range(2):
                        for f in range(2):
                            for th in range(2):
                                at = TOK * f + P * th
                                last = T_.transpose(PS[:, 5 + l, at:at + P], PN[:, l, th, P * f:P * f + P], IDENT[:, :])
                    last.then_inc(aux_done, 1)
                if j == 5:
                    pe.wait_ge(aux_free, a0 + 1)
                    pe.wait_ge(ws_masked, 1)
                    for h in range(HEADS):
                        last = T_.transpose(PS[:, 4 + h // 4, P * (h % 4):P * (h % 4) + P], WN[:, h, :], IDENT[:, :])
                    last.then_inc(aux_done, 1)
                if j == KT + 1:
                    pe.wait_ge(masks_ready, 1)
                    to_column(2, a0 + 2, 1)

            def to_column(bank, a, k):
                pe.wait_ge(aux_free, a)
                pe.wait_ge(rstd_ready, k)
                for th in range(2):
                    last = T_.matmul(PS[:, bank, th:th + 1], RSTD[0:1, P * th:P * th + P], ONE[0:1, 0:1], start=True, stop=True)
                last.then_inc(aux_done, 1)

            for n in range(NT):
                s = n % 2
                if n < 2:
                    pe.wait_ge(aux_free, AT["set-up"]["a"] + (-1 if n == 0 else 2))
                free(n)
                for j in range(KT):
                    t, _, slot = tile_at("v", n, KT, j)
                    pe.wait_ge(operand_ready, j + 1)
                    pe.wait_ge(lo_ready, t + 1)
                    for kk in range(TK):
                        k = TK * j + kk
                        f = slice(NW * kk, NW * kk + NW)
                        for th in range(2):
                            acc = PS[:, QB * s + th, :]
                            hi, lo = M[:, k, P * th:P * th + P], M[:, k, TOK + P * th:TOK + P * th + P]
                            T_.matmul(acc, hi, WHI[:, slot, f], start=(k == 0), stop=False)
                            T_.matmul(acc, hi, WLO[:, slot, f], start=False, stop=False)
                            last = T_.matmul(acc, lo, WHI[:, slot, f], start=False, stop=(k == KB - 1))
                    last.then_inc(split_used, 1)
                    if n < 2:
                        set_up(KT * n + j)

            a = AT["us"]
            for n in range(NT):
                def mix(j):
                    if j != RING + 2:
                        return
                    s = 1 - n % 2
                    free(a["c"] + n + 1)
                    pe.wait_ge(v_ready, n + 1)
                    pe.wait_ge(ln_in, 48)
                    for m in range(QB):
                        h = QB * n + m
                        for c in range(2):
                            T_.matmul(PS[:, QB * s + m, P * c:P * c + P], V[:, c, P * h:P * h + P], WT[:, h, :],
                                      start=(c == 0), stop=False)
                        last = T_.matmul(PS[:, QB * s + m, 0:TOK].rearrange("p (c t) -> p c t", c=2), ONE[0:1, :],
                                         BS[0:1, h, :].unsqueeze(1).to_broadcast([1, 2, P]), start=False, stop=True)
                    last.then_inc(aux_done, 1)

                pe.wait_ge(aux_free, a["a"] + n)
                products("us", n, KT, 0, a["c"] + n, n % 2, KT, in_m, operand_ready, 0, after=mix)

            def tables(b, s, c, q=True, more=True):
                free(c + 1)
                if more:
                    pe.wait_ge(cm_ready, b + 2)
                    for ri in range(2):
                        last = T_.transpose(PS[:, QB * s, P * ri:P * ri + P], CM[:, ri, :, :].rearrange("p g s -> p (g s)"),
                                            IDENT[:, :])
                if q:
                    pe.wait_ge(qt_ready, b + 1)
                    for i in range(2 * QP):
                        T_.transpose(PS[:, QB * s + 1 + i // 4, P * (i % 4):P * (i % 4) + P],
                                     QT[:, i // 2, i % 2, :, :].rearrange("p j c -> p (j c)"), IDENT[:, :])
                    pe.wait_ge(dt_ready, b + 1)
                    T_.matmul(PS[:, QB * s + 3, 0:P], IDENT[:, :], DG[:, :], start=True, stop=False)
                    for k in range(QP):
                        r = slice(32 * k, 32 * k + 32)
                        for ri in range(2):
                            last = T_.matmul(PS[r, QB * s + 3, 0:P], QT[:, k, ri, 0, :],
                                             DT[:, k, ri, 0:T, :].rearrange("p j c -> p (j c)"), start=False, stop=(ri == 1))
                last.then_inc(aux_done, 1)

            a = AT["out0"]
            pe.wait_ge(aux_free, AT["first"]["a"])
            for n in range(NT):
                after = (lambda j: tables(-1, 0, a["c"] + NT - 1, q=False) if j == MID + 2 else None) if n == NT - 1 else None
                products("out0", n, KT, 0, a["c"] + n, n % 2, KT, in_m2, operand_ready, a["q"] - KT, after=after)

            def up_step(i, n, b=None, more=True):
                a, stage = AT[f"up{i}"], f"up{i}"
                for s in range(2):
                    c = n * 2 + (a["c"] + s)
                    after = None
                    if b is not None:
                        pe.wait_ge(aux_free, b + (AT["build"]["a"] + s))
                        after = lambda j: tables(b + s, 1 - s, c, more=(s == 0 or more)) if j == MID else None
                    products(stage, n, 2 * KT, KT * s, c, s, KT, in_h, operand_ready, a["q"] - KT, after=after)

            def up_loop(i, first):
                with nc.tensor.Fori(first, NU) as n:
                    up_step(i, n)

            def down(i):
                a = AT[f"down{i}"]
                with nc.tensor.Fori(0, NT // 2) as e:
                    for s in range(2):
                        products(f"down{i}", e, 2 * FT, FT * s, e * 2 + (a["c"] + s), s, FT, in_m, operand_ready, a["q"] - FT)
                a = AT[f"proj{i}"]
                for n in range(NT):
                    pe.wait_ge(acc_free, a["c"] - 1 + n // 2)
                    tile_in_place(a["t"] + n, n, 0, 1, lambda k: PT[:, 2 * i + k, :])

            def gate(i):
                a = AT[f"gate{i}"]
                with nc.tensor.Fori(0, NT // 2) as e:
                    for s in range(2):
                        products(f"gate{i}", e, 2 * KT, KT * s, e * 2 + (a["c"] + s), s, KT, in_h, operand_ready, a["q"] - KT)

            with nc.tensor.Fori(0, KB // 2 - 1) as n:
                up_step(0, n, b=n * 2)
            up_step(0, KB // 2 - 1, b=KB - 2, more=False)
            pe.wait_ge(aux_free, AT["build"]["a"] + KB)
            up_loop(0, KB // 2)
            down(0)
            gate(0)

            def into_states(b):
                d, par, bl, n = b // 2, table_set(b // 2), b % 2, b // QB
                if b == 0:
                    pe.wait_ge(acc_free, AT["win"]["c"])
                if bl == 0:
                    pe.wait_ge(tq_in[par], 16 * (d // 2 + 1))
                pe.wait_ge(up_in[n], 64)
                if b >= 2:
                    pe.wait_ge(inc_free, b - 1)
                for q in range(QP):
                    for ri in range(2):
                        c0 = P * q + NC * ri
                        last = T_.matmul(PS[:, 4 + bl, c0:c0 + NC], TQ[par][:, bl, q, ri, :], UP[n][:, b % QB, q, :],
                                         start=True, stop=True)
                last.then_inc(in_done, 1)

            def out_of_states(d):
                par = table_set(d)
                pe.wait_ge(td_in[par], 80 * (d // 2 + 1))
                pe.wait_ge(sd_ready, 2 * d + 2)
                if d >= 2:
                    pe.wait_ge(yp_ready, d - 1)
                for bl in range(2):
                    b = 2 * d + bl
                    for q in range(QP):
                        dst = PS[:, 6 + d % 2, TOK * bl + NC * q:TOK * bl + NC * q + NC]
                        T_.matmul(dst, TKK[par][:, bl, q, :], UP[b // QB][:, b % QB, q, :], start=True, stop=False)
                        for ri in range(2):
                            last = T_.matmul(dst, TD[par][:, bl, q, ri, :], SD[b % 4][:, ri, q, :], start=False, stop=(ri == 1))
                last.then_inc(out_of, 1)

            a = AT["win"]
            for g, (n, j) in enumerate(CORE_ORDER):
                if j == 0:
                    pe.wait_ge(acc_free, a["c"] + n - 1)
                if n < NT:
                    pe.wait_ge(operand_ready, a["q"] - KT + j + 1)
                    tile_in_place(a["t"] + g, n % 2, j, KT, in_m)
                else:
                    pe.wait_ge(operand_ready, a["q"] + j + 1)
                    tile_in_place(a["t"] + g, n % 2, j, KT, in_m2)
                for b in range(KB):
                    if g == SCAN[b]:
                        into_states(b)
                for d in range(DUOS):
                    if g == OUT[d]:
                        out_of_states(d)

            a = AT["out1"]
            pe.wait_ge(yp_ready, DUOS)
            pe.wait_ge(inc_free, KB)
            pe.wait_ge(acc_free, a["c"] + 2)
            with nc.tensor.Fori(1, NT) as n:
                for s in range(2):
                    products("out1", n, 2 * KT, KT * s, n * 2 + (a["c"] + s), s, KT, in_m2, operand_ready, a["q"] - KT)
            up_loop(1, 0)
            down(1)

            a, a0 = AT["gate1"], AT["fin"]["a"]

            def transpose_back(n):
                pe.wait_ge(xf_ready, n + 1)
                for m in range(QB):
                    for th in range(2):
                        last = T_.transpose(PS[:, QB * (n % 2) + th, P * m:P * m + P], XF[:, n % 2, m, P * th:P * th + P],
                                            IDENT[:, :])
                last.then_inc(aux_done, 1)

            for n in range(NT):
                def after(j):
                    if j == MID + 1 and n:
                        free(a["c"] + n + 1)
                        transpose_back(n - 1)
                if n >= 2:
                    pe.wait_ge(aux_free, a0 + n - 1)
                products("gate1", n, KT, 0, a["c"] + n, n % 2, KT, in_h, operand_ready, a["q"] - KT, after=after)
            pe.wait_ge(acc_free, AT["fin"]["c"])
            transpose_back(NT - 1)
            to_column(4, a0 + NT, 7)

INPUTS = ["x", "p", "norm_mix", "norm_ffn", "norm_ple", "norm_final", "gm_w_in", "gm_ln_g", "gm_ln_b", "gm_w_s", "gm_b_s",
          "gm_w_out", "s5_w_in", "s5_a_re", "s5_a_im", "s5_log_dt", "s5_b_re", "s5_b_im", "s5_c_re", "s5_c_im", "s5_d",
          "s5_w_out", "ffn_w1", "ffn_w3", "ffn_w2", "ple_w_gate", "ple_w_proj"]


def kernel(**inputs):
    import numpy as np
    import concourse.bacc as bacc
    from concourse.bass_utils import run_bass_kernel_spmd

    nc = bacc.Bacc("TRN2", target_bir_lowering=False, num_devices=1)
    arrays, args = {}, []
    for name in INPUTS:
        a = np.ascontiguousarray(inputs[name])
        arrays[f"in_{name}"] = a
        args.append(nc.dram_tensor(f"in_{name}", a.shape, mybir.dt.from_np(a.dtype), kind="ExternalInput").ap())
    args.append(nc.dram_tensor("out", (1, TOK, D), F32, kind="ExternalOutput").ap())
    trunk(nc, *args)
    return run_bass_kernel_spmd(nc, [arrays], core_ids=[0]).results[0]["out"]
```
